# Optimizing a Trainium2 kernel written in Bass

```python
import math
import jax, jax.numpy as jnp
from jax import lax
import numpy as np

D_MODEL = 1024
BATCH = 1
SEQ = 256
DEPTH = 2

CTX_LEN = 256
GRID_W = 64
NORM_EPS = 1e-6

ML_HEADS = 4
ML_DK = 256
ML_DV = 256
ML_W = ML_HEADS * ML_DV
ML_CHUNK = 128

DA_HEADS = 8
DA_DH = 64
DA_DV = 2 * DA_DH
DA_QK_W = DA_HEADS * 2 * DA_DH
DA_V_W = DA_HEADS * DA_DV
Q_BLOCK = 128
ROPE_BASE = 10000.0

FN_GROUPS = 4
FN_GC = 256
FN_W = FN_GROUPS * FN_GC

N_BRANCH = 3
D_FF = -(-8 * D_MODEL // (3 * 256)) * 256

IN_SPLITS = (ML_DK * ML_HEADS, ML_DK * ML_HEADS, ML_W, ML_W, 4 * ML_HEADS,
             DA_QK_W, DA_QK_W, DA_V_W, FN_W, N_BRANCH * D_MODEL)
D_IN = sum(IN_SPLITS)


def _rmsnorm(x, g):
    xf = x.astype(jnp.float32)
    y = xf * lax.rsqrt(jnp.mean(xf * xf, axis=-1, keepdims=True) + NORM_EPS)
    return (y * g.astype(jnp.float32)).astype(x.dtype)

def _modulate(h, shift, scale):
    return h * (1 + scale) + shift

def _split_cols(u):
    idx, acc = [], 0
    for s in IN_SPLITS[:-1]:
        acc += s
        idx.append(acc)
    return jnp.split(u, idx, axis=-1)

def _axial_rope(rows):
    n_freq = DA_DH // 4
    inv = ROPE_BASE ** (-jnp.arange(n_freq, dtype=jnp.float32) / n_freq)
    r = jnp.repeat(jnp.arange(rows, dtype=jnp.float32), GRID_W)
    col = jnp.tile(jnp.arange(GRID_W, dtype=jnp.float32), rows)
    ang = jnp.concatenate([r[:, None] * inv, col[:, None] * inv], axis=-1)
    return jnp.cos(ang), jnp.sin(ang)

def _rope(x, cos, sin):
    shp = (cos.shape[0],) + (1,) * (x.ndim - 3) + (cos.shape[1],)
    c = cos.reshape(shp).astype(x.dtype)
    s = sin.reshape(shp).astype(x.dtype)
    x1, x2 = jnp.split(x, 2, axis=-1)
    return jnp.concatenate([x1 * c - x2 * s, x1 * s + x2 * c], axis=-1)

def _mlstm_scan(q, k, v, i_pre, f_pre, state):
    B, T, H, DK = q.shape
    DV = v.shape[-1]
    L = ML_CHUNK
    NC = T // L

    def chunks(a):
        a = a.astype(jnp.float32).reshape((B, NC, L, H) + a.shape[3:])
        return jnp.moveaxis(jnp.moveaxis(a, 1, 0), 3, 2)

    tri = jnp.tril(jnp.ones((L, L), dtype=bool))

    def step(carry, xs):
        C, n, m = carry
        qc, kc, vc, ic, fc = xs
        b = jnp.cumsum(jax.nn.log_sigmoid(fc), axis=-1)
        dmat = jnp.where(tri, b[..., :, None] - b[..., None, :] + ic[..., None, :], -jnp.inf)
        inter = b + m[..., None]
        m_t = jnp.maximum(inter, jnp.max(dmat, axis=-1))
        a = jnp.exp(dmat - m_t[..., None]) * jnp.einsum('bhtd,bhsd->bhts', qc, kc)
        sc = jnp.exp(inter - m_t)
        num = sc[..., None] * jnp.einsum('bhtd,bhde->bhte', qc, C) + jnp.einsum('bhts,bhse->bhte', a, vc)
        den = sc * jnp.einsum('bhtd,bhd->bht', qc, n) + jnp.sum(a, axis=-1)
        h = num / jnp.maximum(jnp.abs(den), jnp.exp(-m_t))[..., None]
        b_end = b[..., -1]
        g_s = b_end[..., None] - b + ic
        m_new = jnp.maximum(b_end + m, jnp.max(g_s, axis=-1))
        decay = jnp.exp(b_end + m - m_new)
        kw = kc * jnp.exp(g_s - m_new[..., None])[..., None]
        C_new = decay[..., None, None] * C + jnp.einsum('bhsd,bhse->bhde', kw, vc)
        n_new = decay[..., None] * n + jnp.sum(kw, axis=2)
        return (C_new, n_new, m_new), h

    final, hs = lax.scan(step, state, (chunks(q), chunks(k), chunks(v), chunks(i_pre), chunks(f_pre)))
    h = jnp.transpose(hs, (1, 0, 3, 2, 4)).reshape(B, T, H, DV)
    return h, final

def _mlstm_branch(ul, uc, gate_b, head_g):
    def prep(u):
        B, T, _ = u[0].shape
        q = u[0].reshape(B, T, ML_HEADS, ML_DK)
        k = u[1].reshape(B, T, ML_HEADS, ML_DK) * (ML_DK ** -0.5)
        v = u[2].reshape(B, T, ML_HEADS, ML_DV)
        i_f, f_f, i_b, f_b = jnp.split(u[4] + gate_b, 4, axis=-1)
        return q, k, v, i_f, f_f, i_b, f_b

    flip = lambda a: jnp.flip(a, axis=1)
    ql, kl, vl, ifl, ffl, ibl, fbl = prep(ul)
    qc, kc, vc, ifc, ffc, ibc, fbc = prep(uc)
    B = ql.shape[0]
    zero = (jnp.zeros((B, ML_HEADS, ML_DK, ML_DV), jnp.float32),
            jnp.zeros((B, ML_HEADS, ML_DK), jnp.float32),
            jnp.zeros((B, ML_HEADS), jnp.float32))
    hcf, st_f = _mlstm_scan(qc, kc, vc, ifc, ffc, zero)
    hlf, _ = _mlstm_scan(ql, kl, vl, ifl, ffl, st_f)
    hcb, st_b = _mlstm_scan(flip(qc), flip(kc), flip(vc), flip(ibc), flip(fbc), zero)
    hlb, _ = _mlstm_scan(flip(ql), flip(kl), flip(vl), flip(ibl), flip(fbl), st_b)

    def out(hf, hb, u):
        B, T = hf.shape[:2]
        h = _rmsnorm(hf + hb, head_g.reshape(ML_HEADS, ML_DV)).reshape(B, T, ML_W)
        return h.astype(u[3].dtype) * jax.nn.sigmoid(u[3])

    return out(hlf, flip(hlb), ul), out(hcf, flip(hcb), uc)

def _diff_attn_core(q, k, v, lam):
    s = jnp.einsum('bqhmd,bkhmd->bhmqk', q, k).astype(jnp.float32) * (DA_DH ** -0.5)
    p = jax.nn.softmax(s, axis=-1)
    a = p[:, :, 0] - lam * p[:, :, 1]
    return jnp.einsum('bhqk,bkhe->bqhe', a.astype(v.dtype), v)

def _diff_attn_branch(ul, uc, lam_qk, head_g, cos, sin, lam_init, need_ctx):
    def qkv(u):
        B, T, _ = u[5].shape
        return (u[5].reshape(B, T, DA_HEADS, 2, DA_DH),
                u[6].reshape(B, T, DA_HEADS, 2, DA_DH),
                u[7].reshape(B, T, DA_HEADS, DA_DV))

    lq = lam_qk.astype(jnp.float32)
    lam = jnp.exp(jnp.sum(lq[0] * lq[1])) - jnp.exp(jnp.sum(lq[2] * lq[3])) + lam_init
    ql, kl, vl = qkv(ul)
    qc, kc, vc = qkv(uc)
    ql, kl = _rope(ql, cos, sin), _rope(kl, cos, sin)
    k_all = jnp.concatenate([kl, kc], axis=1)
    v_all = jnp.concatenate([vl, vc], axis=1)
    B, T = ql.shape[:2]
    nb = T // Q_BLOCK
    qb = jnp.moveaxis(ql.reshape(B, nb, Q_BLOCK, DA_HEADS, 2, DA_DH), 1, 0)
    ob = lax.map(lambda qq: _diff_attn_core(qq, k_all, v_all, lam), qb)
    ol = jnp.moveaxis(ob, 0, 1).reshape(B, T, DA_HEADS, DA_DV)

    def post(o):
        Bo, To = o.shape[:2]
        return (_rmsnorm(o, head_g.reshape(DA_HEADS, DA_DV)) * (1.0 - lam_init)).reshape(Bo, To, DA_V_W)

    oc = post(_diff_attn_core(qc, kc, vc, lam)) if need_ctx else None
    return post(ol), oc

def _fourier(u):
    B, T, _ = u.shape
    z = u.astype(jnp.float32).reshape(B, T, FN_GROUPS, FN_GC)
    y = jnp.fft.fftn(z, axes=(1, 3), norm='ortho').real
    return y.reshape(B, T, FN_W).astype(u.dtype)

def _merge(ym, yd, yf, g_pre, w_br_ml, w_br_da, w_br_fn, w_out):
    gm, gd, gf = jnp.split(jax.nn.sigmoid(g_pre), N_BRANCH, axis=-1)
    y = gm * (ym @ w_br_ml) + gd * (yd @ w_br_da) + gf * (yf @ w_br_fn)
    return y @ w_out

def _mixer(hl, hc, w_in, ml_gate_b, ml_head_g, da_lam, da_head_g, w_br_ml, w_br_da, w_br_fn, w_out,
           cos, sin, lam_init, need_ctx):
    ul = _split_cols(hl @ w_in)
    uc = _split_cols(hc @ w_in)
    ml_l, ml_c = _mlstm_branch(ul, uc, ml_gate_b, ml_head_g)
    da_l, da_c = _diff_attn_branch(ul, uc, da_lam, da_head_g, cos, sin, lam_init, need_ctx)
    yl = _merge(ml_l, da_l, _fourier(ul[8]), ul[9], w_br_ml, w_br_da, w_br_fn, w_out)
    yc = _merge(ml_c, da_c, _fourier(uc[8]), uc[9], w_br_ml, w_br_da, w_br_fn, w_out) if need_ctx else None
    return yl, yc

def _swiglu(h, w_in, w_out):
    a, b = jnp.split(h @ w_in, 2, axis=-1)
    return (jax.nn.silu(a) * b) @ w_out

def first_inputs(seed: int = 0) -> dict:
    key = jax.random.key(seed)
    ks = jax.random.split(key, 20)
    f32 = jnp.float32
    D = D_MODEL

    def nrm(k, shape, s):
        return jax.random.normal(k, shape, f32) * s

    f_mask = jnp.array([0.0, 1.0, 0.0, 1.0], f32)[None, :, None]
    f_bias = jnp.linspace(3.0, 6.0, ML_HEADS, dtype=f32)[None, None, :]
    ml_gate_b = (nrm(ks[8], (DEPTH, 4, ML_HEADS), 0.1) + f_mask * f_bias).reshape(DEPTH, 4 * ML_HEADS)
    return {
        'x': nrm(ks[0], (BATCH, SEQ, D), 1.0),
        'c': nrm(ks[1], (BATCH, D), 1.0),
        'ctx': nrm(ks[2], (BATCH, CTX_LEN, D), 1.0),
        'c_ctx': nrm(ks[3], (D,), 1.0),
        'w_ada': nrm(ks[4], (DEPTH, D, 6 * D), 0.5 * D ** -0.5),
        'b_ada': nrm(ks[5], (DEPTH, 6 * D), 0.02),
        'norm_g': 1.0 + nrm(ks[6], (DEPTH, 2, D), 0.02),
        'w_in': nrm(ks[7], (DEPTH, D, D_IN), D ** -0.5),
        'ml_gate_b': ml_gate_b,
        'ml_head_g': 1.0 + nrm(ks[9], (DEPTH, ML_W), 0.02),
        'da_lam': nrm(ks[10], (DEPTH, 4, DA_DH), 0.1),
        'da_head_g': 1.0 + nrm(ks[11], (DEPTH, DA_V_W), 0.02),
        'w_br_ml': nrm(ks[12], (DEPTH, ML_W, D), ML_W ** -0.5),
        'w_br_da': nrm(ks[13], (DEPTH, DA_V_W, D), DA_V_W ** -0.5),
        'w_br_fn': nrm(ks[14], (DEPTH, FN_W, D), FN_W ** -0.5),
        'w_out': nrm(ks[15], (DEPTH, D, D), D ** -0.5),
        'w_ffn_in': nrm(ks[16], (DEPTH, D, 2 * D_FF), D ** -0.5),
        'w_ffn_out': nrm(ks[17], (DEPTH, D_FF, D), D_FF ** -0.5),
        'final_g': 1.0 + nrm(ks[18], (D,), 0.02),
    }

def first_block(x, c, ctx, c_ctx, w_ada, b_ada, norm_g, w_in, ml_gate_b, ml_head_g, da_lam, da_head_g,
              w_br_ml, w_br_da, w_br_fn, w_out, w_ffn_in, w_ffn_out, final_g):
    T = x.shape[1]
    ROWS = T // GRID_W
    cos, sin = _axial_rope(ROWS)
    s_lat = jax.nn.silu(c)
    s_ctx = jax.nn.silu(c_ctx)
    xl, xc = x, ctx
    for l in range(DEPTH):
        need_ctx = l < DEPTH - 1
        lam_init = 0.8 - 0.6 * math.exp(-0.3 * l)
        ml = jnp.split((s_lat @ w_ada[l] + b_ada[l])[:, None, :], 6, axis=-1)
        mc = jnp.split((s_ctx @ w_ada[l] + b_ada[l])[None, None, :], 6, axis=-1)
        hl = _modulate(_rmsnorm(xl, norm_g[l, 0]), ml[0], ml[1])
        hc = _modulate(_rmsnorm(xc, norm_g[l, 0]), mc[0], mc[1])
        yl, yc = _mixer(hl, hc, w_in[l], ml_gate_b[l], ml_head_g[l], da_lam[l], da_head_g[l],
                        w_br_ml[l], w_br_da[l], w_br_fn[l], w_out[l], cos, sin, lam_init, need_ctx)
        xl = xl + ml[2] * yl
        xl = xl + ml[5] * _swiglu(_modulate(_rmsnorm(xl, norm_g[l, 1]), ml[3], ml[4]), w_ffn_in[l], w_ffn_out[l])
        if need_ctx:
            xc = xc + mc[2] * yc
            xc = xc + mc[5] * _swiglu(_modulate(_rmsnorm(xc, norm_g[l, 1]), mc[3], mc[4]), w_ffn_in[l], w_ffn_out[l])
    return _rmsnorm(xl, final_g)


DEPTH_2 = 1

MIX_WIDTH = D_MODEL
HG_WIDTH = MIX_WIDTH // 2
HG_HEADS = 4
HG_DK = HG_WIDTH // HG_HEADS
HG_CHUNK = 64
S5_WIDTH = MIX_WIDTH - HG_WIDTH
S5_GROUP = 16
S5_GROUPS = S5_WIDTH // S5_GROUP
S5_STATE = 64
IN_WIDTH = 4 * HG_WIDTH + S5_WIDTH
PEER_HEADS = 8
PEER_NKEYS = 128
PEER_EXPERTS = PEER_NKEYS * PEER_NKEYS
PEER_TOPK = 16
PEER_QDIM = 256
PEER_HALF = PEER_QDIM // 2
PEER_TOKEN_BLOCK = 128
EPS = 1e-6


def _rmsnorm_2(x, w):
    xf = x.astype(jnp.float32)
    y = xf * lax.rsqrt(jnp.mean(xf * xf, axis=-1, keepdims=True) + EPS)
    return (y * w.astype(jnp.float32)).astype(x.dtype)

def _hgrn2(q, f_logit, i, g, lb, gn_w):
    bsz, seq, _ = q.shape
    f32 = jnp.float32
    f = lb + (1.0 - lb) * jax.nn.sigmoid(f_logit.astype(f32))
    log_f = jnp.log(f)
    k = 1.0 - f
    qs = jax.nn.silu(q.astype(f32)) * (HG_DK ** -0.5)
    v = i.astype(f32)
    n_chunks = seq // HG_CHUNK

    def to_chunks(t):
        return t.reshape(bsz, n_chunks, HG_CHUNK, HG_HEADS, HG_DK).transpose(1, 0, 3, 2, 4)

    causal = jnp.tril(jnp.ones((HG_CHUNK, HG_CHUNK), dtype=bool))[:, :, None]

    def step(state, inp):
        qc, kc, vc, lc = inp
        bcum = jnp.cumsum(lc, axis=2)
        o_inter = jnp.einsum('bhtk,bhkv->bhtv', qc * jnp.exp(bcum), state)
        diff = bcum[:, :, :, None, :] - bcum[:, :, None, :, :]
        decay = jnp.exp(jnp.where(causal, diff, -jnp.inf))
        scores = jnp.einsum('bhtk,bhsk,bhtsk->bhts', qc, kc, decay)
        o_intra = jnp.einsum('bhts,bhsv->bhtv', scores, vc)
        b_last = bcum[:, :, -1:, :]
        new_state = (jnp.exp(b_last[:, :, 0, :])[..., None] * state
                     + jnp.einsum('bhsk,bhsv->bhkv', kc * jnp.exp(b_last - bcum), vc))
        return new_state, o_inter + o_intra

    s0 = jnp.zeros((bsz, HG_HEADS, HG_DK, HG_DK), f32)
    _, o = lax.scan(step, s0, (to_chunks(qs), to_chunks(k), to_chunks(v), to_chunks(log_f)))
    o = o.transpose(1, 0, 3, 2, 4).reshape(bsz, seq, HG_HEADS, HG_DK)
    gate = jax.nn.silu(g.astype(f32)).reshape(bsz, seq, HG_HEADS, HG_DK)
    o = _rmsnorm_2(o, gn_w) * gate
    return o.reshape(bsz, seq, HG_WIDTH)

def _s5(u, a_re, a_im, log_dt, b_re, b_im, c_re, c_im, d_skip, w_glu, b_glu):
    bsz, seq, _ = u.shape
    f32 = jnp.float32
    uf = u.astype(f32).reshape(bsz, seq, S5_GROUPS, S5_GROUP)
    ar = a_re.astype(f32)
    ai = a_im.astype(f32)
    dt = jnp.exp(log_dt.astype(f32))[:, None]
    mag = jnp.exp(ar * dt)
    abar_re = mag * jnp.cos(ai * dt)
    abar_im = mag * jnp.sin(ai * dt)
    den = ar * ar + ai * ai
    nr = abar_re - 1.0
    ni = abar_im
    coef_re = ((nr * ar + ni * ai) / den)[..., None]
    coef_im = ((ni * ar - nr * ai) / den)[..., None]
    br = b_re.astype(f32)
    bi = b_im.astype(f32)
    bb_re = coef_re * br - coef_im * bi
    bb_im = coef_re * bi + coef_im * br
    bu_re = jnp.einsum('bsgh,gph->bsgp', uf, bb_re)
    bu_im = jnp.einsum('bsgh,gph->bsgp', uf, bb_im)
    a_re_t = jnp.broadcast_to(abar_re, bu_re.shape)
    a_im_t = jnp.broadcast_to(abar_im, bu_im.shape)

    def combine(e1, e2):
        a1r, a1i, x1r, x1i = e1
        a2r, a2i, x2r, x2i = e2
        return (a2r * a1r - a2i * a1i,
                a2r * a1i + a2i * a1r,
                a2r * x1r - a2i * x1i + x2r,
                a2r * x1i + a2i * x1r + x2i)

    _, _, xr, xi = lax.associative_scan(combine, (a_re_t, a_im_t, bu_re, bu_im), axis=1)
    y = (jnp.einsum('bsgp,ghp->bsgh', xr, c_re.astype(f32))
         - jnp.einsum('bsgp,ghp->bsgh', xi, c_im.astype(f32)))
    y = y.reshape(bsz, seq, S5_WIDTH) + d_skip.astype(f32) * uf.reshape(bsz, seq, S5_WIDTH)
    y = jax.nn.gelu(y, approximate=False)
    y = y * jax.nn.sigmoid(y @ w_glu.astype(f32) + b_glu.astype(f32))
    return y.astype(u.dtype)

def _peer(h, w_q, keys1, keys2, u_tab, v_tab):
    bsz, seq, d = h.shape
    tb = PEER_TOKEN_BLOCK
    blocks = h.reshape(-1, tb, d)
    kk = PEER_TOPK * PEER_TOPK

    def block(hb):
        qh = (hb @ w_q).reshape(tb, PEER_HEADS, 2, PEER_HALF)
        s1 = jnp.einsum('thd,nd->thn', qh[:, :, 0], keys1)
        s2 = jnp.einsum('thd,nd->thn', qh[:, :, 1], keys2)
        v1, i1 = lax.top_k(s1, PEER_TOPK)
        v2, i2 = lax.top_k(s2, PEER_TOPK)
        cand = (v1[..., :, None] + v2[..., None, :]).reshape(tb, PEER_HEADS, kk)
        cidx = (i1[..., :, None] * PEER_NKEYS + i2[..., None, :]).reshape(tb, PEER_HEADS, kk)
        best, pos = lax.top_k(cand, PEER_TOPK)
        eidx = jnp.take_along_axis(cidx, pos, axis=-1)
        gates = jax.nn.softmax(best.astype(jnp.float32), axis=-1).astype(hb.dtype)
        act = jax.nn.gelu(jnp.einsum('td,thkd->thk', hb, u_tab[eidx]), approximate=False)
        return jnp.einsum('thk,thkd->td', gates * act, v_tab[eidx])

    return lax.map(block, blocks).reshape(bsz, seq, d)

def second_inputs(seed: int = 0) -> dict:
    key = jax.random.key(seed)
    ks = jax.random.split(key, 26)
    f32 = jnp.float32

    def nrm(k, shape, std):
        return std * jax.random.normal(k, shape, f32)

    L = DEPTH_2
    D = D_MODEL
    G = S5_GROUPS
    P = S5_STATE
    return {
        'x': nrm(ks[0], (BATCH, SEQ, D), 1.0),
        'c': nrm(ks[1], (BATCH, D), 1.0),
        'ada_w': nrm(ks[2], (L, D, 6 * D), 0.5 * D ** -0.5),
        'ada_b': nrm(ks[3], (L, 6 * D), 0.01),
        'norm_mix_w': 1.0 + nrm(ks[4], (L, D), 0.02),
        'norm_ffn_w': 1.0 + nrm(ks[5], (L, D), 0.02),
        'w_in': nrm(ks[6], (L, D, IN_WIDTH), D ** -0.5),
        'w_out': nrm(ks[7], (L, MIX_WIDTH, D), MIX_WIDTH ** -0.5),
        'hg_lower_bounds': nrm(ks[8], (L + 1, HG_WIDTH), 0.1),
        'hg_gnorm_w': 1.0 + nrm(ks[9], (L, HG_DK), 0.02),
        's5_a_re': -0.5 + nrm(ks[10], (L, G, P), 0.01),
        's5_a_im': math.pi * jnp.arange(P, dtype=f32) + nrm(ks[11], (L, G, P), 0.01),
        's5_log_dt': jax.random.uniform(ks[12], (L, G), f32, math.log(1e-3), math.log(1e-1)),
        's5_b_re': nrm(ks[13], (L, G, P, S5_GROUP), (2 * S5_GROUP) ** -0.5),
        's5_b_im': nrm(ks[14], (L, G, P, S5_GROUP), (2 * S5_GROUP) ** -0.5),
        's5_c_re': nrm(ks[15], (L, G, S5_GROUP, P), 0.25),
        's5_c_im': nrm(ks[16], (L, G, S5_GROUP, P), 0.25),
        's5_d': nrm(ks[17], (L, S5_WIDTH), 0.5),
        's5_glu_w': nrm(ks[18], (L, S5_WIDTH, S5_WIDTH), S5_WIDTH ** -0.5),
        's5_glu_b': nrm(ks[19], (L, S5_WIDTH), 0.01),
        'peer_wq': nrm(ks[20], (L, D, PEER_HEADS * PEER_QDIM), D ** -0.5),
        'peer_keys1': nrm(ks[21], (L, PEER_NKEYS, PEER_HALF), PEER_HALF ** -0.5),
        'peer_keys2': nrm(ks[22], (L, PEER_NKEYS, PEER_HALF), PEER_HALF ** -0.5),
        'peer_u': nrm(ks[23], (L, PEER_EXPERTS, D), D ** -0.5),
        'peer_v': nrm(ks[24], (L, PEER_EXPERTS, D), PEER_HEADS ** -0.5),
        'final_norm_w': 1.0 + nrm(ks[25], (D,), 0.02),
    }

def second_block(x, c, ada_w, ada_b, norm_mix_w, norm_ffn_w, w_in, w_out, hg_lower_bounds,
              hg_gnorm_w, s5_a_re, s5_a_im, s5_log_dt, s5_b_re, s5_b_im, s5_c_re, s5_c_im,
              s5_d, s5_glu_w, s5_glu_b, peer_wq, peer_keys1, peer_keys2, peer_u, peer_v,
              final_norm_w):
    cond = jax.nn.silu(c)
    lb_all = jnp.cumsum(jax.nn.softmax(hg_lower_bounds.astype(jnp.float32), axis=0), axis=0)
    for l in range(DEPTH_2):
        mod = (cond @ ada_w[l] + ada_b[l])[:, None, :]
        sh1, sc1, gt1, sh2, sc2, gt2 = jnp.split(mod, 6, axis=-1)
        h = _rmsnorm_2(x, norm_mix_w[l]) * (1.0 + sc1) + sh1
        proj = h @ w_in[l]
        q, f_logit, i, g, u = jnp.split(
            proj, [HG_WIDTH, 2 * HG_WIDTH, 3 * HG_WIDTH, 4 * HG_WIDTH], axis=-1)
        o_hg = _hgrn2(q, f_logit, i, g, lb_all[l], hg_gnorm_w[l]).astype(x.dtype)
        o_s5 = _s5(u, s5_a_re[l], s5_a_im[l], s5_log_dt[l], s5_b_re[l], s5_b_im[l],
                   s5_c_re[l], s5_c_im[l], s5_d[l], s5_glu_w[l], s5_glu_b[l])
        mixed = jnp.concatenate([o_hg, o_s5], axis=-1) @ w_out[l]
        x = x + gt1 * mixed
        h2 = _rmsnorm_2(x, norm_ffn_w[l]) * (1.0 + sc2) + sh2
        x = x + gt2 * _peer(h2, peer_wq[l], peer_keys1[l], peer_keys2[l], peer_u[l], peer_v[l])
    return _rmsnorm_2(x, final_norm_w)


def setup_inputs(seed=0):
    out = dict(first_inputs(seed))
    for name, value in second_inputs(seed + 1).items():
        if name != "x":
            out[name + "_2"] = value
    return out


def reference(
    x, c, ctx, c_ctx, w_ada, b_ada, norm_g, w_in, ml_gate_b, ml_head_g, da_lam, da_head_g,
    w_br_ml, w_br_da, w_br_fn, w_out, w_ffn_in, w_ffn_out, final_g, c_2, ada_w_2, ada_b_2,
    norm_mix_w_2, norm_ffn_w_2, w_in_2, w_out_2, hg_lower_bounds_2, hg_gnorm_w_2, s5_a_re_2,
    s5_a_im_2, s5_log_dt_2, s5_b_re_2, s5_b_im_2, s5_c_re_2, s5_c_im_2, s5_d_2, s5_glu_w_2,
    s5_glu_b_2, peer_wq_2, peer_keys1_2, peer_keys2_2, peer_u_2, peer_v_2, final_norm_w_2,
):
    x = first_block(
        x, c, ctx, c_ctx, w_ada, b_ada, norm_g, w_in, ml_gate_b, ml_head_g, da_lam, da_head_g,
        w_br_ml, w_br_da, w_br_fn, w_out, w_ffn_in, w_ffn_out, final_g,
    )
    return second_block(
        x, c_2, ada_w_2, ada_b_2, norm_mix_w_2, norm_ffn_w_2, w_in_2, w_out_2,
        hg_lower_bounds_2, hg_gnorm_w_2, s5_a_re_2, s5_a_im_2, s5_log_dt_2, s5_b_re_2,
        s5_b_im_2, s5_c_re_2, s5_c_im_2, s5_d_2, s5_glu_w_2, s5_glu_b_2, peer_wq_2,
        peer_keys1_2, peer_keys2_2, peer_u_2, peer_v_2, final_norm_w_2,
    )


_drawn_inputs = setup_inputs


def setup_inputs(seed=0):
    import zlib

    import numpy as np

    out = dict(_drawn_inputs(seed))
    spreads = {}
    factors = {'norm_g': 4.022,
     'ml_head_g': 8.0,
     'da_lam': 6.959,
     'da_head_g': 8.0,
     'ada_b_2': 5.743,
     'norm_mix_w_2': 8.0,
     'norm_ffn_w_2': 49.148,
     'hg_lower_bounds_2': 8.0,
     'hg_gnorm_w_2': 24.313,
     's5_a_re_2': 64.0,
     's5_a_im_2': 26.696,
     's5_log_dt_2': 31.848,
     's5_b_re_2': 36.52,
     's5_b_im_2': 37.2,
     's5_c_re_2': 38.416,
     's5_c_im_2': 31.856,
     's5_glu_w_2': 6.065,
     's5_glu_b_2': 64.0,
     'final_norm_w_2': 8.389}
    for name, (base, spread) in spreads.items():
        noise = np.random.default_rng([zlib.crc32(name.encode()), seed]).standard_normal(out[name].shape)
        drawn = base * np.exp(spread * noise) if base else spread * noise
        out[name] = __import__('jax').numpy.asarray(drawn.astype(out[name].dtype))
    for name, factor in factors.items():
        out[name] = (out[name] * factor).astype(out[name].dtype)
    return out
```

```python
import math
from contextlib import ExitStack, contextmanager

import numpy as np
import concourse.bass as bass
from concourse import mybir

F32 = mybir.dt.float32
U32 = mybir.dt.uint32
ALU = mybir.AluOpType
ACT = mybir.ActivationFunctionType
AX = mybir.AxisListType

P = 128
D = 1024
KT = D // P
NCTX, NLAT = 256, 256
T = NCTX + NLAT
DEPTH = 2
EPS = 1e-6
CHUNK = 256
SLOTS = 4
BANKS = 8

ML_HEADS, ML_D = 4, 256
DA_HEADS, DA_DH = 8, 64
FN_GROUPS, FN_C = 4, 256
D_FF = -(-8 * D // (3 * 256)) * 256
COL_Q, COL_K, COL_V, COL_O, COL_GATE = 0, 1024, 2048, 3072, 4096
COL_DAQ = COL_GATE + 4 * ML_HEADS
COL_DAK, COL_DAV = COL_DAQ + 1024, COL_DAQ + 2048
COL_FN = COL_DAV + 1024
COL_MERGE = COL_FN + 1024

HG_HEADS, HG_W, HG_SUB = 4, 512, 16
HG_BLOCKS = NLAT // HG_SUB
S5_G, S5_H, S5_P = 32, 16, 64
S5_TILES = S5_G * S5_P // P
S5_STEPS = NLAT.bit_length() - 1
PEER_H, PEER_K, PEER_N = 8, 16, 128
PEER_SLOTS = PEER_H * PEER_K
PEER_RING = 4

VEC = {}


def _pack_columns():
    at = 0
    for name, width in (("c", 24), ("b_ada", 2 * 48), ("norm_g", 2 * 2 * KT), ("ml_head_g", 2 * KT), ("da_head_g", 2 * KT),
                        ("final_g", KT), ("ada_b_2", 48), ("norm_mix", KT), ("norm_ffn", KT), ("final_norm", KT),
                        ("gnorm", 1), ("s5_d", 4), ("glu_b", 4), ("bounds", 2 * 4), ("lam", 2 * 4 * DA_DH),
                        ("gate_b", 2 * 4), ("s5_are", S5_TILES), ("s5_aim", S5_TILES), ("s5_dt", S5_TILES)):
        VEC[name] = (at, width)
        at += width
    return at


N_VEC = _pack_columns()

CST = {}


def _constant_columns():
    at = 0
    for name, width in (("ident", P), ("ones", P), ("upper", P), ("lower", P), ("turn", P), ("cos", NLAT), ("sin", NLAT),
                        ("dft", 2 * 3 * FN_C), ("pick", HG_SUB * HG_SUB), ("inner", HG_HEADS * NLAT), ("iota", PEER_K)):
        CST[name] = (at, width)
        at += width
    return at


N_CST = _constant_columns()


class Chain:

    def __init__(self, engine, semaphore):
        self.engine, self.semaphore, self.n = engine, semaphore, 0

    def mark(self, instruction):
        instruction.then_inc(self.semaphore, 1)
        self.n += 1
        return self.n

    def wait(self, n=None):
        self.engine.wait_ge(self.semaphore, self.n if n is None else n)

    def __call__(self, instruction):
        self.mark(instruction)
        self.wait()


class Core:

    def __init__(self, nc, ctx):
        self.nc = nc

        def sb(name, shape, dtype=F32):
            return ctx.enter_context(nc.sbuf_tensor(name, shape, dtype))

        self.cst = sb("constants_sb", [P, N_CST])
        self.vec = sb("vectors_sb", [P, N_VEC])
        self.x = sb("stream", [P, KT, T])
        self.h = sb("normed", [P, KT, T])
        self.big = sb("branches", [P, 3 * KT, T])
        self.mg = sb("merged", [P, KT, T])
        self.ring = sb("weight_ring", [P, SLOTS, KT, CHUNK])
        self.mod = sb("modulation", [P, 48, 2])
        self.modA = sb("norm_scales", [P, 2, KT])
        self.cond = sb("condition", [P, 3, KT])
        self.lam = sb("lambda", [P, 16])
        self.work = sb("work", [P, 15360])
        self.banks = [ctx.enter_context(nc.psum_tensor(f"bank{i}", [P, 512], F32)) for i in range(BANKS)]

        def sem(name):
            return ctx.enter_context(nc.semaphore(name))

        self.loaded = [sem(f"loaded{i}") for i in range(SLOTS)]
        self.slot_used = sem("slot_used")
        self.product = sem("product")
        self.drained = sem("drained")
        self.vec_done = sem("vec_done")
        self.act_done = sem("act_done")
        self.pool_done = sem("pool_done")
        self.vec_out = sem("vec_out")
        self.act_out = sem("act_out")
        self.pe_out = sem("pe_out")
        self.side_loaded = sem("side_loaded")
        self.stored = sem("stored")
        self.maxima = sem("maxima")
        self.turned = sem("turned")
        self.u_free = [sem(f"u_free{i}") for i in range(PEER_RING)]
        self.v_free = [sem(f"v_free{i}") for i in range(PEER_RING)]
        self.sems = [*self.loaded, *self.u_free, *self.v_free, self.slot_used, self.product, self.drained, self.vec_done, self.act_done, self.pool_done,
                     self.vec_out, self.act_out, self.pe_out, self.side_loaded, self.stored, self.maxima,
                     self.turned]
        nums = sorted(s.num for s in self.sems)
        assert nums == list(range(nums[0], nums[0] + len(nums)))
        self.sem_range = range(nums[0], nums[-1] + 1)

        self.gathered = [sem(f"gathered{i}") for i in range(2 * PEER_RING)]

    def constant(self, name):
        at, width = CST[name]
        return self.cst[:, at:at + width]

    def vector(self, name, lo=0, hi=None):
        at, width = VEC[name]
        return self.vec[:, at + lo:at + (width if hi is None else hi)]

    @contextmanager
    def stage(self):
        with self.nc.Block(no_gpsimd_drain=True) as block:
            yield block
        self.nc.gpsimd.sem_clear(self.sem_range)
        self.nc.all_engine_barrier(sem_only=True)

    def carve(self, *shapes):
        at, out = 0, []
        for shape in shapes:
            n = math.prod(shape)
            view = self.work[:, at:at + n]
            if len(shape) == 2:
                view = view.rearrange("p (a b) -> p a b", b=shape[1])
            elif len(shape) == 3:
                view = view.rearrange("p (a b c) -> p a b c", b=shape[1], c=shape[2])
            out.append(view)
            at += n
        assert at <= 15360, at
        return out


def rows(w):
    return w.rearrange("(k p) n -> p k n", p=P)


def project(c, weight, col0, n_chunks, rhs, n, evacuate, on="vector", splits=((0, KT),)):
    pieces = len(splits)
    looped = pieces == 1 and n_chunks > 8
    whole = n_chunks // SLOTS

    def run(engine, body):
        if not looped:
            for s in range(n_chunks):
                body(0, s)
            return
        for s in range(SLOTS):
            body(0, s)
        with engine.Fori(0, whole - 1) as j:
            for s in range(SLOTS):
                body(j * SLOTS + SLOTS, s)
        for s in range(n_chunks % SLOTS):
            body(whole * SLOTS, s)

    def later(base, index, depth):
        return not isinstance(base, int) or base + index >= depth

    with c.stage() as block:
        @block.sync
        def _(sp):
            def load(base, s):
                for piece, (k0, nk) in enumerate(splits):
                    i = s * pieces + piece
                    if later(base, i, SLOTS):
                        held, its_piece = (i - SLOTS) // pieces, (i - SLOTS) % pieces
                        if its_piece == pieces - 1:
                            sp.wait_ge(c.product, base * 2 + 2 * (held + 1))
                        else:
                            sp.wait_ge(c.slot_used, held * (pieces - 1) + its_piece + 1)
                    sp.dma_start(c.ring[:, i % SLOTS, 0:nk, :],
                                 weight[:, k0:k0 + nk, bass.ds(base * CHUNK + (s * CHUNK + col0), CHUNK)]
                                 ).then_inc(c.loaded[i % SLOTS], 16)

            run(sp, load)

        @block.tensor
        def _(pe):
            def multiply(base, s):
                for piece, (k0, nk) in enumerate(splits):
                    i = s * pieces + piece
                    pe.wait_ge(c.loaded[i % SLOTS], base * (16 // SLOTS) + 16 * (i // SLOTS + 1))
                    for half in range(2):
                        tile = 2 * s + half
                        if piece == 0 and later(base * 2, tile, BANKS):
                            pe.wait_ge(c.drained, base * 2 + (tile + 1 - BANKS))
                        for k in range(nk):
                            last = pe.matmul(c.banks[tile % BANKS][:, 0:n], c.ring[:, i % SLOTS, k, half * P:(half + 1) * P],
                                             rhs[:, k0 + k, :], start=piece == 0 and k == 0,
                                             stop=piece == pieces - 1 and k == nk - 1)
                        if half == 1 and piece < pieces - 1:
                            last.then_inc(c.slot_used, 1)
                        if piece == pieces - 1:
                            last.then_inc(c.product, 1)

            run(pe, multiply)

        def drain(engine):
            def one(base, s):
                for half in range(2):
                    tile = 2 * s + half
                    engine.wait_ge(c.product, base * 2 + (tile + 1))
                    evacuate(engine, c.banks[tile % BANKS][:, 0:n], base * 2 + tile).then_inc(c.drained, 1)

            run(engine, one)

        by_name = {"vector": block.vector, "scalar": block.scalar}
        by_name[on](drain)


def moving(r, lo, hi):
    return r[:, :, lo:hi]


def load_small(c, a):
    with c.stage() as block:
        @block.sync
        def _(sp):
            sp.dma_start(c.vec[:], a["vectors"]).then_inc(c.side_loaded, 16)
            sp.dma_start(c.cst[:], a["constants"]).then_inc(c.loaded[0], 16)
            sp.dma_start(c.x[:], a["residual"]).then_inc(c.loaded[1], 16)

        @block.scalar
        def _(act):
            act.wait_ge(c.side_loaded, 16)
            act.activation(c.cond[:], c.vector("c").rearrange("p (a k) -> p a k", a=3), ACT.Silu)
            act.wait_ge(c.vec_out, 1)
            act.activation(c.lam[:, 8:12], c.lam[:, 0:4], ACT.Exp).then_inc(c.act_out, 1)

        @block.vector
        def _(dve):
            chain = Chain(dve, c.vec_done)
            dve.wait_ge(c.side_loaded, 16)
            lq = c.vector("lam").rearrange("p (l a d) -> p l a d", l=DEPTH, a=4)
            scratch = c.work[:, 0:DA_DH]
            for layer in range(DEPTH):
                for pair in range(2):
                    col = 2 * layer + pair
                    chain(dve.tensor_tensor(scratch, lq[:, layer, 2 * pair, :], lq[:, layer, 2 * pair + 1, :], ALU.mult))
                    chain(dve.reduce_sum(c.lam[:, col:col + 1], scratch, AX.X))
            dve.sem_inc(c.vec_out, 1)
            dve.wait_ge(c.act_out, 1)
            for layer in range(DEPTH):
                init = 0.8 - 0.6 * math.exp(-0.3 * layer)
                e = c.lam[:, 8 + 2 * layer:10 + 2 * layer]
                chain(dve.tensor_tensor(c.lam[:, 12 + layer:13 + layer], e[:, 0:1], e[:, 1:2], ALU.subtract))
                chain(dve.tensor_scalar(c.lam[:, 14 + layer:15 + layer], c.lam[:, 12 + layer:13 + layer], init, None, ALU.add))
            dve.wait_ge(c.loaded[0], 16)
            dve.wait_ge(c.loaded[1], 16)


def adaln(c, weight, conditions, bias, n):
    rhs = conditions
    flat = c.mod[:].rearrange("p t a -> p (t a)")
    project(c, weight, 0, 6 * D // CHUNK, rhs, n,
            lambda e, bank, tile: e.tensor_copy(flat[:, bass.ds(tile * 2, n)], bank))
    with c.stage() as block:
        @block.vector
        def _(dve):
            for a in range(n):
                dve.tensor_tensor(c.mod[:, :, a], c.mod[:, :, a], bias, ALU.add)


def norm(c, source, out, gain, parts, tiles=KT, spread=D, modulated=True):
    lo, hi = parts[0][0], parts[-1][1]
    n = hi - lo
    mean, rstd = c.carve((n,), (n,))
    with c.stage() as block:
        @block.scalar
        def _(act):
            for k in range(tiles):
                act.activation(out[:, k, lo:hi], source[:, k, lo:hi], ACT.Square).then_inc(c.act_out, 1)
            act.wait_ge(c.vec_out, 1)
            act.activation(rstd, mean, ACT.Sqrt).then_inc(c.act_done, 1)

        @block.tensor
        def _(pe):
            for k in range(tiles):
                pe.wait_ge(c.act_out, k + 1)
                last = pe.matmul(c.banks[0][:, 0:n], c.constant("ones"), out[:, k, lo:hi], start=k == 0, stop=k == tiles - 1)
            last.then_inc(c.product, 1)

        @block.vector
        def _(dve):
            chain = Chain(dve, c.vec_done)
            if modulated:
                for i, (_, _, which, _, scale) in enumerate(parts):
                    chain(dve.scalar_tensor_tensor(c.modA[:, i, :], c.mod[:, scale:scale + tiles, which], 1.0, gain,
                                                   ALU.add, ALU.mult))
            dve.wait_ge(c.product, 1)
            chain(dve.tensor_scalar(mean, c.banks[0][:, 0:n], 1.0 / spread, EPS, ALU.mult, ALU.add))
            dve.reciprocal(mean, mean).then_inc(c.vec_out, 1)
            dve.wait_ge(c.act_done, 1)
            scaled = [chain.mark(dve.tensor_tensor(out[:, k, lo:hi], source[:, k, lo:hi], rstd, ALU.mult))
                      for k in range(tiles)]
            for k in range(tiles):
                chain.wait(scaled[k])
                for i, (a, b, which, shift, _) in enumerate(parts):
                    if modulated:
                        dve.tensor_scalar(out[:, k, a:b], out[:, k, a:b], c.modA[:, i, k:k + 1],
                                          c.mod[:, shift + k, which:which + 1], ALU.mult, ALU.add)
                    else:
                        dve.tensor_scalar(out[:, k, a:b], out[:, k, a:b], gain[:, k:k + 1], None, ALU.mult)


def mlstm(c, a, layer, w_in, full):
    lo = 0 if full else NCTX
    n = T - lo
    gcol, gh, headg, gates, logf, e, b, g, m, ones, out_rows, wg = c.carve(
        (2 * 4, 4), (2 * 4,), (2,), (4, T), (2, T), (2, T), (2, T), (2, T), (2, T), (T,), (4, T), (KT, 16))
    H = ML_HEADS
    with c.stage() as block:
        @block.sync
        def _(sp):
            sp.dma_start(wg, w_in[:, :, COL_GATE:COL_GATE + 16]).then_inc(c.side_loaded, 16)
            sp.wait_ge(c.vec_out, 3)
            sp.wait_ge(c.act_out, 5)
            sp.dma_start(a["rows"], out_rows[0:H]).then_inc(c.stored, 16)
            sp.wait_ge(c.stored, 16)

        @block.tensor
        def _(pe):
            pe.wait_ge(c.side_loaded, 16)
            for j in range(4):
                for k in range(KT):
                    last = pe.matmul(c.banks[j][0:H, :], wg[:, k, H * j:H * j + H], c.h[:, k, :], start=k == 0, stop=k == KT - 1)
                last.then_inc(c.product, 1)
            pe.wait_ge(c.vec_out, 1)
            for d in range(2):
                for j in range(4):
                    last = pe.matmul(c.banks[4][:, (4 * d + j) * 4:(4 * d + j + 1) * 4], g[0:H, d, j * P:(j + 1) * P],
                                     c.constant("ident")[0:H, 0:H], start=True, stop=True)
            last.then_inc(c.product, 1)

        @block.scalar
        def _(act):
            for j in range(4):
                act.wait_ge(c.product, j + 1)
                act.activation(gates[0:H, j, :], c.banks[j][0:H, :], ACT.Identity,
                               bias=c.vector("gate_b", 4 * layer + j, 4 * layer + j + 1)[0:H]).then_inc(c.act_out, 1)
            act.wait_ge(c.vec_done, 4)
            act.activation(e[0:H], e[0:H], ACT.Exp, scale=-1.0).then_inc(c.act_done, 1)
            act.wait_ge(c.act_done, 1)
            act.activation(e[0:H], e[0:H], ACT.Ln, bias=1.0).then_inc(c.act_done, 1)
            act.wait_ge(c.vec_out, 2)
            act.activation(out_rows[0:H, 2:4], m[0:H], ACT.Exp, scale=-1.0).then_inc(c.act_out, 1)

        @block.vector
        def _(dve):
            chain = Chain(dve, c.vec_done)
            dve.wait_ge(c.act_out, 4)
            for d in range(2):
                f = gates[0:H, 2 * d + 1, :]
                chain(dve.tensor_scalar(e[0:H, d], f, -1.0, None, ALU.mult))
                chain(dve.tensor_tensor(e[0:H, d], e[0:H, d], f, ALU.max))
            chain(dve.memset(ones[0:H], 1.0))
            dve.wait_ge(c.act_done, 2)
            for d in range(2):
                chain(dve.scalar_tensor_tensor(logf[0:H, d], gates[0:H, 2 * d + 1, :], 0.0, e[0:H, d], ALU.min, ALU.subtract))
            chain(dve.tensor_tensor_scan(b[0:H, 0], ones[0:H], logf[0:H, 0], 0.0, ALU.mult, ALU.add))
            chain(dve.tensor_tensor_scan(b[0:H, 1, NCTX - 1::-1], ones[0:H, 0:NCTX], logf[0:H, 1, NCTX - 1::-1], 0.0,
                                         ALU.mult, ALU.add))
            chain(dve.tensor_tensor_scan(b[0:H, 1, T - 1:NCTX - 1:-1], ones[0:H, 0:NLAT], logf[0:H, 1, T - 1:NCTX - 1:-1],
                                         b[0:H, 1, 0:1], ALU.mult, ALU.add))
            for d in range(2):
                chain(dve.tensor_tensor(g[0:H, d], gates[0:H, 2 * d, :], b[0:H, d], ALU.subtract))
            dve.sem_inc(c.vec_out, 1)
            chain(dve.tensor_tensor_scan(m[0:H, 0], g[0:H, 0], g[0:H, 0], 0.0, ALU.max, ALU.max))
            chain(dve.tensor_tensor_scan(m[0:H, 1, NCTX - 1::-1], g[0:H, 1, NCTX - 1::-1], g[0:H, 1, NCTX - 1::-1], 0.0,
                                         ALU.max, ALU.max))
            chain(dve.tensor_tensor_scan(m[0:H, 1, T - 1:NCTX - 1:-1], g[0:H, 1, T - 1:NCTX - 1:-1],
                                         g[0:H, 1, T - 1:NCTX - 1:-1], m[0:H, 1, 0:1], ALU.max, ALU.max))
            chain(dve.tensor_scalar(out_rows[0:H, 0:2], m[0:H], -1.0, None, ALU.mult))
            chain(dve.tensor_tensor(m[0:H], m[0:H], b[0:H], ALU.add))
            dve.sem_inc(c.vec_out, 1)
            dve.wait_ge(c.product, 5)
            dve.tensor_copy(gcol, c.banks[4][:, 0:32].rearrange("p (x h) -> p x h", h=4)).then_inc(c.vec_out, 1)
            dve.wait_ge(c.act_out, 5)

    _, _, _, q, k, v, o, bc, A, E, den, hs, sq = c.carve(
        (2 * 4, 4), (2 * 4,), (2,), (2, T), (2, T), (4, ML_D), (2, T), (4, T), (4, T), (2, T), (2, T), (2, T), (2, T))
    runs = [[(j, max(j * P, lo), T) for j in range(4)],
            [(1, lo, T), (0, 0, P), (0, NCTX, T), (3, NCTX, T), (2, NCTX, NCTX + P)]]
    runs = [[r for r in rs if r[1] < r[2] and (full or r[1] >= NCTX)] for rs in runs]
    sources = [(j, max(lo, 0 if j < 2 else NCTX), T) for j in range(4)]
    with c.nc.Fori(0, ML_HEADS) as head:
        with c.stage() as block:
            @block.sync
            def _(sp):
                for s, col in enumerate((COL_Q, COL_K, COL_O, COL_V)):
                    sp.dma_start(c.ring[:, s], w_in[:, :, bass.ds(head * CHUNK + col, CHUNK)]).then_inc(c.loaded[s], 16)

            @block.tensor
            def _(pe):
                for s, (first, width) in enumerate(((lo, n), (0, T), (lo, n))):
                    pe.wait_ge(c.loaded[s], 16)
                    for half in range(2):
                        for kk in range(KT):
                            last = pe.matmul(c.banks[2 * s + half][:, 0:width], c.ring[:, s, kk, half * P:(half + 1) * P],
                                             c.h[:, kk, first:T], start=kk == 0, stop=kk == KT - 1)
                        last.then_inc(c.product, 1)
                pe.wait_ge(c.loaded[3], 16)
                for j in range(4):
                    for kk in range(KT):
                        last = pe.matmul(c.banks[6 + j // 2][:, (j % 2) * ML_D:(j % 2 + 1) * ML_D],
                                         c.h[:, kk, j * P:(j + 1) * P], c.ring[:, 3, kk, :], start=kk == 0, stop=kk == KT - 1)
                    last.then_inc(c.product, 1)

            @block.vector
            def _(dve):
                for half in range(2):
                    dve.wait_ge(c.product, half + 1)
                    dve.tensor_copy(q[:, half, lo:T], c.banks[half][:, 0:n])
                for half in range(2):
                    dve.wait_ge(c.product, half + 3)
                    dve.tensor_scalar(k[:, half, :], c.banks[2 + half][:], ML_D ** -0.5, None, ALU.mult)
                dve.tensor_copy(gh, gcol[:, :, bass.ds(head, 1)].rearrange("p x h -> p (x h)"))
                dve.tensor_copy(headg, c.vector("ml_head_g")[:, bass.ds(head * 2 + layer * KT, 2)])
                for j in range(0, 4, 2):
                    dve.wait_ge(c.product, 8 + j)
                    dve.tensor_copy(v[:, j:j + 2, :], c.banks[6 + j // 2][:].rearrange("p (j e) -> p j e", j=2))

            @block.scalar
            def _(act):
                act.dma_start(bc, a["rows"][bass.ds(head, 1)].rearrange("h a t -> (h a) t").partition_broadcast(P)
                              ).then_inc(c.side_loaded, 16)
                for half in range(2):
                    act.wait_ge(c.product, half + 5)
                    act.activation(o[:, half, lo:T], c.banks[4 + half][:, 0:n], ACT.Sigmoid)
                act.wait_ge(c.side_loaded, 16)

        for d in range(2):
            with c.stage() as block:
                @block.tensor
                def _(pe):
                    for j, a0, a1 in sources:
                        for half in range(2):
                            last = pe.matmul(c.banks[j][:, a0 - lo:a1 - lo], k[:, half, j * P:(j + 1) * P], q[:, half, a0:a1],
                                             start=half == 0, stop=half == 1)
                        last.then_inc(c.product, 1)
                    pe.wait_ge(c.vec_out, 4)
                    for bank, lhs in ((4, 0), (5, 1), (6, None)):
                        for i, (j, a0, a1) in enumerate(runs[d]):
                            weights = c.constant("ones") if lhs is None else v[:, j, lhs * P:(lhs + 1) * P]
                            last = pe.matmul(c.banks[bank][:, a0 - lo:a1 - lo], weights, A[:, j, a0:a1], start=i == 0,
                                             stop=i == len(runs[d]) - 1)
                    last.then_inc(c.pe_out, 1)

                @block.scalar
                def _(act):
                    for i, (j, a0, a1) in enumerate(sources):
                        act.wait_ge(c.vec_done, i + 1)
                        act.activation(A[:, j, a0:a1], A[:, j, a0:a1], ACT.Exp).then_inc(c.act_out, 1)
                    act.wait_ge(c.pe_out, 1)
                    act.activation(den[:, d, lo:T], c.banks[6][:, 0:n], ACT.Abs).then_inc(c.act_out, 1)

                @block.vector
                def _(dve):
                    chain = Chain(dve, c.vec_done)
                    mask = c.constant("upper" if d == 0 else "lower")
                    for j, a0, a1 in sources:
                        chain.mark(dve.tensor_scalar(A[:, j, a0:a1], bc[:, d, a0:a1], gh[:, 4 * d + j:4 * d + j + 1], 0.0,
                                                     ALU.add, ALU.min))
                    for i, (j, a0, a1) in enumerate(sources):
                        dve.wait_ge(c.act_out, i + 1)
                        dve.wait_ge(c.product, i + 1)
                        chain(dve.tensor_tensor(A[:, j, a0:a1], A[:, j, a0:a1], c.banks[j][:, a0 - lo:a1 - lo], ALU.mult))
                        diagonal = A[:, j, j * P:(j + 1) * P]
                        if j * P >= lo:
                            chain(dve.tensor_tensor(diagonal, diagonal, mask, ALU.mult))
                        dve.sem_inc(c.vec_out, 1)
                    dve.wait_ge(c.act_out, 5)
                    chain(dve.tensor_tensor(den[:, d, lo:T], den[:, d, lo:T], bc[:, 2 + d, lo:T], ALU.max))
                    chain(dve.reciprocal(den[:, d, lo:T], den[:, d, lo:T]))
                    for half in range(2):
                        out = hs if d == 0 else E
                        chain(dve.tensor_tensor(out[:, half, lo:T], c.banks[4 + half][:, 0:n], den[:, d, lo:T], ALU.mult))
                        if d == 1:
                            chain(dve.tensor_tensor(hs[:, half, lo:T], hs[:, half, lo:T], E[:, half, lo:T], ALU.add))

        with c.stage() as block:
            @block.scalar
            def _(act):
                for half in range(2):
                    act.activation(sq[:, half, lo:T], hs[:, half, lo:T], ACT.Square).then_inc(c.act_out, 1)
                act.wait_ge(c.vec_out, 1)
                act.activation(E[:, 0, lo:T], den[:, 0, lo:T], ACT.Sqrt).then_inc(c.act_out, 1)

            @block.tensor
            def _(pe):
                for half in range(2):
                    pe.wait_ge(c.act_out, half + 1)
                    last = pe.matmul(c.banks[0][:, 0:n], c.constant("ones"), sq[:, half, lo:T], start=half == 0, stop=half == 1)
                last.then_inc(c.product, 1)

            @block.vector
            def _(dve):
                chain = Chain(dve, c.vec_done)
                dve.wait_ge(c.product, 1)
                chain(dve.tensor_scalar(den[:, 0, lo:T], c.banks[0][:, 0:n], 1.0 / ML_D, EPS, ALU.mult, ALU.add))
                dve.reciprocal(den[:, 0, lo:T], den[:, 0, lo:T]).then_inc(c.vec_out, 1)
                dve.wait_ge(c.act_out, 3)
                flat = c.big[:].rearrange("p k t -> p (k t)")
                for half in range(2):
                    chain(dve.scalar_tensor_tensor(sq[:, half, lo:T], hs[:, half, lo:T], headg[:, half:half + 1],
                                                   E[:, 0, lo:T], ALU.mult, ALU.mult))
                    dve.tensor_tensor(flat[:, bass.ds(head * (2 * T) + (half * T + lo), n)], sq[:, half, lo:T],
                                      o[:, half, lo:T], ALU.mult)


def diff_attention(c, a, layer, w_in, full):
    lo = 0 if full else NCTX
    n = T - lo
    q, k, v, rot, pr, aw, aT, stats, headg, osb, sq, rs = c.carve(
        (2, T), (2, T), (4, 2 * P), (2, NLAT), (4, T), (2, T), (4, T), (4, 8), (2,), (T,), (T,), (2, T))
    keep = 1.0 - (0.8 - 0.6 * math.exp(-0.3 * layer))
    with c.nc.Fori(0, DA_HEADS // 2) as pair:
        with c.stage() as block:
            @block.sync
            def _(sp):
                for s, col in enumerate((COL_DAQ, COL_DAK, COL_DAV)):
                    sp.dma_start(c.ring[:, s], w_in[:, :, bass.ds(pair * CHUNK + col, CHUNK)]).then_inc(c.loaded[s], 16)

            @block.tensor
            def _(pe):
                for s, first in enumerate((lo, 0)):
                    pe.wait_ge(c.loaded[s], 16)
                    for half in range(2):
                        for kk in range(KT):
                            last = pe.matmul(c.banks[2 * s + half][:, first:T], c.ring[:, s, kk, half * P:(half + 1) * P],
                                             c.h[:, kk, first:T], start=kk == 0, stop=kk == KT - 1)
                        last.then_inc(c.product, 1)
                pe.wait_ge(c.loaded[2], 16)
                for j in range(4):
                    for kk in range(KT):
                        last = pe.matmul(c.banks[4 + j // 2][:, (j % 2) * 2 * P:(j % 2 + 1) * 2 * P],
                                         c.h[:, kk, j * P:(j + 1) * P], c.ring[:, 2, kk, :], start=kk == 0, stop=kk == KT - 1)
                    last.then_inc(c.product, 1)
                for i, x in enumerate((q, k)):
                    pe.wait_ge(c.vec_done, 2 * i + 2)
                    for half in range(2):
                        pe.matmul(c.banks[6 + i][:, half * NLAT:(half + 1) * NLAT], c.constant("turn"), x[:, half, NCTX:T],
                                  start=True, stop=True).then_inc(c.pe_out, 1)

            @block.vector
            def _(dve):
                chain = Chain(dve, c.vec_done)
                for i, (x, first) in enumerate(((q, lo), (k, 0))):
                    for half in range(2):
                        dve.wait_ge(c.product, 2 * i + half + 1)
                        chain.mark(dve.tensor_copy(x[:, half, first:T], c.banks[2 * i + half][:, first:T]))
                for j in range(0, 4, 2):
                    dve.wait_ge(c.product, 6 + j)
                    chain.mark(dve.tensor_copy(v[:, j:j + 2, :], c.banks[4 + j // 2][:].rearrange("p (j e) -> p j e", j=2)))
                for i, x in enumerate((q, k)):
                    for half in range(2):
                        dve.wait_ge(c.pe_out, 2 * i + 2)
                        chain(dve.tensor_tensor(rot[:, half], c.banks[6 + i][:, half * NLAT:(half + 1) * NLAT],
                                                c.constant("sin"), ALU.mult))
                        chain(dve.tensor_tensor(x[:, half, NCTX:T], x[:, half, NCTX:T], c.constant("cos"), ALU.mult))
                        chain(dve.tensor_tensor(x[:, half, NCTX:T], x[:, half, NCTX:T], rot[:, half], ALU.add))
                dve.tensor_scalar(headg, c.vector("da_head_g")[:, bass.ds(pair * 2 + layer * KT, 2)], keep, None, ALU.mult)

        tiles = [t for t in range(4) if t * P >= lo]
        for half in range(2):
            with c.stage() as block:
                def keys(t):
                    return NCTX if t < 2 else T

                def turn(pe, i):
                    t = tiles[i]
                    pe.wait_ge(c.vec_out, i + 1)
                    if i >= 2:
                        pe.wait_ge(c.drained, i - 1)
                    for j in range(keys(t) // P):
                        last = pe.transpose(c.banks[4 + i % 2][:, j * P:(j + 1) * P], aw[:, i % 2, j * P:(j + 1) * P],
                                            c.constant("ident"))
                    last.then_inc(c.turned, 1)

                @block.tensor
                def _(pe):
                    for i, t in enumerate(tiles):
                        for m in range(2):
                            u = 2 * i + m
                            if u >= 4:
                                pe.wait_ge(c.act_out, u - 3)
                            pe.matmul(c.banks[u % 4][:, 0:keys(t)], q[m * 64:(m + 1) * 64, half, t * P:(t + 1) * P],
                                      k[m * 64:(m + 1) * 64, half, 0:keys(t)], start=True, stop=True).then_inc(c.product, 1)
                        if i >= 1:
                            turn(pe, i - 1)
                    turn(pe, len(tiles) - 1)
                    pe.wait_ge(c.drained, len(tiles))
                    groups = ([(0, NCTX, 2)] if full else []) + [(NCTX, T, 4)]
                    for a0, a1, sources in groups:
                        for j in range(sources):
                            last = pe.matmul(c.banks[6][:, a0 - lo:a1 - lo], v[:, j, half * P:(half + 1) * P], aT[:, j, a0:a1],
                                             start=j == 0, stop=j == sources - 1)
                    last.then_inc(c.pe_out, 1)
                    pe.wait_ge(c.act_done, 1)
                    pe.matmul(c.banks[7][:, 0:n], c.constant("ones"), sq[:, lo:T], start=True, stop=True).then_inc(c.pe_out, 1)

                @block.scalar
                def _(act):
                    for i, t in enumerate(tiles):
                        for m in range(2):
                            u = 2 * i + m
                            act.wait_ge(c.maxima, u + 1)
                            if i >= 2:
                                act.wait_ge(c.vec_out, i - 1)
                            act.activation(pr[:, u % 4, 0:keys(t)], c.banks[u % 4][:, 0:keys(t)], ACT.Exp,
                                           bias=stats[:, i, m:m + 1], scale=DA_DH ** -0.5,
                                           accum_out=stats[:, i, 2 + m:3 + m]).then_inc(c.act_out, 1)
                    act.wait_ge(c.pe_out, 1)
                    act.activation(sq[:, lo:T], c.banks[6][:, 0:n], ACT.Square).then_inc(c.act_done, 1)
                    act.wait_ge(c.vec_out, len(tiles) + 1)
                    act.activation(rs[:, 1, lo:T], rs[:, 0, lo:T], ACT.Sqrt).then_inc(c.act_done, 1)

                @block.vector
                def _(dve):
                    chain = Chain(dve, c.vec_done)

                    def maxima(i):
                        for m in range(2):
                            dve.wait_ge(c.product, 2 * i + m + 1)
                            chain(dve.reduce_max(stats[:, i, 6 + m:7 + m], c.banks[(2 * i + m) % 4][:, 0:keys(tiles[i])], AX.X))
                            dve.tensor_scalar(stats[:, i, m:m + 1], stats[:, i, 6 + m:7 + m], -(DA_DH ** -0.5), None,
                                              ALU.mult).then_inc(c.maxima, 1)

                    def combine(i):
                        w = keys(tiles[i])
                        dve.wait_ge(c.act_out, 2 * i + 2)
                        chain(dve.reciprocal(stats[:, i, 4:6], stats[:, i, 2:4]))
                        chain(dve.tensor_tensor(stats[:, i, 5:6], stats[:, i, 5:6], c.lam[:, 14 + layer:15 + layer], ALU.mult))
                        p0, p1 = (pr[:, (2 * i + m) % 4, 0:w] for m in range(2))
                        chain(dve.tensor_scalar(p1, p1, stats[:, i, 5:6], None, ALU.mult))
                        if i >= 2:
                            dve.wait_ge(c.turned, i - 1)
                        dve.scalar_tensor_tensor(aw[:, i % 2, 0:w], p0, stats[:, i, 4:5], p1, ALU.mult,
                                                 ALU.subtract).then_inc(c.vec_out, 1)

                    def spread(i):
                        t, w = tiles[i], keys(tiles[i])
                        dve.wait_ge(c.turned, i + 1)
                        dve.tensor_copy(aT[:, 0:w // P, t * P:(t + 1) * P],
                                        c.banks[4 + i % 2][:, 0:w].rearrange("p (j t) -> p j t", t=P)).then_inc(c.drained, 1)

                    maxima(0)
                    for i in range(len(tiles)):
                        if i + 1 < len(tiles):
                            maxima(i + 1)
                        combine(i)
                        if i >= 1:
                            spread(i - 1)
                    spread(len(tiles) - 1)
                    dve.wait_ge(c.pe_out, 2)
                    chain(dve.tensor_scalar(rs[:, 0, lo:T], c.banks[7][:, 0:n], 1.0 / P, EPS, ALU.mult, ALU.add))
                    dve.reciprocal(rs[:, 0, lo:T], rs[:, 0, lo:T]).then_inc(c.vec_out, 1)
                    dve.wait_ge(c.act_done, 2)
                    flat = c.big[:].rearrange("p k t -> p (k t)")
                    dve.scalar_tensor_tensor(flat[:, bass.ds(pair * (2 * T) + ((KT + half) * T + lo), n)],
                                             c.banks[6][:, 0:n], headg[:, half:half + 1], rs[:, 1, lo:T], ALU.mult, ALU.mult)


def fourier(c, w_in, full):
    lo = 0 if full else NCTX
    z, ab = c.carve((2, T), (4, 2 * FN_C))
    dft = c.constant("dft").rearrange("p (k n) -> p k n", k=2)
    tiles = [t for t in range(4) if t * P >= lo]
    with c.nc.Fori(0, FN_GROUPS) as group:
        with c.stage() as block:
            @block.sync
            def _(sp):
                sp.dma_start(c.ring[:, 0], w_in[:, :, bass.ds(group * CHUNK + COL_FN, CHUNK)]).then_inc(c.loaded[0], 16)

            @block.tensor
            def _(pe):
                pe.wait_ge(c.loaded[0], 16)
                for half in range(2):
                    for k in range(KT):
                        last = pe.matmul(c.banks[half][:, lo:T], c.ring[:, 0, k, half * P:(half + 1) * P], c.h[:, k, lo:T],
                                         start=k == 0, stop=k == KT - 1)
                    last.then_inc(c.product, 1)
                pe.wait_ge(c.vec_done, 2)
                for i, t in enumerate(tiles):
                    for k in range(2):
                        last = pe.matmul(c.banks[2 + i][:], z[:, k, t * P:(t + 1) * P], dft[:, k, 0:2 * FN_C], start=k == 0,
                                         stop=k == 1)
                    last.then_inc(c.product, 1)
                pe.wait_ge(c.vec_done, 2 + len(tiles))
                for half in range(2):
                    for stream in range(lo // NCTX, 2):
                        for i in range(4):
                            j, part = i // 2, i % 2
                            last = pe.matmul(c.banks[6 + half][:, stream * NCTX:(stream + 1) * NCTX],
                                             ab[:, 2 * stream + j, part * FN_C + half * P:part * FN_C + (half + 1) * P],
                                             dft[:, j, part * 2 * FN_C:part * 2 * FN_C + FN_C], start=i == 0, stop=i == 3)
                    last.then_inc(c.product, 1)

            @block.vector
            def _(dve):
                chain = Chain(dve, c.vec_done)
                for half in range(2):
                    dve.wait_ge(c.product, half + 1)
                    chain.mark(dve.tensor_copy(z[:, half, lo:T], c.banks[half][:, lo:T]))
                for i, t in enumerate(tiles):
                    dve.wait_ge(c.product, 3 + i)
                    chain.mark(dve.tensor_copy(ab[:, t, :], c.banks[2 + i][:]))
                flat = c.big[:].rearrange("p k t -> p (k t)")
                for half in range(2):
                    dve.wait_ge(c.product, 3 + len(tiles) + half)
                    dve.tensor_copy(flat[:, bass.ds(group * (2 * T) + ((2 * KT + half) * T + lo), T - lo)],
                                    c.banks[6 + half][:, lo:T])


def merge(c, a, layer, w_in, full):
    lo = 0 if full else NCTX
    n = T - lo
    gate, = c.carve((KT, T))
    for i, name in enumerate(("w_br_ml", "w_br_da", "w_br_fn")):
        project(c, w_in, COL_MERGE + i * D, D // CHUNK, moving(c.h, lo, T), n,
                lambda e, bank, tile: e.activation(gate[:, tile, lo:T], bank, ACT.Sigmoid), on="scalar")

        def gated(e, bank, tile):
            out = c.mg[:, tile, lo:T]
            if i == 0:
                return e.tensor_tensor(out, bank, gate[:, tile, lo:T], ALU.mult)
            return e.tensor_tensor(gate[:, tile, lo:T], bank, gate[:, tile, lo:T], ALU.mult)

        project(c, rows(a[name][layer]), 0, D // CHUNK, moving(c.big[:, i * KT:(i + 1) * KT, :], lo, T), n, gated)
        if i:
            with c.stage() as block:
                @block.vector
                def _(dve):
                    for k in range(KT):
                        dve.tensor_tensor(c.mg[:, k, lo:T], c.mg[:, k, lo:T], gate[:, k, lo:T], ALU.add)


def add_gated(c, weight, rhs, parts, gate_tile, splits=((0, KT),)):
    lo = parts[0][0]

    def evacuate(e, bank, tile):
        for first, last, which in parts:
            out = c.x[:, tile, first:last]
            ins = e.scalar_tensor_tensor(out, bank[:, first - lo:last - lo], c.mod[:, gate_tile + tile, which:which + 1], out,
                                         ALU.mult, ALU.add)
        return ins

    project(c, weight, 0, D // CHUNK, rhs, T - lo, evacuate, splits=splits)


def feed_forward(c, a, layer, parts):
    lo = parts[0][0]
    n = T - lo
    flat = c.big[:].rearrange("p k t -> p (k t)")
    w = rows(a["w_ffn_in"][layer])
    project(c, w, 0, D_FF // CHUNK, moving(c.h, lo, T), n,
            lambda e, bank, tile: e.activation(flat[:, bass.ds(tile * T + lo, n)], bank, ACT.Silu), on="scalar")
    project(c, w, D_FF, D_FF // CHUNK, moving(c.h, lo, T), n,
            lambda e, bank, tile: e.tensor_tensor(flat[:, bass.ds(tile * T + lo, n)], bank,
                                                  flat[:, bass.ds(tile * T + lo, n)], ALU.mult))
    ks = D_FF // P
    add_gated(c, rows(a["w_ffn_out"][layer]), moving(c.big[:, 0:ks, :], lo, T), parts, 5 * KT,
              splits=tuple((k0, min(KT, ks - k0)) for k0 in range(0, ks, KT)))


def first_block(c, a, stop):
    for layer in range(DEPTH):
        full = layer < DEPTH - 1
        streams = [(0, NCTX, 0), (NCTX, T, 1)]
        kept = streams if full else streams[1:]
        w_in = rows(a["w_in"][layer])
        conditions = c.cond[:, 0:2, :].rearrange("p a k -> p k a")
        adaln(c, rows(a["w_ada"][layer]), conditions, c.vector("b_ada", 48 * layer, 48 * (layer + 1)), 2)
        gains = [c.vector("norm_g", (2 * layer + i) * KT, (2 * layer + i + 1) * KT) for i in range(2)]
        norm(c, c.x, c.h, gains[0], [(f, l, w, 0, KT) for f, l, w in streams])
        if stop == f"norm{layer}":
            return False
        mlstm(c, a, layer, w_in, full)
        diff_attention(c, a, layer, w_in, full)
        fourier(c, w_in, full)
        if stop == f"branches{layer}":
            return False
        merge(c, a, layer, w_in, full)
        add_gated(c, rows(a["w_out"][layer]), moving(c.mg, kept[0][0], T), kept, 2 * KT)
        if stop == f"mix{layer}":
            return False
        norm(c, c.x, c.h, gains[1], [(f, l, w, 3 * KT, 4 * KT) for f, l, w in kept])
        feed_forward(c, a, layer, kept)
        if stop == f"ffn{layer}":
            return False
    norm(c, c.x, c.h, c.vector("final_g"), [(NCTX, T, 1, 0, 0)], modulated=False)
    return True



def hgrn(c, a):
    w_in = rows(a["w_in_2"][0])
    hs = moving(c.h, NCTX, T)
    H, B, L = HG_HEADS, HG_BLOCKS, HG_SUB
    N = H * NLAT
    big = c.big[:].rearrange("p k t -> p (k t)")
    q, f, g, u, kk, lf, bl, e1, qe, kend, sq, rs = (big[:, i * N:(i + 1) * N] for i in range(12))
    vt, v16, at, pairs, state, lb = c.carve((2, HG_W), (B, HG_W), (N,), (2, N), (2, HG_W), (6, 4))
    kt = c.ring[:].rearrange("p s k n -> p (s k n)")
    per_tile = NLAT
    for buffer, col, func in ((q, 0, ACT.Silu), (g, 3 * HG_W, ACT.Silu), (f, HG_W, ACT.Sigmoid), (u, 4 * HG_W, ACT.Copy)):
        project(c, w_in, col, HG_W // CHUNK, hs, NLAT,
                lambda e, bank, tile: e.activation(buffer[:, tile * per_tile:(tile + 1) * per_tile], bank, func), on="scalar")

    with c.stage() as block:
        @block.sync
        def _(sp):
            for s in range(2):
                sp.dma_start(c.ring[:, s], w_in[:, :, 2 * HG_W + s * CHUNK:2 * HG_W + (s + 1) * CHUNK]
                             ).then_inc(c.loaded[s], 16)
            sp.wait_ge(c.vec_out, 2)
            for b in range(B):
                sp.dma_start(v16[0:L, b, :], vt[(b % 8) * L:(b % 8 + 1) * L, b // 8, :]).then_inc(c.stored, 16)
            sp.wait_ge(c.stored, 16 * B)

        @block.tensor
        def _(pe):
            for s in range(2):
                pe.wait_ge(c.loaded[s], 16)
                for t in range(2):
                    for k in range(KT):
                        last = pe.matmul(c.banks[t][:, s * CHUNK:(s + 1) * CHUNK], hs[:, k, t * P:(t + 1) * P],
                                         c.ring[:, s, k, :], start=k == 0, stop=k == KT - 1)
            last.then_inc(c.product, 1)

        @block.vector
        def _(dve):
            dve.wait_ge(c.product, 1)
            for t in range(2):
                dve.tensor_copy(vt[:, t, :], c.banks[t][:]).then_inc(c.vec_out, 1)

    def blocks(x):
        return x.rearrange("p (b l) -> p b l", l=L)

    with c.stage() as block:
        @block.scalar
        def _(act):
            act.wait_ge(c.vec_out, 1)
            act.activation(lb[:, 1:3, :], lb[:, 1:3, :], ACT.Exp).then_inc(c.act_out, 1)
            act.wait_ge(c.vec_out, 2)
            act.activation(lf, f, ACT.Ln).then_inc(c.act_out, 1)
            act.wait_ge(c.vec_out, 3)
            act.activation(e1, bl, ACT.Exp).then_inc(c.act_out, 1)
            act.wait_ge(c.vec_out, 4)
            act.activation(kend, kend, ACT.Exp).then_inc(c.act_out, 1)

        @block.vector
        def _(dve):
            chain = Chain(dve, c.vec_done)
            b0, b1 = c.vector("bounds", 0, 4), c.vector("bounds", 4, 8)
            chain(dve.tensor_tensor(lb[:, 0, :], b0, b1, ALU.max))
            chain(dve.tensor_tensor(lb[:, 1, :], b0, lb[:, 0, :], ALU.subtract))
            chain(dve.tensor_tensor(lb[:, 2, :], b1, lb[:, 0, :], ALU.subtract))
            dve.sem_inc(c.vec_out, 1)
            dve.wait_ge(c.act_out, 1)
            chain(dve.tensor_tensor(lb[:, 3, :], lb[:, 1, :], lb[:, 2, :], ALU.add))
            chain(dve.reciprocal(lb[:, 3, :], lb[:, 3, :]))
            chain(dve.tensor_tensor(lb[:, 4, :], lb[:, 1, :], lb[:, 3, :], ALU.mult))
            chain(dve.tensor_scalar(lb[:, 5, :], lb[:, 4, :], -1.0, 1.0, ALU.mult, ALU.add))
            for h in range(H):
                part = f[:, h * NLAT:(h + 1) * NLAT]
                chain(dve.tensor_scalar(part, part, lb[:, 5, h:h + 1], lb[:, 4, h:h + 1], ALU.mult, ALU.add))
            dve.sem_inc(c.vec_out, 1)
            dve.tensor_scalar(kk, f, -1.0, 1.0, ALU.mult, ALU.add)
            chain(dve.tensor_scalar(q, q, P ** -0.5, None, ALU.mult))
            dve.wait_ge(c.act_out, 2)
            chain(dve.tensor_tensor_scan(bl, c.constant("inner"), lf, 0.0, ALU.mult, ALU.add))
            dve.sem_inc(c.vec_out, 1)
            chain(dve.tensor_tensor(blocks(kend), blocks(bl)[:, :, L - 1:L].to_broadcast([P, H * B, L]), blocks(bl),
                                    ALU.subtract))
            dve.sem_inc(c.vec_out, 1)
            dve.wait_ge(c.act_out, 3)
            dve.tensor_tensor(qe, q, e1, ALU.mult)
            dve.wait_ge(c.act_out, 4)
            dve.tensor_tensor(kend, kend, kk, ALU.mult)

    with c.stage() as block:
        pick = c.constant("pick").rearrange("p (j l) -> p j l", l=L)

        @block.vector
        def _(dve):
            chain = Chain(dve, c.vec_done)

            def first(j):
                w = L - j
                part = blocks(pairs[:, j % 2])[:, :, 0:w]
                if j >= 2:
                    dve.wait_ge(c.product, j - 1)
                dve.tensor_tensor(part, blocks(bl)[:, :, j:L], blocks(bl)[:, :, j:j + 1].to_broadcast([P, H * B, w]),
                                  ALU.subtract).then_inc(c.vec_out, 1)

            first(0)
            for j in range(L):
                w = L - j
                part = blocks(pairs[:, j % 2])[:, :, 0:w]
                if j + 1 < L:
                    first(j + 1)
                dve.wait_ge(c.act_out, j + 1)
                chain(dve.tensor_tensor(part, part, blocks(q)[:, :, j:L], ALU.mult))
                chain(dve.tensor_tensor(part, part, blocks(kk)[:, :, j:j + 1].to_broadcast([P, H * B, w]), ALU.mult))
            dve.wait_ge(c.product, L)
            for half in range(2):
                dve.tensor_copy(at[0:L, half * 512:(half + 1) * 512], c.banks[half][0:L, :])

        @block.scalar
        def _(act):
            for j in range(L):
                part = blocks(pairs[:, j % 2])[:, :, 0:L - j]
                act.wait_ge(c.vec_out, j + 1)
                act.activation(part, part, ACT.Exp).then_inc(c.act_out, 1)
            for r in range(H * B // 4):
                act.wait_ge(c.turned, r + 1)
                act.activation(kt[0:L, r * 512:(r + 1) * 512], c.banks[2 + r % 6][0:L, :], ACT.Copy).then_inc(c.drained, 1)

        @block.tensor
        def _(pe):
            for j in range(L):
                pe.wait_ge(c.vec_done, 2 * j + 2)
                for half in range(2):
                    last = pe.matmul(blocks(c.banks[half][0:L, :])[:, :, j:L], pick[:, j, :],
                                     blocks(pairs[:, j % 2])[:, half * 32:(half + 1) * 32, 0:L - j],
                                     start=j == 0, stop=j == L - 1)
                last.then_inc(c.product, 1)
            for r in range(H * B // 4):
                if r >= 6:
                    pe.wait_ge(c.drained, r - 5)
                for i in range(4):
                    last = pe.transpose(c.banks[2 + r % 6][0:L, i * P:(i + 1) * P], blocks(kend)[:, 4 * r + i, :],
                                        c.constant("ident"))
                last.then_inc(c.turned, 1)

    with c.stage() as block:
        @block.tensor
        def _(pe):
            for b in range(B):
                if b:
                    pe.wait_ge(c.vec_done, 2 * b)
                for h in range(H):
                    out = c.banks[h // 2][:, (h % 2) * NLAT + b * L:(h % 2) * NLAT + (b + 1) * L]
                    pe.matmul(out, v16[0:L, b, h * P:(h + 1) * P], at[0:L, h * NLAT + b * L:h * NLAT + (b + 1) * L],
                              start=True, stop=b == 0)
                    if b:
                        pe.matmul(out, state[:, b % 2, h * P:(h + 1) * P], qe[:, h * NLAT + b * L:h * NLAT + (b + 1) * L],
                                  start=False, stop=True)
                for h in range(H):
                    last = pe.matmul(c.banks[2 + b % 2][:, h * P:(h + 1) * P], kt[0:L, (h * B + b) * P:(h * B + b + 1) * P],
                                     v16[0:L, b, h * P:(h + 1) * P], start=True, stop=True)
                last.then_inc(c.product, 1)
            for half in range(2):
                pe.wait_ge(c.act_out, half + 1)
                pe.matmul(c.banks[4 + half][:], c.constant("ones"), sq[:, half * 512:(half + 1) * 512], start=True,
                          stop=True).then_inc(c.pe_out, 1)

        @block.vector
        def _(dve):
            chain = Chain(dve, c.vec_done)
            decay = e1.rearrange("p (h b l) -> p h b l", h=H, l=L)
            for b in range(B):
                after, before = state[:, (b + 1) % 2], state[:, b % 2]
                if b == 0:
                    chain(dve.memset(before, 0.0))
                else:
                    chain(dve.tensor_tensor(after.rearrange("p (h v) -> p h v", h=H), before.rearrange("p (h v) -> p h v", h=H),
                                            decay[:, :, b, L - 1:L].to_broadcast([P, H, P]), ALU.mult))
                dve.wait_ge(c.product, b + 1)
                if b == 0:
                    chain(dve.tensor_copy(after, c.banks[2][:]))
                else:
                    chain(dve.tensor_tensor(after, after, c.banks[2 + b % 2][:], ALU.add))
            for half in range(2):
                part = slice(half * 512, (half + 1) * 512)
                dve.wait_ge(c.pe_out, half + 1)
                chain(dve.tensor_scalar(rs[:, part], c.banks[4 + half][:], 1.0 / P, EPS, ALU.mult, ALU.add))
                dve.reciprocal(rs[:, part], rs[:, part]).then_inc(c.vec_out, 1)
            for half in range(2):
                part = slice(half * 512, (half + 1) * 512)
                dve.wait_ge(c.act_out, 3 + half)
                chain(dve.scalar_tensor_tensor(sq[:, part], c.banks[half][:], c.vector("gnorm"), rs[:, part], ALU.mult,
                                               ALU.mult))
                dve.tensor_tensor(c.mg[:, 2 * half:2 * half + 2, 0:NLAT],
                                  sq[:, part].rearrange("p (h t) -> p h t", h=2),
                                  g[:, part].rearrange("p (h t) -> p h t", h=2), ALU.mult)

        @block.scalar
        def _(act):
            act.wait_ge(c.product, B)
            for half in range(2):
                act.activation(sq[:, half * 512:(half + 1) * 512], c.banks[half][:], ACT.Square).then_inc(c.act_out, 1)
            for half in range(2):
                act.wait_ge(c.vec_out, half + 1)
                part = rs[:, half * 512:(half + 1) * 512]
                act.activation(part, part, ACT.Sqrt).then_inc(c.act_out, 1)


S5_PARAMS = 2 + 3 * S5_STEPS


def s5(c, a):
    big = c.big[:].rearrange("p k t -> p (k t)")
    N = S5_TILES
    u = big[:, 3 * HG_HEADS * NLAT:4 * HG_HEADS * NLAT].rearrange("p (i t) -> p i t", i=4)
    y = big[:, 4 * HG_HEADS * NLAT:5 * HG_HEADS * NLAT].rearrange("p (i t) -> p i t", i=4)
    gate = big[:, 5 * HG_HEADS * NLAT:6 * HG_HEADS * NLAT].rearrange("p (i t) -> p i t", i=4)
    wb, wc, params, s, fixed, pad, nc_im = c.carve((2, 4, P), (2, N, 2 * S5_H), (N, S5_PARAMS), (16, N), (2, S5_PARAMS),
                                                   (12, P + NLAT), (N, 2 * S5_H))
    x = c.ring[:].rearrange("p s k n -> p (s k n)").rearrange("p (i r t) -> p i r t", i=N, r=2)
    two_pi = 2.0 * math.pi
    hi = 6.28125
    mid = float(np.float32(two_pi - hi))
    low = two_pi - hi - mid
    magic = 1.5 * 2.0 ** 23

    with c.stage() as block:
        @block.sync
        def _(sp):
            sp.dma_start(wb, a["s5_b"].rearrange("r p i n -> p r i n")).then_inc(c.side_loaded, 16)
            sp.dma_start(wc, a["s5_c"].rearrange("r p i n -> p r i n")).then_inc(c.stored, 16)

        @block.tensor
        def _(pe):
            pe.wait_ge(c.side_loaded, 16)
            for i in range(N):
                rows_ = slice(32 * (i % 4), 32 * (i % 4) + 32)
                if i >= BANKS:
                    pe.wait_ge(c.drained, i - BANKS + 1)
                for r in range(2):
                    last = pe.matmul(c.banks[i % BANKS][:, r * NLAT:(r + 1) * NLAT], wb[rows_, r, i // 4, :],
                                     u[rows_, i // 4, :], start=True, stop=True)
                last.then_inc(c.product, 1)

        @block.scalar
        def _(act):
            act.activation(s[:, 0], c.vector("s5_dt"), ACT.Exp).then_inc(c.act_out, 1)
            act.wait_ge(c.vec_out, 1)
            act.activation(s[:, 2], s[:, 1], ACT.Exp).then_inc(c.act_out, 1)
            act.activation(s[:, 6], s[:, 4], ACT.Sin)
            act.activation(s[:, 7], s[:, 5], ACT.Sin).then_inc(c.act_out, 1)
            for i in range(N):
                act.wait_ge(c.product, i + 1)
                act.activation(x[:, i], c.banks[i % BANKS][:].rearrange("p (r t) -> p r t", r=2), ACT.Copy
                               ).then_inc(c.drained, 1)

        @block.vector
        def _(dve):
            chain = Chain(dve, c.vec_done)
            are, aim = c.vector("s5_are"), c.vector("s5_aim")
            dve.wait_ge(c.act_out, 1)
            chain(dve.tensor_tensor(s[:, 1], are, s[:, 0], ALU.mult))
            chain(dve.tensor_tensor(s[:, 3], aim, s[:, 0], ALU.mult))
            chain(dve.tensor_scalar(s[:, 8], s[:, 3], 1.0 / two_pi, magic, ALU.mult, ALU.add))
            chain(dve.tensor_scalar(s[:, 8], s[:, 8], magic, None, ALU.subtract))
            source = s[:, 3]
            for part in (hi, mid, low):
                chain(dve.scalar_tensor_tensor(s[:, 4], s[:, 8], -part, source, ALU.mult, ALU.add))
                source = s[:, 4]
            chain(dve.tensor_scalar(s[:, 4], s[:, 4], math.pi, -math.pi, ALU.min, ALU.max))
            chain(dve.tensor_scalar(s[:, 5], s[:, 4], math.pi / 2, None, ALU.add))
            chain(dve.tensor_scalar(s[:, 8], s[:, 5], math.pi, -two_pi, ALU.is_gt, ALU.mult))
            chain(dve.tensor_tensor(s[:, 5], s[:, 5], s[:, 8], ALU.add))
            chain(dve.tensor_scalar(s[:, 5], s[:, 5], math.pi, -math.pi, ALU.min, ALU.max))
            dve.sem_inc(c.vec_out, 1)
            dve.wait_ge(c.act_out, 3)
            power = [params[:, :, 2 + r * S5_STEPS:2 + (r + 1) * S5_STEPS] for r in range(3)]
            chain(dve.tensor_tensor(power[0][:, :, 0], s[:, 2], s[:, 7], ALU.mult))
            chain(dve.tensor_tensor(power[1][:, :, 0], s[:, 2], s[:, 6], ALU.mult))
            chain(dve.tensor_scalar(s[:, 9], power[0][:, :, 0], -1.0, None, ALU.add))
            ni = power[1][:, :, 0]
            chain(dve.tensor_tensor(s[:, 10], are, are, ALU.mult))
            chain(dve.tensor_tensor(s[:, 11], aim, aim, ALU.mult))
            chain(dve.tensor_tensor(s[:, 10], s[:, 10], s[:, 11], ALU.add))
            chain(dve.reciprocal(s[:, 10], s[:, 10]))
            for out, first, second, op in ((0, (s[:, 9], are), (ni, aim), ALU.add), (1, (ni, are), (s[:, 9], aim), ALU.subtract)):
                chain(dve.tensor_tensor(s[:, 11], *first, ALU.mult))
                chain(dve.tensor_tensor(s[:, 12], *second, ALU.mult))
                chain(dve.tensor_tensor(s[:, 11], s[:, 11], s[:, 12], op))
                chain(dve.tensor_tensor(params[:, :, out], s[:, 11], s[:, 10], ALU.mult))
            for k in range(1, S5_STEPS):
                re, im = power[0][:, :, k - 1], power[1][:, :, k - 1]
                chain(dve.tensor_tensor(s[:, 11], re, re, ALU.mult))
                chain(dve.tensor_tensor(s[:, 12], im, im, ALU.mult))
                chain(dve.tensor_tensor(power[0][:, :, k], s[:, 11], s[:, 12], ALU.subtract))
                chain(dve.tensor_tensor(s[:, 11], re, im, ALU.mult))
                chain(dve.tensor_scalar(power[1][:, :, k], s[:, 11], 2.0, None, ALU.mult))
            chain(dve.tensor_scalar(power[2], power[1], -1.0, None, ALU.mult))
            chain(dve.memset(pad, 0.0))
            dve.wait_ge(c.stored, 16)
            dve.tensor_scalar(nc_im, wc[:, 1], -1.0, None, ALU.mult)

    with c.nc.Fori(0, N // 2) as turn:
        with c.stage() as block:
            @block.vector
            def _(dve):
                chain = Chain(dve, c.vec_done)
                flat = c.ring[:].rearrange("p s k n -> p (s k n)")
                par = params.rearrange("p i n -> p (i n)")
                chain(dve.tensor_copy(fixed.rearrange("p i n -> p (i n)"), par[:, bass.ds(turn * (2 * S5_PARAMS), 2 * S5_PARAMS)]))

                def raw(i, r):
                    return flat[:, bass.ds(turn * (4 * NLAT) + (2 * i + r) * NLAT, NLAT)]

                def buffer(i, n, shift=0):
                    return pad[:, 6 * i + n, P - shift:P - shift + NLAT]

                def scalar(i, n):
                    return fixed[:, i, n:n + 1]

                def together(steps):
                    marks = [chain.mark(step(i)) for step in steps for i in range(2)]
                    chain.wait(marks[-1])

                together([lambda i: dve.tensor_scalar(buffer(i, 4), raw(i, 1), scalar(i, 1), None, ALU.mult),
                          lambda i: dve.tensor_scalar(buffer(i, 5), raw(i, 0), scalar(i, 1), None, ALU.mult)])
                together([lambda i: dve.scalar_tensor_tensor(buffer(i, 0), raw(i, 0), scalar(i, 0), buffer(i, 4), ALU.mult,
                                                             ALU.subtract),
                          lambda i: dve.scalar_tensor_tensor(buffer(i, 1), raw(i, 1), scalar(i, 0), buffer(i, 5), ALU.mult,
                                                             ALU.add)])
                now = 0
                for k in range(S5_STEPS):
                    last = k == S5_STEPS - 1
                    n = now
                    together([lambda i: dve.scalar_tensor_tensor(buffer(i, 4), buffer(i, n + 1, 1 << k),
                                                                 scalar(i, 2 + 2 * S5_STEPS + k), buffer(i, n), ALU.mult, ALU.add),
                              lambda i: dve.scalar_tensor_tensor(buffer(i, 5), buffer(i, n, 1 << k),
                                                                 scalar(i, 2 + S5_STEPS + k), buffer(i, n + 1), ALU.mult, ALU.add)])
                    together([lambda i: dve.scalar_tensor_tensor(raw(i, 0) if last else buffer(i, 2 - n),
                                                                 buffer(i, n, 1 << k), scalar(i, 2 + k), buffer(i, 4),
                                                                 ALU.mult, ALU.add),
                              lambda i: dve.scalar_tensor_tensor(raw(i, 1) if last else buffer(i, 3 - n),
                                                                 buffer(i, n + 1, 1 << k), scalar(i, 2 + k), buffer(i, 5),
                                                                 ALU.mult, ALU.add)])
                    now = 2 - now

    with c.stage() as block:
        @block.tensor
        def _(pe):
            for i in range(N):
                out = c.banks[i // 4][32 * (i % 4):32 * (i % 4) + 32, 0:NLAT]
                pe.matmul(out, wc[:, 0, i, :], x[:, i, 0, :], start=True, stop=False)
                last = pe.matmul(out, nc_im[:, i, :], x[:, i, 1, :], start=False, stop=True)
                if i % 4 == 3:
                    last.then_inc(c.product, 1)

        @block.vector
        def _(dve):
            for i in range(4):
                dve.wait_ge(c.product, i + 1)
                dve.scalar_tensor_tensor(y[:, i], u[:, i], c.vector("s5_d", i, i + 1), c.banks[i][:, 0:NLAT], ALU.mult,
                                         ALU.add).then_inc(c.vec_out, 1)

        @block.scalar
        def _(act):
            for i in range(4):
                act.wait_ge(c.vec_out, i + 1)
                act.activation(y[:, i], y[:, i], ACT.Gelu)

    ks = HG_W // P
    project(c, rows(a["s5_glu_w_2"][0]), 0, HG_W // CHUNK, y, NLAT,
            lambda e, bank, tile: e.activation(gate[:, tile], bank, ACT.Sigmoid, bias=c.vector("glu_b", tile, tile + 1)),
            on="scalar", splits=((0, ks),))
    with c.stage() as block:
        @block.vector
        def _(dve):
            dve.tensor_tensor(c.mg[:, ks:2 * ks, 0:NLAT], y, gate, ALU.mult)


def peer(c, a):
    H, K, S = PEER_H, PEER_K, PEER_SLOTS
    LOWEST = -3.0e38
    big = c.big[:].rearrange("p k t -> p (k t)")
    qh = big[:, 0:16 * NLAT].rearrange("p (i t) -> p i t", i=16)
    scores = big[:, 16 * NLAT:32 * NLAT]
    tokens = big[:, 32 * NLAT:32 * NLAT + 2 * D].rearrange("p (t f) -> p t f", t=2)
    keys = big[:, 32 * NLAT + 2 * D:32 * NLAT + 2 * D + 2 * PEER_N].rearrange("p (r n) -> p r n", r=2)
    experts = big[:, 11008:11008 + 2 * S]
    gates = big[:, 11264:11264 + 2 * S]
    experts_u = experts.bitcast(U32)
    hs = moving(c.h, NCTX, T)
    project(c, rows(a["peer_wq_2"][0]), 0, 2 * H * P // CHUNK, hs, NLAT,
            lambda e, bank, tile: e.tensor_copy(qh[:, tile, :], bank))

    with c.stage() as block:
        @block.sync
        def _(sp):
            sp.dma_start(keys, a["keys"]).then_inc(c.side_loaded, 16)

        @block.tensor
        def _(pe):
            for r in range(4):
                for i in range(4):
                    t, k = (4 * r + i) // KT, (4 * r + i) % KT
                    last = pe.transpose(c.banks[r][:, i * P:(i + 1) * P], hs[:, k, t * P:(t + 1) * P], c.constant("ident"))
                last.then_inc(c.product, 1)
            pe.wait_ge(c.side_loaded, 16)
            for t in range(2):
                for i in range(2 * H):
                    n = (2 * H * t + i) // 4
                    if i % 4 == 0 and n >= 4:
                        pe.wait_ge(c.drained, n)
                    last = pe.matmul(c.banks[4 + n if n < 4 else n - 4][:, (i % 4) * P:(i % 4 + 1) * P],
                                     qh[:, i, t * P:(t + 1) * P], keys[:, i % 2, :], start=True, stop=True)
                    if i % 4 == 3:
                        last.then_inc(c.product, 1)

        @block.vector
        def _(dve):
            for r in range(4):
                dve.wait_ge(c.product, r + 1)
                dve.tensor_copy(tokens[:, r // 2, (r % 2) * 512:(r % 2 + 1) * 512], c.banks[r][:]).then_inc(c.drained, 1)
            for n in range(8):
                dve.wait_ge(c.product, 5 + n)
                dve.tensor_copy(scores[:, n * 512:(n + 1) * 512], c.banks[4 + n if n < 4 else n - 4][:]).then_inc(c.drained, 1)

    s, v, idx, idf, cand, best, less, pos, sel, eq, ef, small = c.carve(
        (2 * H, PEER_N), (2 * H, K), (2 * H, K), (2 * H, K), (H, K * K), (H, K), (H, K), (H, K), (2, S), (S, K), (2, S), (2, H))
    idx, pos = idx.bitcast(U32), pos.bitcast(U32)
    sel_u = sel.bitcast(U32)
    with c.nc.Fori(0, 2) as t:
        with c.stage() as block:
            @block.vector
            def _(dve):
                chain = Chain(dve, c.vec_done)
                chain(dve.tensor_copy(s.rearrange("p i n -> p (i n)"), scores[:, bass.ds(t * (2 * H * PEER_N), 2 * H * PEER_N)]))

                def best16(table, values, places, count):
                    for r in range(2):
                        part = slice(8 * r, 8 * r + 8)
                        for i in range(count):
                            done = chain.mark(dve.max(out=values[:, i, part], in_=table[:, i, :]))
                        chain.wait(done)
                        for i in range(count):
                            done = chain.mark(dve.max_index(out=places[:, i, part], in_max=values[:, i, part],
                                                            in_values=table[:, i, :]))
                        if r == 0:
                            chain.wait(done)
                            for i in range(count):
                                done = chain.mark(dve.match_replace(out=table[:, i, :], in_to_replace=values[:, i, part],
                                                                    in_values=table[:, i, :], imm_value=LOWEST))
                        chain.wait(done)

                best16(s, v, idx, 2 * H)
                chain(dve.tensor_copy(idf, idx))
                v4 = v.rearrange("p (h r) k -> p h r k", r=2)
                chain(dve.tensor_tensor(cand.rearrange("p h (x y) -> p h x y", y=K),
                                        v4[:, :, 0, :].unsqueeze(3).to_broadcast([P, H, K, K]),
                                        v4[:, :, 1, :].unsqueeze(2).to_broadcast([P, H, K, K]), ALU.add))
                best16(cand, best, pos, H)
                flat = pos.rearrange("p h k -> p (h k)")
                chain(dve.tensor_scalar(sel_u[:, 0], flat, 4, None, ALU.logical_shift_right))
                chain(dve.tensor_scalar(sel_u[:, 1], flat, K - 1, None, ALU.bitwise_and))
                chain(dve.tensor_copy(ef, sel_u))
                i4 = idf.rearrange("p (h r) k -> p h r k", r=2)
                for r in range(2):
                    chain(dve.tensor_tensor(eq, ef[:, r].unsqueeze(2).to_broadcast([P, S, K]),
                                            c.constant("iota").unsqueeze(1).to_broadcast([P, S, K]), ALU.is_equal))
                    e4 = eq.rearrange("p (h k) x -> p h k x", h=H)
                    chain(dve.tensor_tensor(e4, e4, i4[:, :, r, :].unsqueeze(2).to_broadcast([P, H, K, K]), ALU.mult))
                    chain(dve.tensor_reduce(sel[:, r], eq, AX.X, ALU.add))
                chain(dve.tensor_scalar(sel[:, 0], sel[:, 0], float(PEER_N), None, ALU.mult))
                chain(dve.tensor_tensor(experts_u[:, bass.ds(t * S, S)], sel[:, 0], sel[:, 1], ALU.add))
                chain(dve.tensor_tensor(less, best, best[:, :, 0:1].to_broadcast([P, H, K]), ALU.subtract))
                dve.sem_inc(c.vec_out, 1)
                dve.wait_ge(c.act_out, 1)
                chain(dve.reduce_sum(small[:, 0], less, AX.X))
                chain(dve.reciprocal(small[:, 1], small[:, 0]))
                dve.tensor_tensor(gates[:, bass.ds(t * S, S)].rearrange("p (h k) -> p h k", h=H), less,
                                  small[:, 1].unsqueeze(2).to_broadcast([P, H, K]), ALU.mult)

            @block.scalar
            def _(act):
                act.wait_ge(c.vec_out, 1)
                act.activation(less, less, ACT.Exp).then_inc(c.act_out, 1)

    R = PEER_RING
    urows, vrows, diag, place, dot, gl, w, gate4, acc = c.carve(
        (R, D), (R, D), (R, P), (R,), (R,), (R,), (R,), (R,), (D,))
    place_u = place.bitcast(U32)
    groups = S // R
    for t in range(2):
        with c.stage() as block:
            def run(engine, body):
                body(0)
                with engine.Fori(0, groups - 2) as j:
                    body(j + 1)
                body(groups - 1)

            had = 16 * groups * t

            @block.gpsimd
            def _(pool):
                def body(gr):
                    later = not isinstance(gr, int) or gr > 0
                    for r in range(R):
                        if later:
                            pool.wait_ge(c.u_free[r], 1)
                            pool.sem_clear(c.u_free[r])
                            pool.wait_ge(c.v_free[r], 1)
                            pool.sem_clear(c.v_free[r])
                        pool.tensor_copy(place_u[:, r:r + 1], experts_u[:, bass.ds(gr * R + (t * S + r), 1)]
                                         ).then_inc(c.pool_done, 1)
                        pool.wait_ge(c.pool_done, 1)
                        pool.sem_clear(c.pool_done)
                        for rows_, table, which in ((urows, "peer_u_2", 0), (vrows, "peer_v_2", R)):
                            pool.indirect_dma_start(
                                out=rows_[:, r, :], out_offset=None, in_=a[table][0],
                                in_offset=bass.IndirectOffsetOnAxis(ap=place_u[:, r:r + 1], axis=0)
                            ).then_inc(c.gathered[which + r], 16)

                run(pool, body)

            @block.vector
            def _(dve):
                def body(gr):
                    later = not isinstance(gr, int) or gr > 0
                    if later:
                        dve.wait_ge(c.act_out, gr * R)
                    dve.tensor_copy(gate4, gates[:, bass.ds(gr * R + t * S, R)]).then_inc(c.vec_done, 1)
                    for r in range(R):
                        dve.wait_ge(c.gathered[r], gr * 16 + (16 + had))
                        dve.tensor_tensor_reduce(out=urows[:, r, :], in0=urows[:, r, :], in1=tokens[:, t, :], scale=1.0,
                                                 scalar=0.0, op0=ALU.mult, op1=ALU.add, accum_out=dot[:, r:r + 1]
                                                 ).then_inc(c.vec_out, 1)

                run(dve, body)

            @block.scalar
            def _(act):
                def body(gr):
                    later = not isinstance(gr, int) or gr > 0
                    act.wait_ge(c.vec_done, gr + 1)
                    for r in range(R):
                        act.wait_ge(c.vec_out, gr * R + (r + 1))
                        act.sem_inc(c.u_free[r], 1)
                        act.activation(gl[:, r:r + 1], dot[:, r:r + 1], ACT.Gelu).then_inc(c.act_done, 1)
                        act.wait_ge(c.act_done, gr * (2 * R) + (2 * r + 1))
                        act.activation(w[:, r:r + 1], gl[:, r:r + 1], ACT.Copy, scale=gate4[:, r:r + 1]).then_inc(c.act_done, 1)
                        act.wait_ge(c.act_done, gr * (2 * R) + (2 * r + 2))
                        if later:
                            act.wait_ge(c.product, gr * R + (r + 1 - R))
                        act.activation(diag[:, r, :], c.constant("ident"), ACT.Copy, scale=w[:, r:r + 1]).then_inc(c.act_out, 1)

                run(act, body)

            @block.tensor
            def _(pe):
                def body(gr):
                    for r in range(R):
                        pe.wait_ge(c.act_out, gr * R + (r + 1))
                        pe.wait_ge(c.gathered[R + r], gr * 16 + (16 + had))
                        first = isinstance(gr, int) and gr == 0 and r == 0
                        final = isinstance(gr, int) and gr == groups - 1 and r == R - 1
                        for half in range(2):
                            last = pe.matmul(c.banks[half][:], diag[:, r, :], vrows[:, r, half * 512:(half + 1) * 512],
                                             start=first, stop=final)
                        last.then_inc(c.product, 1)
                        pe.wait_ge(c.product, gr * R + (r + 1))
                        pe.sem_inc(c.v_free[r], 1)

                run(pe, body)

        with c.stage() as block:
            @block.vector
            def _(dve):
                for half in range(2):
                    dve.tensor_copy(acc[:, half * 512:(half + 1) * 512], c.banks[half][:]).then_inc(c.vec_out, 1)
                for half in range(2):
                    dve.wait_ge(c.product, half + 1)
                    for i in range(4):
                        k = 4 * half + i
                        out = c.x[:, k, NCTX + t * P:NCTX + (t + 1) * P]
                        dve.scalar_tensor_tensor(out, c.banks[2 + half][:, i * P:(i + 1) * P], c.mod[:, 5 * KT + k, 0:1], out,
                                                 ALU.mult, ALU.add)

            @block.tensor
            def _(pe):
                for half in range(2):
                    pe.wait_ge(c.vec_out, half + 1)
                    for i in range(4):
                        last = pe.transpose(c.banks[2 + half][:, i * P:(i + 1) * P],
                                            acc[:, (4 * half + i) * P:(4 * half + i + 1) * P], c.constant("ident"))
                    last.then_inc(c.product, 1)


def second_block(c, a, stop):
    lat = (NCTX, T)
    with c.stage() as block:
        @block.vector
        def _(dve):
            for k in range(KT):
                dve.tensor_copy(c.x[:, k, NCTX:T], c.h[:, k, NCTX:T])
    adaln(c, rows(a["ada_w_2"][0]), c.cond[:, 2:3, :].rearrange("p a k -> p k a"), c.vector("ada_b_2"), 1)
    norm(c, c.x, c.h, c.vector("norm_mix"), [(*lat, 0, 0, KT)])
    if stop == "norm2":
        return
    hgrn(c, a)
    s5(c, a)
    if stop == "mixers":
        return
    add_gated(c, rows(a["w_out_2"][0]), c.mg[:, :, 0:NLAT], [(*lat, 0)], 2 * KT)
    norm(c, c.x, c.h, c.vector("norm_ffn"), [(*lat, 0, 3 * KT, 4 * KT)])
    if stop == "normf":
        return
    peer(c, a)
    norm(c, c.x, c.h, c.vector("final_norm"), [(*lat, 0, 0, 0)], modulated=False)


STREAMED = ("w_ada", "w_in", "w_br_ml", "w_br_da", "w_br_fn", "w_out", "w_ffn_in", "w_ffn_out", "ada_w_2", "w_in_2", "w_out_2",
            "s5_glu_w_2", "peer_wq_2", "peer_u_2", "peer_v_2")
PACKED = ("vectors", "constants", "residual", "s5_b", "s5_c", "keys")
OUT = (P, KT, NLAT)


def build(nc, a, out, stop=None):
    ctx = ExitStack()
    with ctx:
        c = Core(nc, ctx)
        load_small(c, a)
        if first_block(c, a, stop) and stop != "first":
            second_block(c, a, stop)
        with nc.Block() as block:
            @block.sync
            def _(sp):
                sp.dma_start(out, c.h[:, :, NCTX:T]).then_inc(c.stored, 16)
                sp.wait_ge(c.stored, 16)


def columns(v):
    v = np.asarray(v)
    return v.reshape(-1, P).T


def pack_vectors(x):
    out = np.zeros((P, N_VEC), np.float32)

    def put(name, value):
        at, width = VEC[name]
        assert value.shape[1] == width, (name, value.shape, width)
        out[:value.shape[0], at:at + width] = value

    put("c", np.concatenate([columns(x["c_ctx"]), columns(x["c"]), columns(x["c_2"])], 1))
    for name, key in (("b_ada", "b_ada"), ("norm_g", "norm_g"), ("ml_head_g", "ml_head_g"), ("da_head_g", "da_head_g"),
                      ("final_g", "final_g"), ("ada_b_2", "ada_b_2"), ("norm_mix", "norm_mix_w_2"),
                      ("norm_ffn", "norm_ffn_w_2"), ("final_norm", "final_norm_w_2"), ("gnorm", "hg_gnorm_w_2"),
                      ("s5_d", "s5_d_2"), ("glu_b", "s5_glu_b_2"), ("bounds", "hg_lower_bounds_2")):
        put(name, columns(x[key]))
    put("lam", np.broadcast_to(x["da_lam"].reshape(1, -1), (P, 2 * 4 * DA_DH)))
    put("gate_b", np.ascontiguousarray(x["ml_gate_b"].reshape(DEPTH * 4, ML_HEADS).T))
    put("s5_are", columns(x["s5_a_re_2"]))
    put("s5_aim", columns(x["s5_a_im_2"]))
    put("s5_dt", columns(np.repeat(x["s5_log_dt_2"].reshape(-1), S5_P)))
    return out


def pack_constants():
    out = np.zeros((P, N_CST), np.float32)

    def put(name, value):
        at, width = CST[name]
        out[:, at:at + width] = np.broadcast_to(value, (P, width))

    at = np.arange(P)
    put("ident", np.eye(P))
    put("ones", np.ones((P, P)))
    put("upper", at[:, None] <= at[None, :])
    put("lower", at[:, None] >= at[None, :])
    turn = np.zeros((P, P))
    half = DA_DH // 2
    for p in range(P):
        first = p % DA_DH < half
        turn[p + half if first else p - half, p] = -1.0 if first else 1.0
    put("turn", turn)
    n_freq = DA_DH // 4
    inv = np.float32(10000.0) ** (-np.arange(n_freq, dtype=np.float32) / n_freq)
    r, col = np.repeat(np.arange(NLAT // 64, dtype=np.float32), 64), np.tile(np.arange(64, dtype=np.float32), NLAT // 64)
    angle = np.concatenate([r[:, None] * inv, col[:, None] * inv], -1)
    spread = angle[:, at % half].T
    put("cos", np.cos(spread))
    put("sin", np.sin(spread))
    k = np.arange(FN_C)
    phase = 2 * np.pi * (np.outer(k, k) % FN_C) / FN_C
    dft = np.concatenate([np.cos(phase), np.sin(phase), -np.sin(phase)], 1) / FN_C ** 0.5
    put("dft", dft.reshape(2, P, 3 * FN_C).transpose(1, 0, 2).reshape(P, -1))
    put("pick", np.eye(HG_SUB).reshape(1, -1))
    put("inner", (np.arange(HG_HEADS * NLAT) % HG_SUB != 0)[None, :])
    put("iota", np.arange(PEER_K)[None, :])
    return out


def pack_inputs(x):
    tokens = np.concatenate([x["ctx"][0], x["x"][0]], 0)
    m = {name: np.ascontiguousarray(x[name]) for name in STREAMED}
    m["vectors"] = pack_vectors(x)
    m["constants"] = pack_constants()
    m["residual"] = np.ascontiguousarray(tokens.T.reshape(KT, P, T).transpose(1, 0, 2))
    b = np.zeros((2, P, 4, P), np.float32)
    cc = np.zeros((2, P, S5_TILES, 2 * S5_H), np.float32)
    for part, (bn, cn) in enumerate((("s5_b_re_2", "s5_c_re_2"), ("s5_b_im_2", "s5_c_im_2"))):
        for g in range(S5_G):
            i, second = g // 2, g % 2
            row = 2 * S5_H * (i % 4) + S5_H * second
            b[part, row:row + S5_H, i // 4, S5_P * second:S5_P * (second + 1)] = x[bn][0, g].T
            cc[part, S5_P * second:S5_P * (second + 1), i, S5_H * second:S5_H * (second + 1)] = x[cn][0, g].T
    m["s5_b"], m["s5_c"] = b, cc
    m["keys"] = np.ascontiguousarray(np.stack([x["peer_keys1_2"][0].T, x["peer_keys2_2"][0].T], 1))
    return m


def kernel(**inputs):
    import concourse.bacc as _bacc
    from concourse.bass_utils import run_bass_kernel_spmd as _run

    arrays = pack_inputs({k: np.asarray(v) for k, v in inputs.items()})
    nc = _bacc.Bacc("TRN2", target_bir_lowering=False, num_devices=1)
    a = {n: nc.dram_tensor(n, v.shape, F32, kind="ExternalInput").ap() for n, v in arrays.items()}
    a["rows"] = nc.dram_tensor("rows", (ML_HEADS, 4, T), F32, kind="Internal").ap()
    out = nc.dram_tensor("out", OUT, F32, kind="ExternalOutput").ap()
    build(nc, a, out)
    r = _run(nc, [arrays], core_ids=[0])
    got = r.results[0]["out"]
    return np.ascontiguousarray(got.transpose(2, 1, 0)).reshape(1, NLAT, D)
```

```python
import math
from contextlib import ExitStack, contextmanager

import numpy as np
import concourse.bass as bass
from concourse import mybir

F32 = mybir.dt.float32
U32 = mybir.dt.uint32
I32 = mybir.dt.int32
ALU = mybir.AluOpType
ACT = mybir.ActivationFunctionType
AX = mybir.AxisListType

P = 128
D = 1024
KT = D // P
NCTX, NLAT = 256, 256
T = NCTX + NLAT
DEPTH = 2
EPS = 1e-6
CHUNK = 256
SLOTS = 4
BANKS = 8

ML_HEADS, ML_D = 4, 256
DA_HEADS, DA_DH = 8, 64
FN_GROUPS, FN_C = 4, 256
D_FF = -(-8 * D // (3 * 256)) * 256
COL_Q, COL_K, COL_V, COL_O, COL_GATE = 0, 1024, 2048, 3072, 4096
COL_DAQ = COL_GATE + 4 * ML_HEADS
COL_DAK, COL_DAV = COL_DAQ + 1024, COL_DAQ + 2048
COL_FN = COL_DAV + 1024
COL_MERGE = COL_FN + 1024
ML_COLUMNS, DA_COLUMNS, FN_COLUMNS = (COL_Q, COL_K, COL_O, COL_V), (COL_DAQ, COL_DAK, COL_DAV), (COL_FN,)

HG_HEADS, HG_W, HG_SUB = 4, 512, 16
HG_BLOCKS = NLAT // HG_SUB
S5_G, S5_H, S5_P = 32, 16, 64
S5_TILES = S5_G * S5_P // P
S5_STEPS = NLAT.bit_length() - 1
PEER_H, PEER_K, PEER_N = 8, 16, 128
PEER_SLOTS = PEER_H * PEER_K
PEER_RING = 4

VEC = {}


def _pack_columns():
    at = 0
    for name, width in (("c", 24), ("b_ada", 2 * 48), ("norm_g", 2 * 2 * KT), ("ml_head_g", 2 * KT), ("da_head_g", 2 * KT),
                        ("final_g", KT), ("ada_b_2", 48), ("norm_mix", KT), ("norm_ffn", KT), ("final_norm", KT),
                        ("gnorm", 1), ("s5_d", 4), ("glu_b", 4), ("bounds", 2 * 4), ("lam", 2 * 4 * DA_DH),
                        ("gate_b", 2 * 4), ("s5_are", S5_TILES), ("s5_aim", S5_TILES), ("s5_dt", S5_TILES)):
        VEC[name] = (at, width)
        at += width
    return at


N_VEC = _pack_columns()

CST = {}


def _constant_columns():
    at = 0
    for name, width in (("ident", P), ("ones", P), ("upper", P), ("lower", P), ("turn", P), ("cos", NLAT), ("sin", NLAT),
                        ("dft", 2 * 3 * FN_C), ("pick", HG_SUB * HG_SUB), ("inner", HG_HEADS * NLAT), ("iota", PEER_K)):
        CST[name] = (at, width)
        at += width
    return at


N_CST = _constant_columns()


class Chain:

    def __init__(self, engine, semaphore):
        self.engine, self.semaphore, self.n = engine, semaphore, 0

    def mark(self, instruction):
        instruction.then_inc(self.semaphore, 1)
        self.n += 1
        return self.n

    def wait(self, n=None):
        self.engine.wait_ge(self.semaphore, self.n if n is None else n)

    def __call__(self, instruction):
        self.mark(instruction)
        self.wait()


class Core:

    def __init__(self, nc, ctx):
        self.nc = nc

        def sb(name, shape, dtype=F32):
            return ctx.enter_context(nc.sbuf_tensor(name, shape, dtype))

        self.cst = sb("constants_sb", [P, N_CST])
        self.vec = sb("vectors_sb", [P, N_VEC])
        self.x = sb("stream", [P, KT, T])
        self.h = sb("normed", [P, KT, T])
        self.big = sb("branches", [P, 3 * KT, T])
        self.mg = sb("merged", [P, KT, T])
        self.ring = sb("weight_ring", [P, SLOTS, KT, CHUNK])
        self.mod = sb("modulation", [P, 48, 2])
        self.modA = sb("norm_scales", [P, 2, KT])
        self.cond = sb("condition", [P, 3, KT])
        self.lam = sb("lambda", [P, 16])
        self.s5_kept = sb("s5_kept", [P, 3, S5_TILES])
        self.hg_bounds = sb("hg_bounds", [P, 6, 4])
        self.work = sb("work", [P, 15360])
        self.banks = [ctx.enter_context(nc.psum_tensor(f"bank{i}", [P, 512], F32)) for i in range(BANKS)]

        def sem(name):
            return ctx.enter_context(nc.semaphore(name))

        self.loaded = [sem(f"loaded{i}") for i in range(SLOTS)]
        self.slot_used = sem("slot_used")
        self.product = sem("product")
        self.drained = sem("drained")
        self.vec_done = sem("vec_done")
        self.act_done = sem("act_done")
        self.pool_done = sem("pool_done")
        self.vec_out = sem("vec_out")
        self.act_out = sem("act_out")
        self.pe_out = sem("pe_out")
        self.side_loaded = sem("side_loaded")
        self.stored = sem("stored")
        self.maxima = sem("maxima")
        self.turned = sem("turned")
        self.u_free = [sem(f"u_free{i}") for i in range(PEER_RING)]
        self.v_free = [sem(f"v_free{i}") for i in range(PEER_RING)]
        self.sems = [*self.loaded, *self.u_free, *self.v_free, self.slot_used, self.product, self.drained, self.vec_done, self.act_done, self.pool_done,
                     self.vec_out, self.act_out, self.pe_out, self.side_loaded, self.stored, self.maxima,
                     self.turned]
        nums = sorted(s.num for s in self.sems)
        assert nums == list(range(nums[0], nums[0] + len(nums)))
        self.sem_range = range(nums[0], nums[-1] + 1)

        self.ahead = [sem(f"ahead{i}") for i in range(SLOTS)]
        self.ahead_n = [0] * SLOTS
        self.fetched = False
        self.gathered = [sem(f"gathered{i}") for i in range(PEER_RING)]

    def constant(self, name):
        at, width = CST[name]
        return self.cst[:, at:at + width]

    def vector(self, name, lo=0, hi=None):
        at, width = VEC[name]
        return self.vec[:, at + lo:at + (width if hi is None else hi)]

    @contextmanager
    def stage(self):
        with self.nc.Block(no_gpsimd_drain=True) as block:
            yield block
        self.nc.gpsimd.sem_clear(self.sem_range)
        self.nc.all_engine_barrier(sem_only=True)

    def carve(self, *shapes):
        at, out = 0, []
        for shape in shapes:
            n = math.prod(shape)
            view = self.work[:, at:at + n]
            if len(shape) == 2:
                view = view.rearrange("p (a b) -> p a b", b=shape[1])
            elif len(shape) == 3:
                view = view.rearrange("p (a b c) -> p a b c", b=shape[1], c=shape[2])
            out.append(view)
            at += n
        assert at <= 15360, at
        return out


def rows(w):
    return w.rearrange("(k p) n -> p k n", p=P)


def first_loads(weight, col0, n_chunks, splits=((0, KT),)):
    pieces = [(chunk, k0, nk) for chunk in range(n_chunks) for k0, nk in splits][:SLOTS]
    return [weight[:, k0:k0 + nk, col0 + chunk * CHUNK:col0 + (chunk + 1) * CHUNK] for chunk, k0, nk in pieces]


def fetch(c, engine, loads, wait_free=None):
    for s, source in enumerate(loads or ()):
        if wait_free:
            wait_free(s)
        engine.dma_start(c.ring[:, s, 0:source.shape[1], :], source).then_inc(c.ahead[s], 16)
        c.ahead_n[s] += 1
    c.fetched = bool(loads)


def project(c, weight, col0, n_chunks, rhs, n, evacuate, on="vector", splits=((0, KT),), following=None):
    pieces = len(splits)
    looped = pieces == 1 and n_chunks > 8
    whole = n_chunks // SLOTS

    def run(engine, body):
        if not looped:
            for s in range(n_chunks):
                body(0, s)
            return
        for s in range(SLOTS):
            body(0, s)
        with engine.Fori(0, whole - 1) as j:
            for s in range(SLOTS):
                body(j * SLOTS + SLOTS, s)
        for s in range(n_chunks % SLOTS):
            body(whole * SLOTS, s)

    def later(base, index, depth):
        return not isinstance(base, int) or base + index >= depth

    if not c.fetched:
        with c.stage() as block:
            @block.sync
            def _(sp):
                fetch(c, sp, first_loads(weight, col0, n_chunks, splits))
    had = list(c.ahead_n)

    with c.stage() as block:
        @block.sync
        def _(sp):
            def load(base, s):
                for piece, (k0, nk) in enumerate(splits):
                    i = s * pieces + piece
                    if not later(base, i, SLOTS):
                        continue
                    held, its_piece = (i - SLOTS) // pieces, (i - SLOTS) % pieces
                    if its_piece == pieces - 1:
                        sp.wait_ge(c.product, base * 2 + 2 * (held + 1))
                    else:
                        sp.wait_ge(c.slot_used, held * (pieces - 1) + its_piece + 1)
                    sp.dma_start(c.ring[:, i % SLOTS, 0:nk, :],
                                 weight[:, k0:k0 + nk, bass.ds(base * CHUNK + (s * CHUNK + col0), CHUNK)]
                                 ).then_inc(c.loaded[i % SLOTS], 16)

            run(sp, load)

            def wait_free(s):
                mine = [i for i in range(n_chunks * pieces) if i % SLOTS == s]
                if mine:
                    chunk, piece = mine[-1] // pieces, mine[-1] % pieces
                    if piece == pieces - 1:
                        sp.wait_ge(c.product, 2 * (chunk + 1))
                    else:
                        sp.wait_ge(c.slot_used, chunk * (pieces - 1) + piece + 1)

            fetch(c, sp, following, wait_free)

        @block.tensor
        def _(pe):
            def multiply(base, s):
                for piece, (k0, nk) in enumerate(splits):
                    i = s * pieces + piece
                    if later(base, i, SLOTS):
                        pe.wait_ge(c.loaded[i % SLOTS], base * (16 // SLOTS) + 16 * (i // SLOTS))
                    else:
                        pe.wait_ge(c.ahead[i], 16 * had[i])
                    for half in range(2):
                        tile = 2 * s + half
                        if piece == 0 and later(base * 2, tile, BANKS):
                            pe.wait_ge(c.drained, base * 2 + (tile + 1 - BANKS))
                        for k in range(nk):
                            last = pe.matmul(c.banks[tile % BANKS][:, 0:n], c.ring[:, i % SLOTS, k, half * P:(half + 1) * P],
                                             rhs[:, k0 + k, :], start=piece == 0 and k == 0,
                                             stop=piece == pieces - 1 and k == nk - 1)
                        if half == 1 and piece < pieces - 1:
                            last.then_inc(c.slot_used, 1)
                        if piece == pieces - 1:
                            last.then_inc(c.product, 1)

            run(pe, multiply)

        def drain(engine):
            def one(base, s):
                for half in range(2):
                    tile = 2 * s + half
                    engine.wait_ge(c.product, base * 2 + (tile + 1))
                    evacuate(engine, c.banks[tile % BANKS][:, 0:n], base * 2 + tile).then_inc(c.drained, 1)

            run(engine, one)

        by_name = {"vector": block.vector, "scalar": block.scalar}
        by_name[on](drain)


def moving(r, lo, hi):
    return r[:, :, lo:hi]


def load_small(c, a):
    with c.stage() as block:
        @block.sync
        def _(sp):
            sp.dma_start(c.vec[:], a["vectors"]).then_inc(c.side_loaded, 16)
            sp.dma_start(c.cst[:], a["constants"]).then_inc(c.loaded[0], 16)
            sp.dma_start(c.x[:], a["residual"]).then_inc(c.loaded[1], 16)

        @block.scalar
        def _(act):
            act.wait_ge(c.side_loaded, 16)
            act.activation(c.cond[:], c.vector("c").rearrange("p (a k) -> p a k", a=3), ACT.Silu)
            act.wait_ge(c.vec_out, 1)
            act.activation(c.lam[:, 8:12], c.lam[:, 0:4], ACT.Exp).then_inc(c.act_out, 1)

        @block.vector
        def _(dve):
            chain = Chain(dve, c.vec_done)
            dve.wait_ge(c.side_loaded, 16)
            lq = c.vector("lam").rearrange("p (l a d) -> p l a d", l=DEPTH, a=4)
            scratch = c.work[:, 0:DA_DH]
            for layer in range(DEPTH):
                for pair in range(2):
                    col = 2 * layer + pair
                    chain(dve.tensor_tensor(scratch, lq[:, layer, 2 * pair, :], lq[:, layer, 2 * pair + 1, :], ALU.mult))
                    chain(dve.reduce_sum(c.lam[:, col:col + 1], scratch, AX.X))
            dve.sem_inc(c.vec_out, 1)
            dve.wait_ge(c.act_out, 1)
            for layer in range(DEPTH):
                init = 0.8 - 0.6 * math.exp(-0.3 * layer)
                e = c.lam[:, 8 + 2 * layer:10 + 2 * layer]
                chain(dve.tensor_tensor(c.lam[:, 12 + layer:13 + layer], e[:, 0:1], e[:, 1:2], ALU.subtract))
                chain(dve.tensor_scalar(c.lam[:, 14 + layer:15 + layer], c.lam[:, 12 + layer:13 + layer], init, None, ALU.add))
            dve.wait_ge(c.loaded[0], 16)
            dve.wait_ge(c.loaded[1], 16)


def adaln(c, weight, conditions, bias, n, following, beside=None):
    rows_out, = c.carve((6 * D,))
    chunks = 6 * D // CHUNK
    if not c.fetched:
        with c.stage() as block:
            @block.sync
            def _(sp):
                fetch(c, sp, first_loads(weight, 0, chunks))
    had = list(c.ahead_n)
    rounds = chunks // SLOTS

    with c.stage() as block:
        @block.sync
        def _(sp):
            with sp.Fori(0, rounds - 1) as j:
                for s in range(SLOTS):
                    sp.wait_ge(c.product, j * SLOTS + (s + 1))
                    sp.dma_start(c.ring[:, s], weight[:, :, bass.ds(j * (SLOTS * CHUNK) + (SLOTS + s) * CHUNK, CHUNK)]
                                 ).then_inc(c.loaded[s], 16)
            fetch(c, sp, following, lambda s: sp.wait_ge(c.product, (rounds - 1) * SLOTS + s + 1))

        @block.tensor
        def _(pe):
            def multiply(base, s):
                first = isinstance(base, int)
                if first:
                    pe.wait_ge(c.ahead[s], 16 * had[s])
                else:
                    pe.wait_ge(c.loaded[s], base * (16 // SLOTS))
                    pe.wait_ge(c.drained, base + (s + 1 - SLOTS))
                for k in range(KT):
                    last = pe.matmul(c.banks[s][0:n, 0:CHUNK], conditions[:, k, :], c.ring[:, s, k, :], start=k == 0,
                                     stop=k == KT - 1)
                last.then_inc(c.product, 1)

            for s in range(SLOTS):
                multiply(0, s)
            with pe.Fori(0, rounds - 1) as j:
                for s in range(SLOTS):
                    multiply(j * SLOTS + SLOTS, s)
            pe.wait_ge(c.drained, chunks)
            for tile in range(6 * KT):
                last = pe.transpose(c.banks[SLOTS][:, tile * n:(tile + 1) * n], rows_out[0:n, tile * P:(tile + 1) * P],
                                    c.constant("ident")[0:n, 0:n])
            last.then_inc(c.turned, 1)

        @block.scalar
        def _(act):
            with act.Fori(0, rounds) as j:
                for s in range(SLOTS):
                    act.wait_ge(c.product, j * SLOTS + (s + 1))
                    act.activation(rows_out[0:n, bass.ds(j * (SLOTS * CHUNK) + s * CHUNK, CHUNK)],
                                   c.banks[s][0:n, 0:CHUNK], ACT.Copy).then_inc(c.drained, 1)

        @block.vector
        def _(dve):
            if beside:
                beside.vector(dve)
            dve.wait_ge(c.turned, 1)
            turned = c.banks[SLOTS][:, 0:6 * KT * n].rearrange("p (t a) -> p t a", a=n)
            for condition in range(n):
                dve.tensor_tensor(c.mod[:, :, condition], turned[:, :, condition], bias, ALU.add)


def norm(c, source, out, gain, parts, tiles=KT, spread=D, modulated=True):
    lo, hi = parts[0][0], parts[-1][1]
    n = hi - lo
    mean, rstd = c.carve((n,), (n,))
    with c.stage() as block:
        @block.scalar
        def _(act):
            for k in range(tiles):
                act.activation(out[:, k, lo:hi], source[:, k, lo:hi], ACT.Square).then_inc(c.act_out, 1)
            act.wait_ge(c.vec_out, 1)
            act.activation(rstd, mean, ACT.Sqrt).then_inc(c.act_done, 1)

        @block.tensor
        def _(pe):
            for k in range(tiles):
                pe.wait_ge(c.act_out, k + 1)
                last = pe.matmul(c.banks[0][:, 0:n], c.constant("ones"), out[:, k, lo:hi], start=k == 0, stop=k == tiles - 1)
            last.then_inc(c.product, 1)

        @block.vector
        def _(dve):
            chain = Chain(dve, c.vec_done)
            if modulated:
                for i, (_, _, which, _, scale) in enumerate(parts):
                    chain(dve.scalar_tensor_tensor(c.modA[:, i, :], c.mod[:, scale:scale + tiles, which], 1.0, gain,
                                                   ALU.add, ALU.mult))
            dve.wait_ge(c.product, 1)
            chain(dve.tensor_scalar(mean, c.banks[0][:, 0:n], 1.0 / spread, EPS, ALU.mult, ALU.add))
            dve.reciprocal(mean, mean).then_inc(c.vec_out, 1)
            dve.wait_ge(c.act_done, 1)
            scaled = [chain.mark(dve.tensor_tensor(out[:, k, lo:hi], source[:, k, lo:hi], rstd, ALU.mult))
                      for k in range(tiles)]
            for k in range(tiles):
                chain.wait(scaled[k])
                for i, (a, b, which, shift, _) in enumerate(parts):
                    if modulated:
                        dve.tensor_scalar(out[:, k, a:b], out[:, k, a:b], c.modA[:, i, k:k + 1],
                                          c.mod[:, shift + k, which:which + 1], ALU.mult, ALU.add)
                    else:
                        dve.tensor_scalar(out[:, k, a:b], out[:, k, a:b], gain[:, k:k + 1], None, ALU.mult)


def head_loads(w_in, columns, turn):
    return [w_in[:, :, bass.ds(turn * CHUNK + col, CHUNK)] for col in columns]


def over_turns(c, turns, columns, w_in, body, following):
    if not c.fetched:
        with c.stage() as block:
            @block.sync
            def _(sp):
                fetch(c, sp, head_loads(w_in, columns, 0))
    had = list(c.ahead_n)

    def wait_loaded(turn):
        return lambda engine, s: engine.wait_ge(c.ahead[s], turn * 16 + 16 * had[s])

    with c.nc.Fori(0, turns - 1) as turn:
        body(turn, wait_loaded(turn),
             lambda sp, wait_free=None: fetch(c, sp, head_loads(w_in, [col + CHUNK for col in columns], turn), wait_free))
    for s in range(len(columns)):
        c.ahead_n[s] = had[s] + turns - 1
    body(turns - 1, wait_loaded(turns - 1), lambda sp, wait_free=None: fetch(c, sp, following, wait_free))


def mlstm(c, a, layer, w_in, full, following):
    lo = 0 if full else NCTX
    n = T - lo
    gcol, gh, headg, gates, logf, e, b, g, m, ones, out_rows, wg = c.carve(
        (2 * 4, 4), (2 * 4,), (2,), (4, T), (2, T), (2, T), (2, T), (2, T), (2, T), (T,), (4, T), (KT, 16))
    H = ML_HEADS
    with c.stage() as block:
        @block.sync
        def _(sp):
            sp.dma_start(wg, w_in[:, :, COL_GATE:COL_GATE + 16]).then_inc(c.side_loaded, 16)
            sp.wait_ge(c.vec_out, 3)
            sp.wait_ge(c.act_out, 5)
            sp.dma_start(a["rows"], out_rows[0:H]).then_inc(c.stored, 16)
            sp.wait_ge(c.stored, 16)

        @block.tensor
        def _(pe):
            pe.wait_ge(c.side_loaded, 16)
            for j in range(4):
                for k in range(KT):
                    last = pe.matmul(c.banks[j][0:H, :], wg[:, k, H * j:H * j + H], c.h[:, k, :], start=k == 0, stop=k == KT - 1)
                last.then_inc(c.product, 1)
            pe.wait_ge(c.vec_out, 1)
            for d in range(2):
                for j in range(4):
                    last = pe.matmul(c.banks[4][:, (4 * d + j) * 4:(4 * d + j + 1) * 4], g[0:H, d, j * P:(j + 1) * P],
                                     c.constant("ident")[0:H, 0:H], start=True, stop=True)
            last.then_inc(c.product, 1)

        @block.scalar
        def _(act):
            for j in range(4):
                act.wait_ge(c.product, j + 1)
                act.activation(gates[0:H, j, :], c.banks[j][0:H, :], ACT.Identity,
                               bias=c.vector("gate_b", 4 * layer + j, 4 * layer + j + 1)[0:H]).then_inc(c.act_out, 1)
            act.wait_ge(c.vec_done, 4)
            act.activation(e[0:H], e[0:H], ACT.Exp, scale=-1.0).then_inc(c.act_done, 1)
            act.wait_ge(c.act_done, 1)
            act.activation(e[0:H], e[0:H], ACT.Ln, bias=1.0).then_inc(c.act_done, 1)
            act.wait_ge(c.vec_out, 2)
            act.activation(out_rows[0:H, 2:4], m[0:H], ACT.Exp, scale=-1.0).then_inc(c.act_out, 1)

        @block.vector
        def _(dve):
            chain = Chain(dve, c.vec_done)
            dve.wait_ge(c.act_out, 4)
            for d in range(2):
                f = gates[0:H, 2 * d + 1, :]
                chain(dve.tensor_scalar(e[0:H, d], f, -1.0, None, ALU.mult))
                chain(dve.tensor_tensor(e[0:H, d], e[0:H, d], f, ALU.max))
            chain(dve.memset(ones[0:H], 1.0))
            dve.wait_ge(c.act_done, 2)
            for d in range(2):
                chain(dve.scalar_tensor_tensor(logf[0:H, d], gates[0:H, 2 * d + 1, :], 0.0, e[0:H, d], ALU.min, ALU.subtract))
            chain(dve.tensor_tensor_scan(b[0:H, 0], ones[0:H], logf[0:H, 0], 0.0, ALU.mult, ALU.add))
            chain(dve.tensor_tensor_scan(b[0:H, 1, NCTX - 1::-1], ones[0:H, 0:NCTX], logf[0:H, 1, NCTX - 1::-1], 0.0,
                                         ALU.mult, ALU.add))
            chain(dve.tensor_tensor_scan(b[0:H, 1, T - 1:NCTX - 1:-1], ones[0:H, 0:NLAT], logf[0:H, 1, T - 1:NCTX - 1:-1],
                                         b[0:H, 1, 0:1], ALU.mult, ALU.add))
            for d in range(2):
                chain(dve.tensor_tensor(g[0:H, d], gates[0:H, 2 * d, :], b[0:H, d], ALU.subtract))
            dve.sem_inc(c.vec_out, 1)
            chain(dve.tensor_tensor_scan(m[0:H, 0], g[0:H, 0], g[0:H, 0], 0.0, ALU.max, ALU.max))
            chain(dve.tensor_tensor_scan(m[0:H, 1, NCTX - 1::-1], g[0:H, 1, NCTX - 1::-1], g[0:H, 1, NCTX - 1::-1], 0.0,
                                         ALU.max, ALU.max))
            chain(dve.tensor_tensor_scan(m[0:H, 1, T - 1:NCTX - 1:-1], g[0:H, 1, T - 1:NCTX - 1:-1],
                                         g[0:H, 1, T - 1:NCTX - 1:-1], m[0:H, 1, 0:1], ALU.max, ALU.max))
            chain(dve.tensor_scalar(out_rows[0:H, 0:2], m[0:H], -1.0, None, ALU.mult))
            chain(dve.tensor_tensor(m[0:H], m[0:H], b[0:H], ALU.add))
            dve.sem_inc(c.vec_out, 1)
            dve.wait_ge(c.product, 5)
            dve.tensor_copy(gcol, c.banks[4][:, 0:32].rearrange("p (x h) -> p x h", h=4)).then_inc(c.vec_out, 1)
            dve.wait_ge(c.act_out, 5)

    _, _, _, q, k, v, o, bc, A, E, den, hs, sq = c.carve(
        (2 * 4, 4), (2 * 4,), (2,), (2, T), (2, T), (4, ML_D), (2, T), (4, T), (4, T), (2, T), (2, T), (2, T), (2, T))
    runs = [[(j, max(j * P, lo), T) for j in range(4)],
            [(1, lo, T), (0, 0, P), (0, NCTX, T), (3, NCTX, T), (2, NCTX, NCTX + P)]]
    runs = [[r for r in rs if r[1] < r[2] and (full or r[1] >= NCTX)] for rs in runs]
    sources = [(j, max(lo, 0 if j < 2 else NCTX), T) for j in range(4)]

    def one_head(head, wait_loaded, fetch_next):
        with c.stage() as block:
            @block.tensor
            def _(pe):
                for s, (first, width) in enumerate(((lo, n), (0, T), (lo, n))):
                    wait_loaded(pe, s)
                    for half in range(2):
                        for kk in range(KT):
                            last = pe.matmul(c.banks[2 * s + half][:, 0:width], c.ring[:, s, kk, half * P:(half + 1) * P],
                                             c.h[:, kk, first:T], start=kk == 0, stop=kk == KT - 1)
                        last.then_inc(c.product, 1)
                wait_loaded(pe, 3)
                for j in range(4):
                    for kk in range(KT):
                        last = pe.matmul(c.banks[6 + j // 2][:, (j % 2) * ML_D:(j % 2 + 1) * ML_D],
                                         c.h[:, kk, j * P:(j + 1) * P], c.ring[:, 3, kk, :], start=kk == 0, stop=kk == KT - 1)
                    last.then_inc(c.product, 1)

            @block.vector
            def _(dve):
                for half in range(2):
                    dve.wait_ge(c.product, half + 1)
                    dve.tensor_copy(q[:, half, lo:T], c.banks[half][:, 0:n])
                for half in range(2):
                    dve.wait_ge(c.product, half + 3)
                    dve.tensor_scalar(k[:, half, :], c.banks[2 + half][:], ML_D ** -0.5, None, ALU.mult)
                dve.tensor_copy(gh, gcol[:, :, bass.ds(head, 1)].rearrange("p x h -> p (x h)"))
                dve.tensor_copy(headg, c.vector("ml_head_g")[:, bass.ds(head * 2 + layer * KT, 2)])
                for j in range(0, 4, 2):
                    dve.wait_ge(c.product, 8 + j)
                    dve.tensor_copy(v[:, j:j + 2, :], c.banks[6 + j // 2][:].rearrange("p (j e) -> p j e", j=2))

            @block.scalar
            def _(act):
                act.dma_start(bc, a["rows"][bass.ds(head, 1)].rearrange("h a t -> (h a) t").partition_broadcast(P)
                              ).then_inc(c.side_loaded, 16)
                for half in range(2):
                    act.wait_ge(c.product, half + 5)
                    act.activation(o[:, half, lo:T], c.banks[4 + half][:, 0:n], ACT.Sigmoid)
                act.wait_ge(c.side_loaded, 16)

        for d in range(2):
            with c.stage() as block:
                if d == 0:
                    @block.sync
                    def _(sp):
                        fetch_next(sp)

                @block.tensor
                def _(pe):
                    for j, a0, a1 in sources:
                        for half in range(2):
                            last = pe.matmul(c.banks[j][:, a0 - lo:a1 - lo], k[:, half, j * P:(j + 1) * P], q[:, half, a0:a1],
                                             start=half == 0, stop=half == 1)
                        last.then_inc(c.product, 1)
                    pe.wait_ge(c.vec_out, 4)
                    for bank, lhs in ((4, 0), (5, 1), (6, None)):
                        for i, (j, a0, a1) in enumerate(runs[d]):
                            weights = c.constant("ones") if lhs is None else v[:, j, lhs * P:(lhs + 1) * P]
                            last = pe.matmul(c.banks[bank][:, a0 - lo:a1 - lo], weights, A[:, j, a0:a1], start=i == 0,
                                             stop=i == len(runs[d]) - 1)
                    last.then_inc(c.pe_out, 1)

                @block.scalar
                def _(act):
                    for i, (j, a0, a1) in enumerate(sources):
                        act.wait_ge(c.vec_done, i + 1)
                        act.activation(A[:, j, a0:a1], A[:, j, a0:a1], ACT.Exp).then_inc(c.act_out, 1)
                    act.wait_ge(c.pe_out, 1)
                    act.activation(den[:, d, lo:T], c.banks[6][:, 0:n], ACT.Abs).then_inc(c.act_out, 1)

                @block.vector
                def _(dve):
                    chain = Chain(dve, c.vec_done)
                    mask = c.constant("upper" if d == 0 else "lower")
                    for j, a0, a1 in sources:
                        chain.mark(dve.tensor_scalar(A[:, j, a0:a1], bc[:, d, a0:a1], gh[:, 4 * d + j:4 * d + j + 1], 0.0,
                                                     ALU.add, ALU.min))
                    for i, (j, a0, a1) in enumerate(sources):
                        dve.wait_ge(c.act_out, i + 1)
                        dve.wait_ge(c.product, i + 1)
                        chain(dve.tensor_tensor(A[:, j, a0:a1], A[:, j, a0:a1], c.banks[j][:, a0 - lo:a1 - lo], ALU.mult))
                        diagonal = A[:, j, j * P:(j + 1) * P]
                        if j * P >= lo:
                            chain(dve.tensor_tensor(diagonal, diagonal, mask, ALU.mult))
                        dve.sem_inc(c.vec_out, 1)
                    dve.wait_ge(c.act_out, 5)
                    chain(dve.tensor_tensor(den[:, d, lo:T], den[:, d, lo:T], bc[:, 2 + d, lo:T], ALU.max))
                    chain(dve.reciprocal(den[:, d, lo:T], den[:, d, lo:T]))
                    for half in range(2):
                        out = hs if d == 0 else E
                        chain(dve.tensor_tensor(out[:, half, lo:T], c.banks[4 + half][:, 0:n], den[:, d, lo:T], ALU.mult))
                        if d == 1:
                            chain(dve.tensor_tensor(hs[:, half, lo:T], hs[:, half, lo:T], E[:, half, lo:T], ALU.add))

        with c.stage() as block:
            @block.scalar
            def _(act):
                for half in range(2):
                    act.activation(sq[:, half, lo:T], hs[:, half, lo:T], ACT.Square).then_inc(c.act_out, 1)
                act.wait_ge(c.vec_out, 1)
                act.activation(E[:, 0, lo:T], den[:, 0, lo:T], ACT.Sqrt).then_inc(c.act_out, 1)

            @block.tensor
            def _(pe):
                for half in range(2):
                    pe.wait_ge(c.act_out, half + 1)
                    last = pe.matmul(c.banks[0][:, 0:n], c.constant("ones"), sq[:, half, lo:T], start=half == 0, stop=half == 1)
                last.then_inc(c.product, 1)

            @block.vector
            def _(dve):
                chain = Chain(dve, c.vec_done)
                dve.wait_ge(c.product, 1)
                chain(dve.tensor_scalar(den[:, 0, lo:T], c.banks[0][:, 0:n], 1.0 / ML_D, EPS, ALU.mult, ALU.add))
                dve.reciprocal(den[:, 0, lo:T], den[:, 0, lo:T]).then_inc(c.vec_out, 1)
                dve.wait_ge(c.act_out, 3)
                flat = c.big[:].rearrange("p k t -> p (k t)")
                for half in range(2):
                    chain(dve.scalar_tensor_tensor(sq[:, half, lo:T], hs[:, half, lo:T], headg[:, half:half + 1],
                                                   E[:, 0, lo:T], ALU.mult, ALU.mult))
                    dve.tensor_tensor(flat[:, bass.ds(head * (2 * T) + (half * T + lo), n)], sq[:, half, lo:T],
                                      o[:, half, lo:T], ALU.mult)

    over_turns(c, ML_HEADS, ML_COLUMNS, w_in, one_head, following)


def diff_attention(c, a, layer, w_in, full, following):
    lo = 0 if full else NCTX
    n = T - lo
    q, k, v, rot, pr, aw, aT, stats, headg, osb, sq, rs = c.carve(
        (2, T), (2, T), (4, 2 * P), (2, NLAT), (4, T), (2, T), (4, T), (4, 8), (2,), (T,), (T,), (2, T))
    keep = 1.0 - (0.8 - 0.6 * math.exp(-0.3 * layer))

    def one_pair(pair, wait_loaded, fetch_next):
        with c.stage() as block:
            @block.tensor
            def _(pe):
                for s, first in enumerate((lo, 0)):
                    wait_loaded(pe, s)
                    for half in range(2):
                        for kk in range(KT):
                            last = pe.matmul(c.banks[2 * s + half][:, first:T], c.ring[:, s, kk, half * P:(half + 1) * P],
                                             c.h[:, kk, first:T], start=kk == 0, stop=kk == KT - 1)
                        last.then_inc(c.product, 1)
                wait_loaded(pe, 2)
                for j in range(4):
                    for kk in range(KT):
                        last = pe.matmul(c.banks[4 + j // 2][:, (j % 2) * 2 * P:(j % 2 + 1) * 2 * P],
                                         c.h[:, kk, j * P:(j + 1) * P], c.ring[:, 2, kk, :], start=kk == 0, stop=kk == KT - 1)
                    last.then_inc(c.product, 1)
                for i, x in enumerate((q, k)):
                    pe.wait_ge(c.vec_done, 2 * i + 2)
                    for half in range(2):
                        pe.matmul(c.banks[6 + i][:, half * NLAT:(half + 1) * NLAT], c.constant("turn"), x[:, half, NCTX:T],
                                  start=True, stop=True).then_inc(c.pe_out, 1)

            @block.vector
            def _(dve):
                chain = Chain(dve, c.vec_done)
                for i, (x, first) in enumerate(((q, lo), (k, 0))):
                    for half in range(2):
                        dve.wait_ge(c.product, 2 * i + half + 1)
                        chain.mark(dve.tensor_copy(x[:, half, first:T], c.banks[2 * i + half][:, first:T]))
                for j in range(0, 4, 2):
                    dve.wait_ge(c.product, 6 + j)
                    chain.mark(dve.tensor_copy(v[:, j:j + 2, :], c.banks[4 + j // 2][:].rearrange("p (j e) -> p j e", j=2)))
                for i, x in enumerate((q, k)):
                    for half in range(2):
                        dve.wait_ge(c.pe_out, 2 * i + 2)
                        chain(dve.tensor_tensor(rot[:, half], c.banks[6 + i][:, half * NLAT:(half + 1) * NLAT],
                                                c.constant("sin"), ALU.mult))
                        chain(dve.tensor_tensor(x[:, half, NCTX:T], x[:, half, NCTX:T], c.constant("cos"), ALU.mult))
                        chain(dve.tensor_tensor(x[:, half, NCTX:T], x[:, half, NCTX:T], rot[:, half], ALU.add))
                dve.tensor_scalar(headg, c.vector("da_head_g")[:, bass.ds(pair * 2 + layer * KT, 2)], keep, None, ALU.mult)

        tiles = [t for t in range(4) if t * P >= lo]
        for half in range(2):
            with c.stage() as block:
                if half == 0:
                    @block.sync
                    def _(sp):
                        fetch_next(sp)

                def keys(t):
                    return NCTX if t < 2 else T

                def turn(pe, i):
                    t = tiles[i]
                    pe.wait_ge(c.vec_out, i + 1)
                    if i >= 2:
                        pe.wait_ge(c.drained, i - 1)
                    for j in range(keys(t) // P):
                        last = pe.transpose(c.banks[4 + i % 2][:, j * P:(j + 1) * P], aw[:, i % 2, j * P:(j + 1) * P],
                                            c.constant("ident"))
                    last.then_inc(c.turned, 1)

                @block.tensor
                def _(pe):
                    for i, t in enumerate(tiles):
                        for m in range(2):
                            u = 2 * i + m
                            if u >= 4:
                                pe.wait_ge(c.act_out, u - 3)
                            pe.matmul(c.banks[u % 4][:, 0:keys(t)], q[m * 64:(m + 1) * 64, half, t * P:(t + 1) * P],
                                      k[m * 64:(m + 1) * 64, half, 0:keys(t)], start=True, stop=True).then_inc(c.product, 1)
                        if i >= 1:
                            turn(pe, i - 1)
                    turn(pe, len(tiles) - 1)
                    pe.wait_ge(c.drained, len(tiles))
                    groups = ([(0, NCTX, 2)] if full else []) + [(NCTX, T, 4)]
                    for a0, a1, sources in groups:
                        for j in range(sources):
                            last = pe.matmul(c.banks[6][:, a0 - lo:a1 - lo], v[:, j, half * P:(half + 1) * P], aT[:, j, a0:a1],
                                             start=j == 0, stop=j == sources - 1)
                    last.then_inc(c.pe_out, 1)
                    pe.wait_ge(c.act_done, 1)
                    pe.matmul(c.banks[7][:, 0:n], c.constant("ones"), sq[:, lo:T], start=True, stop=True).then_inc(c.pe_out, 1)

                @block.scalar
                def _(act):
                    for i, t in enumerate(tiles):
                        for m in range(2):
                            u = 2 * i + m
                            act.wait_ge(c.maxima, u + 1)
                            if i >= 2:
                                act.wait_ge(c.vec_out, i - 1)
                            act.activation(pr[:, u % 4, 0:keys(t)], c.banks[u % 4][:, 0:keys(t)], ACT.Exp,
                                           bias=stats[:, i, m:m + 1], scale=DA_DH ** -0.5,
                                           accum_out=stats[:, i, 2 + m:3 + m]).then_inc(c.act_out, 1)
                    act.wait_ge(c.pe_out, 1)
                    act.activation(sq[:, lo:T], c.banks[6][:, 0:n], ACT.Square).then_inc(c.act_done, 1)
                    act.wait_ge(c.vec_out, len(tiles) + 1)
                    act.activation(rs[:, 1, lo:T], rs[:, 0, lo:T], ACT.Sqrt).then_inc(c.act_done, 1)

                @block.vector
                def _(dve):
                    chain = Chain(dve, c.vec_done)

                    def maxima(i):
                        for m in range(2):
                            dve.wait_ge(c.product, 2 * i + m + 1)
                            chain(dve.reduce_max(stats[:, i, 6 + m:7 + m], c.banks[(2 * i + m) % 4][:, 0:keys(tiles[i])], AX.X))
                            dve.tensor_scalar(stats[:, i, m:m + 1], stats[:, i, 6 + m:7 + m], -(DA_DH ** -0.5), None,
                                              ALU.mult).then_inc(c.maxima, 1)

                    def combine(i):
                        w = keys(tiles[i])
                        dve.wait_ge(c.act_out, 2 * i + 2)
                        chain(dve.reciprocal(stats[:, i, 4:6], stats[:, i, 2:4]))
                        chain(dve.tensor_tensor(stats[:, i, 5:6], stats[:, i, 5:6], c.lam[:, 14 + layer:15 + layer], ALU.mult))
                        p0, p1 = (pr[:, (2 * i + m) % 4, 0:w] for m in range(2))
                        chain(dve.tensor_scalar(p1, p1, stats[:, i, 5:6], None, ALU.mult))
                        if i >= 2:
                            dve.wait_ge(c.turned, i - 1)
                        dve.scalar_tensor_tensor(aw[:, i % 2, 0:w], p0, stats[:, i, 4:5], p1, ALU.mult,
                                                 ALU.subtract).then_inc(c.vec_out, 1)

                    def spread(i):
                        t, w = tiles[i], keys(tiles[i])
                        dve.wait_ge(c.turned, i + 1)
                        dve.tensor_copy(aT[:, 0:w // P, t * P:(t + 1) * P],
                                        c.banks[4 + i % 2][:, 0:w].rearrange("p (j t) -> p j t", t=P)).then_inc(c.drained, 1)

                    maxima(0)
                    for i in range(len(tiles)):
                        if i + 1 < len(tiles):
                            maxima(i + 1)
                        combine(i)
                        if i >= 1:
                            spread(i - 1)
                    spread(len(tiles) - 1)
                    dve.wait_ge(c.pe_out, 2)
                    chain(dve.tensor_scalar(rs[:, 0, lo:T], c.banks[7][:, 0:n], 1.0 / P, EPS, ALU.mult, ALU.add))
                    dve.reciprocal(rs[:, 0, lo:T], rs[:, 0, lo:T]).then_inc(c.vec_out, 1)
                    dve.wait_ge(c.act_done, 2)
                    flat = c.big[:].rearrange("p k t -> p (k t)")
                    dve.scalar_tensor_tensor(flat[:, bass.ds(pair * (2 * T) + ((KT + half) * T + lo), n)],
                                             c.banks[6][:, 0:n], headg[:, half:half + 1], rs[:, 1, lo:T], ALU.mult, ALU.mult)

    over_turns(c, DA_HEADS // 2, DA_COLUMNS, w_in, one_pair, following)


def fourier(c, w_in, full, following):
    lo = 0 if full else NCTX
    z, ab = c.carve((2, T), (4, 2 * FN_C))
    dft = c.constant("dft").rearrange("p (k n) -> p k n", k=2)
    tiles = [t for t in range(4) if t * P >= lo]

    def one_group(group, wait_loaded, fetch_next):
        with c.stage() as block:
            @block.sync
            def _(sp):
                fetch_next(sp, lambda s: sp.wait_ge(c.product, 2) if s == 0 else None)

            @block.tensor
            def _(pe):
                wait_loaded(pe, 0)
                for half in range(2):
                    for k in range(KT):
                        last = pe.matmul(c.banks[half][:, lo:T], c.ring[:, 0, k, half * P:(half + 1) * P], c.h[:, k, lo:T],
                                         start=k == 0, stop=k == KT - 1)
                    last.then_inc(c.product, 1)
                pe.wait_ge(c.vec_done, 2)
                for i, t in enumerate(tiles):
                    for k in range(2):
                        last = pe.matmul(c.banks[2 + i][:], z[:, k, t * P:(t + 1) * P], dft[:, k, 0:2 * FN_C], start=k == 0,
                                         stop=k == 1)
                    last.then_inc(c.product, 1)
                pe.wait_ge(c.vec_done, 2 + len(tiles))
                for half in range(2):
                    for stream in range(lo // NCTX, 2):
                        for i in range(4):
                            j, part = i // 2, i % 2
                            last = pe.matmul(c.banks[6 + half][:, stream * NCTX:(stream + 1) * NCTX],
                                             ab[:, 2 * stream + j, part * FN_C + half * P:part * FN_C + (half + 1) * P],
                                             dft[:, j, part * 2 * FN_C:part * 2 * FN_C + FN_C], start=i == 0, stop=i == 3)
                    last.then_inc(c.product, 1)

            @block.vector
            def _(dve):
                chain = Chain(dve, c.vec_done)
                for half in range(2):
                    dve.wait_ge(c.product, half + 1)
                    chain.mark(dve.tensor_copy(z[:, half, lo:T], c.banks[half][:, lo:T]))
                for i, t in enumerate(tiles):
                    dve.wait_ge(c.product, 3 + i)
                    chain.mark(dve.tensor_copy(ab[:, t, :], c.banks[2 + i][:]))
                flat = c.big[:].rearrange("p k t -> p (k t)")
                for half in range(2):
                    dve.wait_ge(c.product, 3 + len(tiles) + half)
                    dve.tensor_copy(flat[:, bass.ds(group * (2 * T) + ((2 * KT + half) * T + lo), T - lo)],
                                    c.banks[6 + half][:, lo:T])

    over_turns(c, FN_GROUPS, FN_COLUMNS, w_in, one_group, following)


def merge(c, a, layer, w_in, full, following):
    lo = 0 if full else NCTX
    n = T - lo
    gate, = c.carve((KT, T))
    names = ("w_br_ml", "w_br_da", "w_br_fn")
    for i, name in enumerate(names):
        branch = rows(a[name][layer])
        project(c, w_in, COL_MERGE + i * D, D // CHUNK, moving(c.h, lo, T), n,
                lambda e, bank, tile: e.activation(gate[:, tile, lo:T], bank, ACT.Sigmoid), on="scalar",
                following=first_loads(branch, 0, D // CHUNK))

        def gated(e, bank, tile):
            out = c.mg[:, tile, lo:T]
            if i == 0:
                return e.tensor_tensor(out, bank, gate[:, tile, lo:T], ALU.mult)
            return e.tensor_tensor(gate[:, tile, lo:T], bank, gate[:, tile, lo:T], ALU.mult)

        after = first_loads(w_in, COL_MERGE + (i + 1) * D, D // CHUNK) if i + 1 < len(names) else following
        project(c, branch, 0, D // CHUNK, moving(c.big[:, i * KT:(i + 1) * KT, :], lo, T), n, gated, following=after)
        if i:
            with c.stage() as block:
                @block.vector
                def _(dve):
                    for k in range(KT):
                        dve.tensor_tensor(c.mg[:, k, lo:T], c.mg[:, k, lo:T], gate[:, k, lo:T], ALU.add)


def add_gated(c, weight, rhs, parts, gate_tile, splits=((0, KT),), following=None):
    lo = parts[0][0]

    def evacuate(e, bank, tile):
        for first, last, which in parts:
            out = c.x[:, tile, first:last]
            ins = e.scalar_tensor_tensor(out, bank[:, first - lo:last - lo], c.mod[:, gate_tile + tile, which:which + 1], out,
                                         ALU.mult, ALU.add)
        return ins

    project(c, weight, 0, D // CHUNK, rhs, T - lo, evacuate, splits=splits, following=following)


def feed_forward(c, a, layer, parts, following):
    lo = parts[0][0]
    n = T - lo
    flat = c.big[:].rearrange("p k t -> p (k t)")
    w, w_out = rows(a["w_ffn_in"][layer]), rows(a["w_ffn_out"][layer])
    ks = D_FF // P
    splits = tuple((k0, min(KT, ks - k0)) for k0 in range(0, ks, KT))
    project(c, w, 0, D_FF // CHUNK, moving(c.h, lo, T), n,
            lambda e, bank, tile: e.activation(flat[:, bass.ds(tile * T + lo, n)], bank, ACT.Silu), on="scalar",
            following=first_loads(w, D_FF, D_FF // CHUNK))
    project(c, w, D_FF, D_FF // CHUNK, moving(c.h, lo, T), n,
            lambda e, bank, tile: e.tensor_tensor(flat[:, bass.ds(tile * T + lo, n)], bank,
                                                  flat[:, bass.ds(tile * T + lo, n)], ALU.mult),
            following=first_loads(w_out, 0, D // CHUNK, splits))
    add_gated(c, w_out, moving(c.big[:, 0:ks, :], lo, T), parts, 5 * KT, splits=splits, following=following)


def first_block(c, a, stop):
    for layer in range(DEPTH):
        full = layer < DEPTH - 1
        streams = [(0, NCTX, 0), (NCTX, T, 1)]
        kept = streams if full else streams[1:]
        w_in = rows(a["w_in"][layer])
        conditions = c.cond[:, 0:2, :].rearrange("p a k -> p k a")
        adaln(c, rows(a["w_ada"][layer]), conditions, c.vector("b_ada", 48 * layer, 48 * (layer + 1)), 2,
              head_loads(w_in, ML_COLUMNS, 0))
        gains = [c.vector("norm_g", (2 * layer + i) * KT, (2 * layer + i + 1) * KT) for i in range(2)]
        norm(c, c.x, c.h, gains[0], [(f, l, w, 0, KT) for f, l, w in streams])
        if stop == f"norm{layer}":
            return False
        mlstm(c, a, layer, w_in, full, head_loads(w_in, DA_COLUMNS, 0))
        diff_attention(c, a, layer, w_in, full, head_loads(w_in, FN_COLUMNS, 0))
        fourier(c, w_in, full, first_loads(w_in, COL_MERGE, D // CHUNK))
        if stop == f"branches{layer}":
            return False
        w_out = rows(a["w_out"][layer])
        merge(c, a, layer, w_in, full, first_loads(w_out, 0, D // CHUNK))
        add_gated(c, w_out, moving(c.mg, kept[0][0], T), kept, 2 * KT,
                  following=first_loads(rows(a["w_ffn_in"][layer]), 0, D_FF // CHUNK))
        if stop == f"mix{layer}":
            return False
        norm(c, c.x, c.h, gains[1], [(f, l, w, 3 * KT, 4 * KT) for f, l, w in kept])
        next_ada = rows(a["w_ada"][layer + 1]) if full else rows(a["ada_w_2"][0])
        feed_forward(c, a, layer, kept, first_loads(next_ada, 0, 6 * D // CHUNK))
        if stop == f"ffn{layer}":
            return False
    norm(c, c.x, c.h, c.vector("final_g"), [(NCTX, T, 1, 0, 0)], modulated=False)
    return True



def hgrn(c, a):
    w_in = rows(a["w_in_2"][0])
    hs = moving(c.h, NCTX, T)
    H, B, L = HG_HEADS, HG_BLOCKS, HG_SUB
    N = H * NLAT
    big = c.big[:].rearrange("p k t -> p (k t)")
    q, f, g, u, kk, lf, bl, e1, qe, kend, sq, rs = (big[:, i * N:(i + 1) * N] for i in range(12))
    vt, v16, at, pairs, state = c.carve((2, HG_W), (B, HG_W), (N,), (2, N), (2, HG_W))
    lb = c.hg_bounds[:]
    kt = c.ring[:].rearrange("p s k n -> p (s k n)")
    per_tile = NLAT
    parts = ((q, 0, ACT.Silu), (g, 3 * HG_W, ACT.Silu), (f, HG_W, ACT.Sigmoid), (u, 4 * HG_W, ACT.Copy))
    for i, (buffer, col, func) in enumerate(parts):
        project(c, w_in, col, HG_W // CHUNK, hs, NLAT,
                lambda e, bank, tile: e.activation(buffer[:, tile * per_tile:(tile + 1) * per_tile], bank, func), on="scalar",
                following=first_loads(w_in, parts[i + 1][1] if i + 1 < len(parts) else 2 * HG_W, HG_W // CHUNK))

    c.fetched = False
    with c.stage() as block:
        @block.sync
        def _(sp):
            sp.wait_ge(c.vec_out, 2)
            for b in range(B):
                sp.dma_start(v16[0:L, b, :], vt[(b % 8) * L:(b % 8 + 1) * L, b // 8, :]).then_inc(c.stored, 16)
            sp.wait_ge(c.stored, 16 * B)

        @block.tensor
        def _(pe):
            for s in range(2):
                pe.wait_ge(c.ahead[s], 16 * c.ahead_n[s])
                for t in range(2):
                    for k in range(KT):
                        last = pe.matmul(c.banks[t][:, s * CHUNK:(s + 1) * CHUNK], hs[:, k, t * P:(t + 1) * P],
                                         c.ring[:, s, k, :], start=k == 0, stop=k == KT - 1)
            last.then_inc(c.product, 1)

        @block.vector
        def _(dve):
            dve.wait_ge(c.product, 1)
            for t in range(2):
                dve.tensor_copy(vt[:, t, :], c.banks[t][:]).then_inc(c.vec_out, 1)

    def blocks(x):
        return x.rearrange("p (b l) -> p b l", l=L)

    with c.stage() as block:
        @block.scalar
        def _(act):
            act.wait_ge(c.vec_out, 1)
            act.activation(lb[:, 1:3, :], lb[:, 1:3, :], ACT.Exp).then_inc(c.act_out, 1)
            act.wait_ge(c.vec_out, 2)
            act.activation(lf, f, ACT.Ln).then_inc(c.act_out, 1)
            act.wait_ge(c.vec_out, 3)
            act.activation(e1, bl, ACT.Exp).then_inc(c.act_out, 1)
            act.wait_ge(c.vec_out, 4)
            act.activation(kend, kend, ACT.Exp).then_inc(c.act_out, 1)

        @block.vector
        def _(dve):
            chain = Chain(dve, c.vec_done)
            b0, b1 = c.vector("bounds", 0, 4), c.vector("bounds", 4, 8)
            chain(dve.tensor_tensor(lb[:, 0, :], b0, b1, ALU.max))
            chain(dve.tensor_tensor(lb[:, 1, :], b0, lb[:, 0, :], ALU.subtract))
            chain(dve.tensor_tensor(lb[:, 2, :], b1, lb[:, 0, :], ALU.subtract))
            dve.sem_inc(c.vec_out, 1)
            dve.wait_ge(c.act_out, 1)
            chain(dve.tensor_tensor(lb[:, 3, :], lb[:, 1, :], lb[:, 2, :], ALU.add))
            chain(dve.reciprocal(lb[:, 3, :], lb[:, 3, :]))
            chain(dve.tensor_tensor(lb[:, 4, :], lb[:, 1, :], lb[:, 3, :], ALU.mult))
            chain(dve.tensor_scalar(lb[:, 5, :], lb[:, 4, :], -1.0, 1.0, ALU.mult, ALU.add))
            for h in range(H):
                part = f[:, h * NLAT:(h + 1) * NLAT]
                chain(dve.tensor_scalar(part, part, lb[:, 5, h:h + 1], lb[:, 4, h:h + 1], ALU.mult, ALU.add))
            dve.sem_inc(c.vec_out, 1)
            dve.tensor_scalar(kk, f, -1.0, 1.0, ALU.mult, ALU.add)
            chain(dve.tensor_scalar(q, q, P ** -0.5, None, ALU.mult))
            dve.wait_ge(c.act_out, 2)
            chain(dve.tensor_tensor_scan(bl, c.constant("inner"), lf, 0.0, ALU.mult, ALU.add))
            dve.sem_inc(c.vec_out, 1)
            chain(dve.tensor_tensor(blocks(kend), blocks(bl)[:, :, L - 1:L].to_broadcast([P, H * B, L]), blocks(bl),
                                    ALU.subtract))
            dve.sem_inc(c.vec_out, 1)
            dve.wait_ge(c.act_out, 3)
            dve.tensor_tensor(qe, q, e1, ALU.mult)
            dve.wait_ge(c.act_out, 4)
            dve.tensor_tensor(kend, kend, kk, ALU.mult)

    with c.stage() as block:
        pick = c.constant("pick").rearrange("p (j l) -> p j l", l=L)

        @block.vector
        def _(dve):
            chain = Chain(dve, c.vec_done)

            def first(j):
                w = L - j
                part = blocks(pairs[:, j % 2])[:, :, 0:w]
                if j >= 2:
                    dve.wait_ge(c.product, j - 1)
                dve.tensor_tensor(part, blocks(bl)[:, :, j:L], blocks(bl)[:, :, j:j + 1].to_broadcast([P, H * B, w]),
                                  ALU.subtract).then_inc(c.vec_out, 1)

            first(0)
            for j in range(L):
                w = L - j
                part = blocks(pairs[:, j % 2])[:, :, 0:w]
                if j + 1 < L:
                    first(j + 1)
                dve.wait_ge(c.act_out, j + 1)
                chain(dve.tensor_tensor(part, part, blocks(q)[:, :, j:L], ALU.mult))
                chain(dve.tensor_tensor(part, part, blocks(kk)[:, :, j:j + 1].to_broadcast([P, H * B, w]), ALU.mult))
            dve.wait_ge(c.product, L)
            for half in range(2):
                dve.tensor_copy(at[0:L, half * 512:(half + 1) * 512], c.banks[half][0:L, :])

        @block.scalar
        def _(act):
            for j in range(L):
                part = blocks(pairs[:, j % 2])[:, :, 0:L - j]
                act.wait_ge(c.vec_out, j + 1)
                act.activation(part, part, ACT.Exp).then_inc(c.act_out, 1)
            for r in range(H * B // 4):
                act.wait_ge(c.turned, r + 1)
                act.activation(kt[0:L, r * 512:(r + 1) * 512], c.banks[2 + r % 6][0:L, :], ACT.Copy).then_inc(c.drained, 1)

        @block.tensor
        def _(pe):
            for j in range(L):
                pe.wait_ge(c.vec_done, 2 * j + 2)
                for half in range(2):
                    last = pe.matmul(blocks(c.banks[half][0:L, :])[:, :, j:L], pick[:, j, :],
                                     blocks(pairs[:, j % 2])[:, half * 32:(half + 1) * 32, 0:L - j],
                                     start=j == 0, stop=j == L - 1)
                last.then_inc(c.product, 1)
            for r in range(H * B // 4):
                if r >= 6:
                    pe.wait_ge(c.drained, r - 5)
                for i in range(4):
                    last = pe.transpose(c.banks[2 + r % 6][0:L, i * P:(i + 1) * P], blocks(kend)[:, 4 * r + i, :],
                                        c.constant("ident"))
                last.then_inc(c.turned, 1)

    with c.stage() as block:
        @block.tensor
        def _(pe):
            for b in range(B):
                if b:
                    pe.wait_ge(c.vec_done, 2 * b)
                for h in range(H):
                    out = c.banks[h // 2][:, (h % 2) * NLAT + b * L:(h % 2) * NLAT + (b + 1) * L]
                    pe.matmul(out, v16[0:L, b, h * P:(h + 1) * P], at[0:L, h * NLAT + b * L:h * NLAT + (b + 1) * L],
                              start=True, stop=b == 0)
                    if b:
                        pe.matmul(out, state[:, b % 2, h * P:(h + 1) * P], qe[:, h * NLAT + b * L:h * NLAT + (b + 1) * L],
                                  start=False, stop=True)
                for h in range(H):
                    last = pe.matmul(c.banks[2 + b % 2][:, h * P:(h + 1) * P], kt[0:L, (h * B + b) * P:(h * B + b + 1) * P],
                                     v16[0:L, b, h * P:(h + 1) * P], start=True, stop=True)
                last.then_inc(c.product, 1)
            for half in range(2):
                pe.wait_ge(c.act_out, half + 1)
                pe.matmul(c.banks[4 + half][:], c.constant("ones"), sq[:, half * 512:(half + 1) * 512], start=True,
                          stop=True).then_inc(c.pe_out, 1)

        @block.vector
        def _(dve):
            chain = Chain(dve, c.vec_done)
            decay = e1.rearrange("p (h b l) -> p h b l", h=H, l=L)
            for b in range(B):
                after, before = state[:, (b + 1) % 2], state[:, b % 2]
                if b == 0:
                    chain(dve.memset(before, 0.0))
                else:
                    chain(dve.tensor_tensor(after.rearrange("p (h v) -> p h v", h=H), before.rearrange("p (h v) -> p h v", h=H),
                                            decay[:, :, b, L - 1:L].to_broadcast([P, H, P]), ALU.mult))
                dve.wait_ge(c.product, b + 1)
                if b == 0:
                    chain(dve.tensor_copy(after, c.banks[2][:]))
                else:
                    chain(dve.tensor_tensor(after, after, c.banks[2 + b % 2][:], ALU.add))
            for half in range(2):
                part = slice(half * 512, (half + 1) * 512)
                dve.wait_ge(c.pe_out, half + 1)
                chain(dve.tensor_scalar(rs[:, part], c.banks[4 + half][:], 1.0 / P, EPS, ALU.mult, ALU.add))
                dve.reciprocal(rs[:, part], rs[:, part]).then_inc(c.vec_out, 1)
            for half in range(2):
                part = slice(half * 512, (half + 1) * 512)
                dve.wait_ge(c.act_out, 3 + half)
                chain(dve.scalar_tensor_tensor(sq[:, part], c.banks[half][:], c.vector("gnorm"), rs[:, part], ALU.mult,
                                               ALU.mult))
                dve.tensor_tensor(c.mg[:, 2 * half:2 * half + 2, 0:NLAT],
                                  sq[:, part].rearrange("p (h t) -> p h t", h=2),
                                  g[:, part].rearrange("p (h t) -> p h t", h=2), ALU.mult)

        @block.scalar
        def _(act):
            act.wait_ge(c.product, B)
            for half in range(2):
                act.activation(sq[:, half * 512:(half + 1) * 512], c.banks[half][:], ACT.Square).then_inc(c.act_out, 1)
            for half in range(2):
                act.wait_ge(c.vec_out, half + 1)
                part = rs[:, half * 512:(half + 1) * 512]
                act.activation(part, part, ACT.Sqrt).then_inc(c.act_out, 1)


class S5Tables:

    def __init__(self, c):
        self.c = c
        spare = c.work[:, 15360 - 8 * NLAT:].rearrange("p (i t) -> p i t", i=8)
        self.table = ((c.x[:, :, 0:NLAT], c.h[:, :, 0:NLAT]), (c.mg[:, :, NLAT:T], spare))
        self.kept = c.s5_kept
        self.s = c.work[:, 8192:8192 + 16 * S5_TILES].rearrange("p (a i) -> p a i", i=S5_TILES)
        self.turn = c.work[:, 9216:9216 + 2 * S5_TILES].rearrange("p (a i) -> p a i", i=S5_TILES)
        at = 9728
        self.scratch = [c.work[:, at + i * (4 * NLAT):at + (i + 1) * (4 * NLAT)] for i in range(2)]

    MAGIC = 1.5 * 2.0 ** 23

    def reduce(self, dve, chain, out, n, x, step, parts):
        chain(dve.tensor_scalar(n, x, 1.0 / step, self.MAGIC, ALU.mult, ALU.add))
        chain(dve.tensor_scalar(n, n, self.MAGIC, None, ALU.subtract))
        for part in parts:
            chain(dve.scalar_tensor_tensor(out, n, -part, x, ALU.mult, ALU.add))
            x = out

    def series(self, dve, chain, out, x, coefficients):
        *rest, last = coefficients
        chain(dve.tensor_scalar(out, x, last, None, ALU.mult))
        for coefficient in reversed(rest):
            chain(dve.scalar_tensor_tensor(out, out, coefficient, x, ALU.add, ALU.mult))

    def exponential(self, dve, chain, out, x, r, n, scratch):
        ln2 = math.log(2.0)
        hi = 0.693359375
        chain(dve.tensor_scalar(scratch, x, -87.0, 88.0, ALU.max, ALU.min))
        self.reduce(dve, chain, r, n, scratch, ln2, (hi, ln2 - hi))
        self.series(dve, chain, out, r, [1.0 / math.factorial(i) for i in range(1, 9)])
        chain(dve.tensor_scalar(n, n, 127.0, 2.0 ** 23, ALU.add, ALU.mult))
        chain(dve.tensor_copy(scratch.bitcast(I32), n))
        chain(dve.scalar_tensor_tensor(out, out, 1.0, scratch, ALU.add, ALU.mult))

    def vector(self, dve):
        c, s, kept, turn = self.c, self.s, self.kept, self.turn
        chain = Chain(dve, c.vec_done)
        are, aim = c.vector("s5_are"), c.vector("s5_aim")
        for half in range(2):
            dve.memset(self.table[0][half][:, :, 0:1], 1.0)
            chain(dve.memset(self.table[1][half][:, :, 0:1], 0.0))
        self.exponential(dve, chain, s[:, 0], c.vector("s5_dt"), s[:, 8], s[:, 9], s[:, 10])
        chain(dve.tensor_tensor(s[:, 1], are, s[:, 0], ALU.mult))
        self.exponential(dve, chain, kept[:, 0], s[:, 1], s[:, 8], s[:, 9], s[:, 10])
        chain(dve.tensor_tensor(s[:, 3], aim, s[:, 0], ALU.mult))
        hi = 1.5703125
        mid = float(np.float32(math.pi / 2 - hi))
        self.reduce(dve, chain, s[:, 4], s[:, 8], s[:, 3], math.pi / 2, (hi, mid, math.pi / 2 - hi - mid))
        chain(dve.tensor_tensor(s[:, 5], s[:, 4], s[:, 4], ALU.mult))
        self.series(dve, chain, s[:, 9], s[:, 5], [(-1.0) ** i / math.factorial(2 * i + 1) for i in range(1, 6)])
        chain(dve.scalar_tensor_tensor(s[:, 9], s[:, 9], 1.0, s[:, 4], ALU.add, ALU.mult))
        self.series(dve, chain, s[:, 10], s[:, 5], [(-1.0) ** i / math.factorial(2 * i) for i in range(1, 7)])
        chain(dve.tensor_scalar(s[:, 10], s[:, 10], 1.0, None, ALU.add))
        self.reduce(dve, chain, s[:, 11], s[:, 12], s[:, 8], 4.0, (4.0,))
        chain(dve.tensor_scalar(s[:, 12], s[:, 11], -1.0, None, ALU.mult))
        chain(dve.tensor_tensor(s[:, 12], s[:, 12], s[:, 11], ALU.max))
        chain(dve.tensor_scalar(s[:, 13], s[:, 12], -1.0, 1.0, ALU.mult, ALU.add))
        chain(dve.scalar_tensor_tensor(s[:, 14], s[:, 12], -2.0, s[:, 11], ALU.add, ALU.mult))
        for out, first, second, op in ((7, (10, 13), (9, 14), ALU.add), (6, (9, 13), (10, 14), ALU.subtract)):
            chain(dve.tensor_tensor(s[:, 11], s[:, first[0]], s[:, first[1]], ALU.mult))
            chain(dve.tensor_tensor(s[:, 12], s[:, second[0]], s[:, second[1]], ALU.mult))
            chain(dve.tensor_tensor(s[:, out], s[:, 11], s[:, 12], op))
        chain(dve.tensor_tensor(s[:, 9], kept[:, 0], s[:, 7], ALU.mult))
        chain(dve.tensor_tensor(s[:, 2], kept[:, 0], s[:, 6], ALU.mult))
        chain(dve.tensor_scalar(s[:, 9], s[:, 9], -1.0, None, ALU.add))
        chain(dve.tensor_tensor(s[:, 10], are, are, ALU.mult))
        chain(dve.tensor_tensor(s[:, 11], aim, aim, ALU.mult))
        chain(dve.tensor_tensor(s[:, 10], s[:, 10], s[:, 11], ALU.add))
        chain(dve.reciprocal(s[:, 10], s[:, 10]))
        for out, first, second, op in ((1, (s[:, 9], are), (s[:, 2], aim), ALU.add),
                                       (2, (s[:, 2], are), (s[:, 9], aim), ALU.subtract)):
            chain(dve.tensor_tensor(s[:, 11], *first, ALU.mult))
            chain(dve.tensor_tensor(s[:, 12], *second, ALU.mult))
            chain(dve.tensor_tensor(s[:, 11], s[:, 11], s[:, 12], op))
            chain(dve.tensor_tensor(kept[:, out], s[:, 11], s[:, 10], ALU.mult))
        dve.tensor_copy(turn[:, 0], s[:, 7])
        chain(dve.tensor_copy(turn[:, 1], s[:, 6]))
        for k in range(S5_STEPS):
            w = 1 << k
            for half in range(2):
                cos, sin = self.table[0][half], self.table[1][half]
                re, im = (turn[:, r, 8 * half:8 * half + 8].unsqueeze(2).to_broadcast([P, 8, w]) for r in range(2))
                s0, s1 = (x[:, 0:8 * w].rearrange("p (i t) -> p i t", i=8) for x in self.scratch)
                chain.mark(dve.tensor_tensor(s0, cos[:, :, 0:w], re, ALU.mult))
                chain(dve.tensor_tensor(s1, sin[:, :, 0:w], im, ALU.mult))
                chain(dve.tensor_tensor(cos[:, :, w:2 * w], s0, s1, ALU.subtract))
                chain.mark(dve.tensor_tensor(s0, cos[:, :, 0:w], im, ALU.mult))
                chain(dve.tensor_tensor(s1, sin[:, :, 0:w], re, ALU.mult))
                chain(dve.tensor_tensor(sin[:, :, w:2 * w], s0, s1, ALU.add))
            if k + 1 < S5_STEPS:
                chain.mark(dve.tensor_tensor(s[:, 11], turn[:, 0], turn[:, 0], ALU.mult))
                chain.mark(dve.tensor_tensor(s[:, 12], turn[:, 1], turn[:, 1], ALU.mult))
                chain(dve.tensor_tensor(s[:, 13], turn[:, 0], turn[:, 1], ALU.mult))
                chain.mark(dve.tensor_tensor(turn[:, 0], s[:, 11], s[:, 12], ALU.subtract))
                chain(dve.tensor_scalar(turn[:, 1], s[:, 13], 2.0, None, ALU.mult))


def s5(c, a, tables, following):
    big = c.big[:].rearrange("p k t -> p (k t)")
    N = S5_TILES
    u = big[:, 3 * HG_HEADS * NLAT:4 * HG_HEADS * NLAT].rearrange("p (i t) -> p i t", i=4)
    y = big[:, 4 * HG_HEADS * NLAT:5 * HG_HEADS * NLAT].rearrange("p (i t) -> p i t", i=4)
    gate = big[:, 5 * HG_HEADS * NLAT:6 * HG_HEADS * NLAT].rearrange("p (i t) -> p i t", i=4)
    G = 4
    parts = [big[:, (6 + i) * G * NLAT:(7 + i) * G * NLAT].rearrange("p (i t) -> p i t", i=G) for i in range(6)]
    wb, wc, ws, scratch = c.carve((2, 4, P), (2, N, 2 * S5_H), (2, N, 2 * S5_H), (2, N, 2 * S5_H))
    x = c.ring[:].rearrange("p s k n -> p (s k n)").rearrange("p (i r t) -> p i r t", i=N, r=2)
    glu = rows(a["s5_glu_w_2"][0])

    with c.stage() as block:
        @block.sync
        def _(sp):
            sp.dma_start(wb, a["s5_b"].rearrange("r p i n -> p r i n")).then_inc(c.side_loaded, 16)
            sp.dma_start(wc, a["s5_c"].rearrange("r p i n -> p r i n")).then_inc(c.stored, 16)
            fetch(c, sp, first_loads(glu, 0, HG_W // CHUNK, ((0, HG_W // P),)), lambda s: sp.wait_ge(c.pe_out, 4))

        @block.tensor
        def _(pe):
            pe.wait_ge(c.side_loaded, 16)
            for i in range(N):
                rows_ = slice(32 * (i % 4), 32 * (i % 4) + 32)
                if i >= 4:
                    pe.wait_ge(c.drained, i - 3)
                for r in range(2):
                    last = pe.matmul(c.banks[4 + i % 4][:, r * NLAT:(r + 1) * NLAT], wb[rows_, r, i // 4, :],
                                     u[rows_, i // 4, :], start=True, stop=True)
                last.then_inc(c.product, 1)
            for i in range(N):
                if i % G == 0:
                    pe.wait_ge(c.vec_out, i // G + 1)
                out = c.banks[i // 4][32 * (i % 4):32 * (i % 4) + 32, 0:NLAT]
                pe.matmul(out, ws[:, 0, i, :], x[:, i, 0, :], start=True, stop=False)
                last = pe.matmul(out, ws[:, 1, i, :], x[:, i, 1, :], start=False, stop=True)
                if i % 4 == 3:
                    last.then_inc(c.pe_out, 1)

        @block.scalar
        def _(act):
            for i in range(N):
                act.wait_ge(c.product, i + 1)
                act.activation(x[:, i], c.banks[4 + i % 4][:].rearrange("p (r t) -> p r t", r=2), ACT.Copy
                               ).then_inc(c.drained, 1)
            for i in range(4):
                act.wait_ge(c.vec_out, N // G + i + 1)
                act.activation(y[:, i], y[:, i], ACT.Gelu)

        @block.vector
        def _(dve):
            chain = Chain(dve, c.vec_done)
            re, im = (tables.kept[:, r].unsqueeze(2).to_broadcast([P, N, 2 * S5_H]) for r in (1, 2))
            dve.wait_ge(c.stored, 16)
            chain.mark(dve.tensor_tensor(scratch[:, 0], wc[:, 0], re, ALU.mult))
            chain(dve.tensor_tensor(scratch[:, 1], wc[:, 1], im, ALU.mult))
            chain(dve.tensor_tensor(ws[:, 0], scratch[:, 0], scratch[:, 1], ALU.subtract))
            chain.mark(dve.tensor_tensor(scratch[:, 0], wc[:, 0], im, ALU.mult))
            chain(dve.tensor_tensor(scratch[:, 1], wc[:, 1], re, ALU.mult))
            chain(dve.scalar_tensor_tensor(ws[:, 1], scratch[:, 0], -1.0, scratch[:, 1], ALU.mult, ALU.subtract))
            a0, a1, b0, b1, re, im = parts
            for g in range(N // G):
                dve.wait_ge(c.drained, (g + 1) * G)
                half, first = g * G // 8, g * G % 8
                cos, sin = (tables.table[r][half][:, first:first + G, :] for r in range(2))
                xr, xi = x[:, g * G:(g + 1) * G, 0, :], x[:, g * G:(g + 1) * G, 1, :]
                chain.mark(dve.tensor_tensor(a0, xr, cos, ALU.mult))
                mark = chain.mark(dve.tensor_tensor(a1, xi, sin, ALU.mult))
                chain.mark(dve.tensor_tensor(b0, xi, cos, ALU.mult))
                chain.wait(mark)
                mark = chain.mark(dve.tensor_tensor(re, a0, a1, ALU.add))
                other = chain.mark(dve.tensor_tensor(b1, xr, sin, ALU.mult))
                chain.wait(other)
                done = chain.mark(dve.tensor_tensor(im, b0, b1, ALU.subtract))
                chain.wait(mark)
                for part in (re, im):
                    if part is im:
                        chain.wait(done)
                    for i in range(G):
                        t = g * G + i
                        mark = chain.mark(dve.tensor_tensor_scan(part[:, i], tables.kept[:, 0, t:t + 1].to_broadcast([P, NLAT]),
                                                                 part[:, i], 0.0, ALU.mult, ALU.add))
                chain.wait(mark)
                chain.mark(dve.tensor_tensor(a0, re, cos, ALU.mult))
                mark = chain.mark(dve.tensor_tensor(a1, im, sin, ALU.mult))
                chain.mark(dve.tensor_tensor(b0, im, cos, ALU.mult))
                chain.wait(mark)
                chain.mark(dve.tensor_tensor(xr, a0, a1, ALU.subtract))
                chain(dve.tensor_tensor(b1, re, sin, ALU.mult))
                chain(dve.tensor_tensor(xi, b0, b1, ALU.add))
                dve.sem_inc(c.vec_out, 1)
            for i in range(4):
                dve.wait_ge(c.pe_out, i + 1)
                dve.scalar_tensor_tensor(y[:, i], u[:, i], c.vector("s5_d", i, i + 1), c.banks[i][:, 0:NLAT], ALU.mult,
                                         ALU.add).then_inc(c.vec_out, 1)

    ks = HG_W // P
    project(c, glu, 0, HG_W // CHUNK, y, NLAT,
            lambda e, bank, tile: e.activation(gate[:, tile], bank, ACT.Sigmoid, bias=c.vector("glu_b", tile, tile + 1)),
            on="scalar", splits=((0, ks),), following=following)
    with c.stage() as block:
        @block.vector
        def _(dve):
            dve.tensor_tensor(c.mg[:, ks:2 * ks, 0:NLAT], y, gate, ALU.mult)


def peer(c, a):
    H, K, S = PEER_H, PEER_K, PEER_SLOTS
    LOWEST = -3.0e38
    big = c.big[:].rearrange("p k t -> p (k t)")
    qh = big[:, 0:16 * NLAT].rearrange("p (i t) -> p i t", i=16)
    scores = big[:, 16 * NLAT:32 * NLAT]
    tokens = big[:, 32 * NLAT:32 * NLAT + 2 * D].rearrange("p (t f) -> p t f", t=2)
    keys = big[:, 32 * NLAT + 2 * D:32 * NLAT + 2 * D + 2 * PEER_N].rearrange("p (r n) -> p r n", r=2)
    experts = big[:, 11008:11008 + 2 * S]
    gates = big[:, 11264:11264 + 2 * S]
    experts_u = experts.bitcast(U32)
    hs = moving(c.h, NCTX, T)
    project(c, rows(a["peer_wq_2"][0]), 0, 2 * H * P // CHUNK, hs, NLAT,
            lambda e, bank, tile: e.tensor_copy(qh[:, tile, :], bank))

    with c.stage() as block:
        @block.sync
        def _(sp):
            sp.dma_start(keys, a["keys"]).then_inc(c.side_loaded, 16)

        @block.tensor
        def _(pe):
            for r in range(4):
                for i in range(4):
                    t, k = (4 * r + i) // KT, (4 * r + i) % KT
                    last = pe.transpose(c.banks[r][:, i * P:(i + 1) * P], hs[:, k, t * P:(t + 1) * P], c.constant("ident"))
                last.then_inc(c.product, 1)
            pe.wait_ge(c.side_loaded, 16)
            for t in range(2):
                for i in range(2 * H):
                    n = (2 * H * t + i) // 4
                    if i % 4 == 0 and n >= 4:
                        pe.wait_ge(c.drained, n)
                    last = pe.matmul(c.banks[4 + n if n < 4 else n - 4][:, (i % 4) * P:(i % 4 + 1) * P],
                                     qh[:, i, t * P:(t + 1) * P], keys[:, i % 2, :], start=True, stop=True)
                    if i % 4 == 3:
                        last.then_inc(c.product, 1)

        @block.vector
        def _(dve):
            for r in range(4):
                dve.wait_ge(c.product, r + 1)
                dve.tensor_copy(tokens[:, r // 2, (r % 2) * 512:(r % 2 + 1) * 512], c.banks[r][:]).then_inc(c.drained, 1)
            for n in range(8):
                dve.wait_ge(c.product, 5 + n)
                dve.tensor_copy(scores[:, n * 512:(n + 1) * 512], c.banks[4 + n if n < 4 else n - 4][:]).then_inc(c.drained, 1)

    s, v, idx, idf, cand, best, less, pos, sel, eq, ef, small = c.carve(
        (2 * H, PEER_N), (2 * H, K), (2 * H, K), (2 * H, K), (H, K * K), (H, K), (H, K), (H, K), (2, S), (S, K), (2, S), (2, H))
    idx, pos = idx.bitcast(U32), pos.bitcast(U32)
    sel_u = sel.bitcast(U32)
    with c.nc.Fori(0, 2) as t:
        with c.stage() as block:
            @block.vector
            def _(dve):
                chain = Chain(dve, c.vec_done)
                chain(dve.tensor_copy(s.rearrange("p i n -> p (i n)"), scores[:, bass.ds(t * (2 * H * PEER_N), 2 * H * PEER_N)]))

                def best16(table, values, places, count):
                    for r in range(2):
                        part = slice(8 * r, 8 * r + 8)
                        for i in range(count):
                            done = chain.mark(dve.max(out=values[:, i, part], in_=table[:, i, :]))
                        chain.wait(done)
                        for i in range(count):
                            done = chain.mark(dve.max_index(out=places[:, i, part], in_max=values[:, i, part],
                                                            in_values=table[:, i, :]))
                        if r == 0:
                            chain.wait(done)
                            for i in range(count):
                                done = chain.mark(dve.match_replace(out=table[:, i, :], in_to_replace=values[:, i, part],
                                                                    in_values=table[:, i, :], imm_value=LOWEST))
                        chain.wait(done)

                best16(s, v, idx, 2 * H)
                chain(dve.tensor_copy(idf, idx))
                v4 = v.rearrange("p (h r) k -> p h r k", r=2)
                chain(dve.tensor_tensor(cand.rearrange("p h (x y) -> p h x y", y=K),
                                        v4[:, :, 0, :].unsqueeze(3).to_broadcast([P, H, K, K]),
                                        v4[:, :, 1, :].unsqueeze(2).to_broadcast([P, H, K, K]), ALU.add))
                best16(cand, best, pos, H)
                flat = pos.rearrange("p h k -> p (h k)")
                chain(dve.tensor_scalar(sel_u[:, 0], flat, 4, None, ALU.logical_shift_right))
                chain(dve.tensor_scalar(sel_u[:, 1], flat, K - 1, None, ALU.bitwise_and))
                chain(dve.tensor_copy(ef, sel_u))
                i4 = idf.rearrange("p (h r) k -> p h r k", r=2)
                for r in range(2):
                    chain(dve.tensor_tensor(eq, ef[:, r].unsqueeze(2).to_broadcast([P, S, K]),
                                            c.constant("iota").unsqueeze(1).to_broadcast([P, S, K]), ALU.is_equal))
                    e4 = eq.rearrange("p (h k) x -> p h k x", h=H)
                    chain(dve.tensor_tensor(e4, e4, i4[:, :, r, :].unsqueeze(2).to_broadcast([P, H, K, K]), ALU.mult))
                    chain(dve.tensor_reduce(sel[:, r], eq, AX.X, ALU.add))
                chain(dve.tensor_scalar(sel[:, 0], sel[:, 0], float(PEER_N), None, ALU.mult))
                chain(dve.tensor_tensor(experts_u[:, bass.ds(t * S, S)], sel[:, 0], sel[:, 1], ALU.add))
                chain(dve.tensor_tensor(less, best, best[:, :, 0:1].to_broadcast([P, H, K]), ALU.subtract))
                dve.sem_inc(c.vec_out, 1)
                dve.wait_ge(c.act_out, 1)
                chain(dve.reduce_sum(small[:, 0], less, AX.X))
                chain(dve.reciprocal(small[:, 1], small[:, 0]))
                dve.tensor_tensor(gates[:, bass.ds(t * S, S)].rearrange("p (h k) -> p h k", h=H), less,
                                  small[:, 1].unsqueeze(2).to_broadcast([P, H, K]), ALU.mult)

            @block.scalar
            def _(act):
                act.wait_ge(c.vec_out, 1)
                act.activation(less, less, ACT.Exp).then_inc(c.act_out, 1)

    R = PEER_RING
    fetched, diag, place, dot, gl, w, gate4, acc = c.carve(
        (R, 2 * D), (R, P), (R,), (R,), (R,), (R,), (R,), (D,))
    urows, vrows = fetched[:, :, 0:D], fetched[:, :, D:2 * D]
    place_u = place.bitcast(U32)
    groups = S // R
    for t in range(2):
        with c.stage() as block:
            def run(engine, body):
                body(0)
                with engine.Fori(0, groups - 2) as j:
                    body(j + 1)
                body(groups - 1)

            had = 16 * groups * t

            @block.gpsimd
            def _(pool):
                def body(gr):
                    later = not isinstance(gr, int) or gr > 0
                    for r in range(R):
                        if later:
                            pool.wait_ge(c.u_free[r], 1)
                            pool.sem_clear(c.u_free[r])
                            pool.wait_ge(c.v_free[r], 1)
                            pool.sem_clear(c.v_free[r])
                        pool.tensor_copy(place_u[:, r:r + 1], experts_u[:, bass.ds(gr * R + (t * S + r), 1)]
                                         ).then_inc(c.pool_done, 1)
                        pool.wait_ge(c.pool_done, 1)
                        pool.sem_clear(c.pool_done)
                        pool.indirect_dma_start(
                            out=fetched[:, r, :], out_offset=None, in_=a["experts"],
                            in_offset=bass.IndirectOffsetOnAxis(ap=place_u[:, r:r + 1], axis=0)
                        ).then_inc(c.gathered[r], 16)

                run(pool, body)

            @block.vector
            def _(dve):
                def body(gr):
                    later = not isinstance(gr, int) or gr > 0
                    if later:
                        dve.wait_ge(c.act_out, gr * R)
                    dve.tensor_copy(gate4, gates[:, bass.ds(gr * R + t * S, R)]).then_inc(c.vec_done, 1)
                    for r in range(R):
                        dve.wait_ge(c.gathered[r], gr * 16 + (16 + had))
                        dve.tensor_tensor_reduce(out=urows[:, r, :], in0=urows[:, r, :], in1=tokens[:, t, :], scale=1.0,
                                                 scalar=0.0, op0=ALU.mult, op1=ALU.add, accum_out=dot[:, r:r + 1]
                                                 ).then_inc(c.vec_out, 1)

                run(dve, body)

            @block.scalar
            def _(act):
                def body(gr):
                    later = not isinstance(gr, int) or gr > 0
                    act.wait_ge(c.vec_done, gr + 1)
                    for r in range(R):
                        act.wait_ge(c.vec_out, gr * R + (r + 1))
                        act.sem_inc(c.u_free[r], 1)
                        act.activation(gl[:, r:r + 1], dot[:, r:r + 1], ACT.Gelu).then_inc(c.act_done, 1)
                        act.wait_ge(c.act_done, gr * (2 * R) + (2 * r + 1))
                        act.activation(w[:, r:r + 1], gl[:, r:r + 1], ACT.Copy, scale=gate4[:, r:r + 1]).then_inc(c.act_done, 1)
                        act.wait_ge(c.act_done, gr * (2 * R) + (2 * r + 2))
                        if later:
                            act.wait_ge(c.product, gr * R + (r + 1 - R))
                        act.activation(diag[:, r, :], c.constant("ident"), ACT.Copy, scale=w[:, r:r + 1]).then_inc(c.act_out, 1)

                run(act, body)

            @block.tensor
            def _(pe):
                def body(gr):
                    for r in range(R):
                        pe.wait_ge(c.act_out, gr * R + (r + 1))
                        pe.wait_ge(c.gathered[r], gr * 16 + (16 + had))
                        first = isinstance(gr, int) and gr == 0 and r == 0
                        final = isinstance(gr, int) and gr == groups - 1 and r == R - 1
                        for half in range(2):
                            last = pe.matmul(c.banks[half][:], diag[:, r, :], vrows[:, r, half * 512:(half + 1) * 512],
                                             start=first, stop=final)
                        last.then_inc(c.product, 1)
                        pe.wait_ge(c.product, gr * R + (r + 1))
                        pe.sem_inc(c.v_free[r], 1)

                run(pe, body)

        with c.stage() as block:
            @block.vector
            def _(dve):
                for half in range(2):
                    dve.tensor_copy(acc[:, half * 512:(half + 1) * 512], c.banks[half][:]).then_inc(c.vec_out, 1)
                for half in range(2):
                    dve.wait_ge(c.product, half + 1)
                    for i in range(4):
                        k = 4 * half + i
                        out = c.x[:, k, NCTX + t * P:NCTX + (t + 1) * P]
                        dve.scalar_tensor_tensor(out, c.banks[2 + half][:, i * P:(i + 1) * P], c.mod[:, 5 * KT + k, 0:1], out,
                                                 ALU.mult, ALU.add)

            @block.tensor
            def _(pe):
                for half in range(2):
                    pe.wait_ge(c.vec_out, half + 1)
                    for i in range(4):
                        last = pe.transpose(c.banks[2 + half][:, i * P:(i + 1) * P],
                                            acc[:, (4 * half + i) * P:(4 * half + i + 1) * P], c.constant("ident"))
                    last.then_inc(c.product, 1)


def second_block(c, a, stop):
    lat = (NCTX, T)
    with c.stage() as block:
        @block.vector
        def _(dve):
            for k in range(KT):
                dve.tensor_copy(c.x[:, k, NCTX:T], c.h[:, k, NCTX:T])
    tables = S5Tables(c)
    adaln(c, rows(a["ada_w_2"][0]), c.cond[:, 2:3, :].rearrange("p a k -> p k a"), c.vector("ada_b_2"), 1,
          first_loads(rows(a["w_in_2"][0]), 0, HG_W // CHUNK), beside=tables)
    norm(c, c.x, c.h, c.vector("norm_mix"), [(*lat, 0, 0, KT)])
    if stop == "norm2":
        return
    hgrn(c, a)
    w_out = rows(a["w_out_2"][0])
    s5(c, a, tables, first_loads(w_out, 0, D // CHUNK))
    if stop == "mixers":
        return
    add_gated(c, w_out, c.mg[:, :, 0:NLAT], [(*lat, 0)], 2 * KT,
              following=first_loads(rows(a["peer_wq_2"][0]), 0, 2 * PEER_H * P // CHUNK))
    norm(c, c.x, c.h, c.vector("norm_ffn"), [(*lat, 0, 3 * KT, 4 * KT)])
    if stop == "normf":
        return
    peer(c, a)
    norm(c, c.x, c.h, c.vector("final_norm"), [(*lat, 0, 0, 0)], modulated=False)


STREAMED = ("w_ada", "w_in", "w_br_ml", "w_br_da", "w_br_fn", "w_out", "w_ffn_in", "w_ffn_out", "ada_w_2", "w_in_2", "w_out_2",
            "s5_glu_w_2", "peer_wq_2")
PACKED = ("vectors", "constants", "residual", "s5_b", "s5_c", "keys", "experts")
OUT = (P, KT, NLAT)


def build(nc, a, out, stop=None):
    ctx = ExitStack()
    with ctx:
        c = Core(nc, ctx)
        load_small(c, a)
        if first_block(c, a, stop) and stop != "first":
            second_block(c, a, stop)
        with nc.Block() as block:
            @block.sync
            def _(sp):
                sp.dma_start(out, c.h[:, :, NCTX:T]).then_inc(c.stored, 16)
                sp.wait_ge(c.stored, 16)


def columns(v):
    v = np.asarray(v)
    return v.reshape(-1, P).T


def pack_vectors(x):
    out = np.zeros((P, N_VEC), np.float32)

    def put(name, value):
        at, width = VEC[name]
        assert value.shape[1] == width, (name, value.shape, width)
        out[:value.shape[0], at:at + width] = value

    put("c", np.concatenate([columns(x["c_ctx"]), columns(x["c"]), columns(x["c_2"])], 1))
    for name, key in (("b_ada", "b_ada"), ("norm_g", "norm_g"), ("ml_head_g", "ml_head_g"), ("da_head_g", "da_head_g"),
                      ("final_g", "final_g"), ("ada_b_2", "ada_b_2"), ("norm_mix", "norm_mix_w_2"),
                      ("norm_ffn", "norm_ffn_w_2"), ("final_norm", "final_norm_w_2"), ("gnorm", "hg_gnorm_w_2"),
                      ("s5_d", "s5_d_2"), ("glu_b", "s5_glu_b_2"), ("bounds", "hg_lower_bounds_2")):
        put(name, columns(x[key]))
    put("lam", np.broadcast_to(x["da_lam"].reshape(1, -1), (P, 2 * 4 * DA_DH)))
    put("gate_b", np.ascontiguousarray(x["ml_gate_b"].reshape(DEPTH * 4, ML_HEADS).T))
    put("s5_are", columns(x["s5_a_re_2"]))
    put("s5_aim", columns(x["s5_a_im_2"]))
    put("s5_dt", columns(np.repeat(x["s5_log_dt_2"].reshape(-1), S5_P)))
    return out


def pack_constants():
    out = np.zeros((P, N_CST), np.float32)

    def put(name, value):
        at, width = CST[name]
        out[:, at:at + width] = np.broadcast_to(value, (P, width))

    at = np.arange(P)
    put("ident", np.eye(P))
    put("ones", np.ones((P, P)))
    put("upper", at[:, None] <= at[None, :])
    put("lower", at[:, None] >= at[None, :])
    turn = np.zeros((P, P))
    half = DA_DH // 2
    for p in range(P):
        first = p % DA_DH < half
        turn[p + half if first else p - half, p] = -1.0 if first else 1.0
    put("turn", turn)
    n_freq = DA_DH // 4
    inv = np.float32(10000.0) ** (-np.arange(n_freq, dtype=np.float32) / n_freq)
    r, col = np.repeat(np.arange(NLAT // 64, dtype=np.float32), 64), np.tile(np.arange(64, dtype=np.float32), NLAT // 64)
    angle = np.concatenate([r[:, None] * inv, col[:, None] * inv], -1)
    spread = angle[:, at % half].T
    put("cos", np.cos(spread))
    put("sin", np.sin(spread))
    k = np.arange(FN_C)
    phase = 2 * np.pi * (np.outer(k, k) % FN_C) / FN_C
    dft = np.concatenate([np.cos(phase), np.sin(phase), -np.sin(phase)], 1) / FN_C ** 0.5
    put("dft", dft.reshape(2, P, 3 * FN_C).transpose(1, 0, 2).reshape(P, -1))
    put("pick", np.eye(HG_SUB).reshape(1, -1))
    put("inner", (np.arange(HG_HEADS * NLAT) % HG_SUB != 0)[None, :])
    put("iota", np.arange(PEER_K)[None, :])
    return out


def pack_inputs(x):
    tokens = np.concatenate([x["ctx"][0], x["x"][0]], 0)
    m = {name: np.ascontiguousarray(x[name]) for name in STREAMED}
    m["vectors"] = pack_vectors(x)
    m["constants"] = pack_constants()
    m["residual"] = np.ascontiguousarray(tokens.T.reshape(KT, P, T).transpose(1, 0, 2))
    b = np.zeros((2, P, 4, P), np.float32)
    cc = np.zeros((2, P, S5_TILES, 2 * S5_H), np.float32)
    for part, (bn, cn) in enumerate((("s5_b_re_2", "s5_c_re_2"), ("s5_b_im_2", "s5_c_im_2"))):
        for g in range(S5_G):
            i, second = g // 2, g % 2
            row = 2 * S5_H * (i % 4) + S5_H * second
            b[part, row:row + S5_H, i // 4, S5_P * second:S5_P * (second + 1)] = x[bn][0, g].T
            cc[part, S5_P * second:S5_P * (second + 1), i, S5_H * second:S5_H * (second + 1)] = x[cn][0, g].T
    m["s5_b"], m["s5_c"] = b, cc
    m["experts"] = np.concatenate([x["peer_u_2"][0], x["peer_v_2"][0]], 1)
    m["keys"] = np.ascontiguousarray(np.stack([x["peer_keys1_2"][0].T, x["peer_keys2_2"][0].T], 1))
    return m


def kernel(**inputs):
    import concourse.bacc as _bacc
    from concourse.bass_utils import run_bass_kernel_spmd as _run

    arrays = pack_inputs({k: np.asarray(v) for k, v in inputs.items()})
    nc = _bacc.Bacc("TRN2", target_bir_lowering=False, num_devices=1)
    a = {n: nc.dram_tensor(n, v.shape, F32, kind="ExternalInput").ap() for n, v in arrays.items()}
    a["rows"] = nc.dram_tensor("rows", (ML_HEADS, 4, T), F32, kind="Internal").ap()
    out = nc.dram_tensor("out", OUT, F32, kind="ExternalOutput").ap()
    build(nc, a, out)
    r = _run(nc, [arrays], core_ids=[0])
    got = r.results[0]["out"]
    return np.ascontiguousarray(got.transpose(2, 1, 0)).reshape(1, NLAT, D)
```

```python
import math
from contextlib import ExitStack, contextmanager

import numpy as np
import concourse.bass as bass
from concourse import mybir

F32 = mybir.dt.float32
U32 = mybir.dt.uint32
I32 = mybir.dt.int32
ALU = mybir.AluOpType
ACT = mybir.ActivationFunctionType
AX = mybir.AxisListType

P = 128
D = 1024
KT = D // P
NCTX, NLAT = 256, 256
T = NCTX + NLAT
DEPTH = 2
EPS = 1e-6
CHUNK = 256
SLOTS = 4
BANKS = 8

ML_HEADS, ML_D = 4, 256
DA_HEADS, DA_DH = 8, 64
FN_GROUPS, FN_C = 4, 256
D_FF = -(-8 * D // (3 * 256)) * 256
COL_Q, COL_K, COL_V, COL_O, COL_GATE = 0, 1024, 2048, 3072, 4096
COL_DAQ = COL_GATE + 4 * ML_HEADS
COL_DAK, COL_DAV = COL_DAQ + 1024, COL_DAQ + 2048
COL_FN = COL_DAV + 1024
COL_MERGE = COL_FN + 1024
ML_COLUMNS, DA_COLUMNS, FN_COLUMNS = (COL_Q, COL_K, COL_O, COL_V), (COL_DAQ, COL_DAK, COL_DAV), (COL_FN,)

HG_HEADS, HG_W, HG_SUB = 4, 512, 16
HG_BLOCKS = NLAT // HG_SUB
S5_G, S5_H, S5_P = 32, 16, 64
S5_TILES = S5_G * S5_P // P
S5_STEPS = NLAT.bit_length() - 1
PEER_H, PEER_K, PEER_N = 8, 16, 128
PEER_SLOTS = PEER_H * PEER_K
PEER_RING = 8

VEC = {}


def _pack_columns():
    at = 0
    for name, width in (("c", 24), ("b_ada", 2 * 48), ("norm_g", 2 * 2 * KT), ("ml_head_g", 2 * KT), ("da_head_g", 2 * KT),
                        ("final_g", KT), ("ada_b_2", 48), ("norm_mix", KT), ("norm_ffn", KT), ("final_norm", KT),
                        ("gnorm", 1), ("s5_d", 4), ("glu_b", 4), ("bounds", 2 * 4), ("lam", 2 * 4 * DA_DH),
                        ("gate_b", 2), ("s5_are", S5_TILES), ("s5_aim", S5_TILES), ("s5_dt", S5_TILES)):
        VEC[name] = (at, width)
        at += width
    return at


N_VEC = _pack_columns()

CST = {}


def _constant_columns():
    at = 0
    for name, width in (("ident", P), ("ones", P), ("upper", P), ("lower", P), ("turn", P), ("cos", NLAT), ("sin", NLAT),
                        ("dft", 2 * 3 * FN_C), ("pick", HG_SUB * HG_SUB), ("inner", HG_HEADS * NLAT), ("iota", PEER_K)):
        CST[name] = (at, width)
        at += width
    return at


N_CST = _constant_columns()


class Chain:

    def __init__(self, engine, semaphore):
        self.engine, self.semaphore, self.n = engine, semaphore, 0

    def mark(self, instruction):
        instruction.then_inc(self.semaphore, 1)
        self.n += 1
        return self.n

    def wait(self, n=None):
        self.engine.wait_ge(self.semaphore, self.n if n is None else n)

    def __call__(self, instruction):
        self.mark(instruction)
        self.wait()


class Core:

    def __init__(self, nc, ctx):
        self.nc = nc

        def sb(name, shape, dtype=F32):
            return ctx.enter_context(nc.sbuf_tensor(name, shape, dtype))

        self.cst = sb("constants_sb", [P, N_CST])
        self.vec = sb("vectors_sb", [P, N_VEC])
        self.x = sb("stream", [P, KT, T])
        self.h = sb("normed", [P, KT, T])
        self.big = sb("branches", [P, 3 * KT, T])
        self.mg = sb("merged", [P, KT, T])
        self.ring = sb("weight_ring", [P, SLOTS, KT, CHUNK])
        self.mod = sb("modulation", [P, 48, 2])
        self.modA = sb("norm_scales", [P, 2, KT])
        self.cond = sb("condition", [P, 3, KT])
        self.lam = sb("lambda", [P, 16])
        self.s5_kept = sb("s5_kept", [P, 3, S5_TILES])
        self.hg_bounds = sb("hg_bounds", [P, 6, 4])
        self.work = sb("work", [P, 15360])
        self.banks = [ctx.enter_context(nc.psum_tensor(f"bank{i}", [P, 512], F32)) for i in range(BANKS)]

        def sem(name):
            return ctx.enter_context(nc.semaphore(name))

        self.loaded = [sem(f"loaded{i}") for i in range(SLOTS)]
        self.slot_used = sem("slot_used")
        self.product = sem("product")
        self.drained = sem("drained")
        self.vec_done = sem("vec_done")
        self.act_done = sem("act_done")
        self.pool_done = sem("pool_done")
        self.vec_out = sem("vec_out")
        self.act_out = sem("act_out")
        self.pe_out = sem("pe_out")
        self.side_loaded = sem("side_loaded")
        self.stored = sem("stored")
        self.maxima = sem("maxima")
        self.turned = sem("turned")
        self.searched = sem("searched")
        self.shifted = sem("shifted")
        self.powers = sem("powers")
        self.ranked = sem("ranked")
        self.copied = sem("copied")
        self.u_free = [sem(f"u_free{i}") for i in range(PEER_RING)]
        self.v_free = [sem(f"v_free{i}") for i in range(PEER_RING)]
        self.sems = [*self.loaded, *self.u_free, *self.v_free, self.slot_used, self.product, self.drained,
                     self.vec_done, self.act_done, self.pool_done,
                     self.vec_out, self.act_out, self.pe_out, self.side_loaded, self.stored, self.maxima,
                     self.turned, self.copied, self.searched, self.shifted, self.powers, self.ranked]
        nums = sorted(s.num for s in self.sems)
        assert nums == list(range(nums[0], nums[0] + len(nums)))
        self.sem_range = range(nums[0], nums[-1] + 1)

        self.ahead = [sem(f"ahead{i}") for i in range(SLOTS)]
        self.ahead_n = [0] * SLOTS
        self.fetched = False
        self.gathered = [sem(f"gathered{i}") for i in range(PEER_RING)]

    def constant(self, name):
        at, width = CST[name]
        return self.cst[:, at:at + width]

    def vector(self, name, lo=0, hi=None):
        at, width = VEC[name]
        return self.vec[:, at + lo:at + (width if hi is None else hi)]

    @contextmanager
    def stage(self):
        with self.nc.Block(no_gpsimd_drain=True) as block:
            yield block
        self.nc.gpsimd.sem_clear(self.sem_range)
        self.nc.all_engine_barrier(sem_only=True)

    def carve(self, *shapes):
        at, out = 0, []
        for shape in shapes:
            n = math.prod(shape)
            view = self.work[:, at:at + n]
            if len(shape) == 2:
                view = view.rearrange("p (a b) -> p a b", b=shape[1])
            elif len(shape) == 3:
                view = view.rearrange("p (a b c) -> p a b c", b=shape[1], c=shape[2])
            out.append(view)
            at += n
        assert at <= 15360, at
        return out


def rows(w):
    return w.rearrange("(k p) n -> p k n", p=P)


def first_loads(weight, col0, n_chunks, splits=((0, KT),)):
    pieces = [(chunk, k0, nk) for chunk in range(n_chunks) for k0, nk in splits][:SLOTS]
    return [weight[:, k0:k0 + nk, col0 + chunk * CHUNK:col0 + (chunk + 1) * CHUNK] for chunk, k0, nk in pieces]


def fetch(c, engine, loads, wait_free=None):
    for s, source in enumerate(loads or ()):
        if wait_free:
            wait_free(s)
        engine.dma_start(c.ring[:, s, 0:source.shape[1], :], source).then_inc(c.ahead[s], 16)
        c.ahead_n[s] += 1
    c.fetched = bool(loads)


def project(c, weight, col0, n_chunks, rhs, n, evacuate, on="vector", splits=((0, KT),), following=None):
    pieces = len(splits)
    looped = pieces == 1 and n_chunks > 8
    whole = n_chunks // SLOTS

    def run(engine, body):
        if not looped:
            for s in range(n_chunks):
                body(0, s)
            return
        for s in range(SLOTS):
            body(0, s)
        with engine.Fori(0, whole - 1) as j:
            for s in range(SLOTS):
                body(j * SLOTS + SLOTS, s)
        for s in range(n_chunks % SLOTS):
            body(whole * SLOTS, s)

    def later(base, index, depth):
        return not isinstance(base, int) or base + index >= depth

    if not c.fetched:
        with c.stage() as block:
            @block.sync
            def _(sp):
                fetch(c, sp, first_loads(weight, col0, n_chunks, splits))
    had = list(c.ahead_n)

    with c.stage() as block:
        @block.sync
        def _(sp):
            def load(base, s):
                for piece, (k0, nk) in enumerate(splits):
                    i = s * pieces + piece
                    if not later(base, i, SLOTS):
                        continue
                    held, its_piece = (i - SLOTS) // pieces, (i - SLOTS) % pieces
                    if its_piece == pieces - 1:
                        sp.wait_ge(c.product, base * 2 + 2 * (held + 1))
                    else:
                        sp.wait_ge(c.slot_used, held * (pieces - 1) + its_piece + 1)
                    sp.dma_start(c.ring[:, i % SLOTS, 0:nk, :],
                                 weight[:, k0:k0 + nk, bass.ds(base * CHUNK + (s * CHUNK + col0), CHUNK)]
                                 ).then_inc(c.loaded[i % SLOTS], 16)

            run(sp, load)

            def wait_free(s):
                mine = [i for i in range(n_chunks * pieces) if i % SLOTS == s]
                if mine:
                    chunk, piece = mine[-1] // pieces, mine[-1] % pieces
                    if piece == pieces - 1:
                        sp.wait_ge(c.product, 2 * (chunk + 1))
                    else:
                        sp.wait_ge(c.slot_used, chunk * (pieces - 1) + piece + 1)

            fetch(c, sp, following, wait_free)

        @block.tensor
        def _(pe):
            def multiply(base, s):
                for piece, (k0, nk) in enumerate(splits):
                    i = s * pieces + piece
                    if later(base, i, SLOTS):
                        pe.wait_ge(c.loaded[i % SLOTS], base * (16 // SLOTS) + 16 * (i // SLOTS))
                    else:
                        pe.wait_ge(c.ahead[i], 16 * had[i])
                    for half in range(2):
                        tile = 2 * s + half
                        if piece == 0 and later(base * 2, tile, BANKS):
                            pe.wait_ge(c.drained, base * 2 + (tile + 1 - BANKS))
                        for k in range(nk):
                            last = pe.matmul(c.banks[tile % BANKS][:, 0:n], c.ring[:, i % SLOTS, k, half * P:(half + 1) * P],
                                             rhs[:, k0 + k, :], start=piece == 0 and k == 0,
                                             stop=piece == pieces - 1 and k == nk - 1)
                        if half == 1 and piece < pieces - 1:
                            last.then_inc(c.slot_used, 1)
                        if piece == pieces - 1:
                            last.then_inc(c.product, 1)

            run(pe, multiply)

        def drain(engine):
            def one(base, s):
                for half in range(2):
                    tile = 2 * s + half
                    engine.wait_ge(c.product, base * 2 + (tile + 1))
                    evacuate(engine, c.banks[tile % BANKS][:, 0:n], base * 2 + tile).then_inc(c.drained, 1)

            run(engine, one)

        by_name = {"vector": block.vector, "scalar": block.scalar}
        by_name[on](drain)


def moving(r, lo, hi):
    return r[:, :, lo:hi]


def load_small(c, a, following):
    with c.stage() as block:
        @block.sync
        def _(sp):
            sp.dma_start(c.vec[:], a["vectors"]).then_inc(c.side_loaded, 16)
            sp.dma_start(c.cst[:], a["constants"]).then_inc(c.loaded[0], 16)
            sp.dma_start(c.x[:], a["residual"]).then_inc(c.loaded[1], 16)
            fetch(c, sp, following)

        @block.scalar
        def _(act):
            act.wait_ge(c.side_loaded, 16)
            act.activation(c.cond[:], c.vector("c").rearrange("p (a k) -> p a k", a=3), ACT.Silu)
            act.wait_ge(c.vec_out, 1)
            act.activation(c.lam[:, 8:12], c.lam[:, 0:4], ACT.Exp).then_inc(c.act_out, 1)

        @block.vector
        def _(dve):
            chain = Chain(dve, c.vec_done)
            dve.wait_ge(c.side_loaded, 16)
            lq = c.vector("lam").rearrange("p (l a d) -> p l a d", l=DEPTH, a=4)
            scratch = c.work[:, 0:DA_DH]
            for layer in range(DEPTH):
                for pair in range(2):
                    col = 2 * layer + pair
                    chain(dve.tensor_tensor(scratch, lq[:, layer, 2 * pair, :], lq[:, layer, 2 * pair + 1, :], ALU.mult))
                    chain(dve.reduce_sum(c.lam[:, col:col + 1], scratch, AX.X))
            dve.sem_inc(c.vec_out, 1)
            dve.wait_ge(c.act_out, 1)
            for layer in range(DEPTH):
                init = 0.8 - 0.6 * math.exp(-0.3 * layer)
                e = c.lam[:, 8 + 2 * layer:10 + 2 * layer]
                chain(dve.tensor_tensor(c.lam[:, 12 + layer:13 + layer], e[:, 0:1], e[:, 1:2], ALU.subtract))
                chain(dve.tensor_scalar(c.lam[:, 14 + layer:15 + layer], c.lam[:, 12 + layer:13 + layer], init, None, ALU.add))
            dve.wait_ge(c.loaded[0], 16)
            dve.wait_ge(c.loaded[1], 16)


def adaln(c, weight, conditions, bias, n, following, beside=None):
    rows_out, = c.carve((6 * D,))
    chunks = 6 * D // CHUNK
    if not c.fetched:
        with c.stage() as block:
            @block.sync
            def _(sp):
                fetch(c, sp, first_loads(weight, 0, chunks))
    had = list(c.ahead_n)
    rounds = chunks // SLOTS

    with c.stage() as block:
        @block.sync
        def _(sp):
            with sp.Fori(0, rounds - 1) as j:
                for s in range(SLOTS):
                    sp.wait_ge(c.product, j * SLOTS + (s + 1))
                    sp.dma_start(c.ring[:, s], weight[:, :, bass.ds(j * (SLOTS * CHUNK) + (SLOTS + s) * CHUNK, CHUNK)]
                                 ).then_inc(c.loaded[s], 16)
            fetch(c, sp, following, lambda s: sp.wait_ge(c.product, (rounds - 1) * SLOTS + s + 1))

        @block.tensor
        def _(pe):
            def multiply(base, s):
                first = isinstance(base, int)
                if first:
                    pe.wait_ge(c.ahead[s], 16 * had[s])
                else:
                    pe.wait_ge(c.loaded[s], base * (16 // SLOTS))
                    pe.wait_ge(c.drained, base + (s + 1 - SLOTS))
                for k in range(KT):
                    last = pe.matmul(c.banks[s][0:n, 0:CHUNK], conditions[:, k, :], c.ring[:, s, k, :], start=k == 0,
                                     stop=k == KT - 1)
                last.then_inc(c.product, 1)

            for s in range(SLOTS):
                multiply(0, s)
            with pe.Fori(0, rounds - 1) as j:
                for s in range(SLOTS):
                    multiply(j * SLOTS + SLOTS, s)
            pe.wait_ge(c.drained, chunks)
            for tile in range(6 * KT):
                last = pe.transpose(c.banks[SLOTS][:, tile * n:(tile + 1) * n], rows_out[0:n, tile * P:(tile + 1) * P],
                                    c.constant("ident")[0:n, 0:n])
            last.then_inc(c.turned, 1)

        @block.scalar
        def _(act):
            with act.Fori(0, rounds) as j:
                for s in range(SLOTS):
                    act.wait_ge(c.product, j * SLOTS + (s + 1))
                    act.activation(rows_out[0:n, bass.ds(j * (SLOTS * CHUNK) + s * CHUNK, CHUNK)],
                                   c.banks[s][0:n, 0:CHUNK], ACT.Copy).then_inc(c.drained, 1)

        @block.vector
        def _(dve):
            if beside:
                beside.vector(dve)
            dve.wait_ge(c.turned, 1)
            turned = c.banks[SLOTS][:, 0:6 * KT * n].rearrange("p (t a) -> p t a", a=n)
            for condition in range(n):
                dve.tensor_tensor(c.mod[:, :, condition], turned[:, :, condition], bias, ALU.add)


def norm(c, source, out, gain, parts, tiles=KT, spread=D, modulated=True, into=None):
    into = out if into is None else into
    lo, hi = parts[0][0], parts[-1][1]
    n = hi - lo
    mean, rstd = c.carve((n,), (n,))
    with c.stage() as block:
        @block.scalar
        def _(act):
            for k in range(tiles):
                act.activation(out[:, k, lo:hi], source[:, k, lo:hi], ACT.Square).then_inc(c.act_out, 1)
            act.wait_ge(c.vec_out, 1)
            act.activation(rstd, mean, ACT.Sqrt).then_inc(c.act_done, 1)
            if modulated:
                for k in range(tiles):
                    for i, (a, b, which, shift, _) in enumerate(parts):
                        act.wait_ge(c.turned, k * len(parts) + i + 1)
                        act.activation(into[:, k, a:b], into[:, k, a:b], ACT.Identity, bias=c.mod[:, shift + k, which:which + 1])

        @block.tensor
        def _(pe):
            for k in range(tiles):
                pe.wait_ge(c.act_out, k + 1)
                last = pe.matmul(c.banks[0][:, 0:n], c.constant("ones"), out[:, k, lo:hi], start=k == 0, stop=k == tiles - 1)
            last.then_inc(c.product, 1)

        @block.vector
        def _(dve):
            chain = Chain(dve, c.vec_done)
            if modulated:
                for i, (_, _, which, _, scale) in enumerate(parts):
                    chain(dve.scalar_tensor_tensor(c.modA[:, i, :], c.mod[:, scale:scale + tiles, which], 1.0, gain,
                                                   ALU.add, ALU.mult))
            dve.wait_ge(c.product, 1)
            chain(dve.tensor_scalar(mean, c.banks[0][:, 0:n], 1.0 / spread, EPS, ALU.mult, ALU.add))
            dve.reciprocal(mean, mean).then_inc(c.vec_out, 1)
            dve.wait_ge(c.act_done, 1)
            for k in range(tiles):
                for i, (a, b, *_) in enumerate(parts):
                    scale = c.modA[:, i, k:k + 1] if modulated else gain[:, k:k + 1]
                    dve.scalar_tensor_tensor(into[:, k, a:b], source[:, k, a:b], scale, rstd[:, a - lo:b - lo], ALU.mult,
                                             ALU.mult).then_inc(c.turned, 1)


def head_loads(w_in, columns, turn):
    return [w_in[:, :, bass.ds(turn * CHUNK + col, CHUNK)] for col in columns]


def over_turns(c, turns, columns, w_in, body, following):
    if not c.fetched:
        with c.stage() as block:
            @block.sync
            def _(sp):
                fetch(c, sp, head_loads(w_in, columns, 0))
    had = list(c.ahead_n)

    def wait_loaded(turn):
        return lambda engine, s: engine.wait_ge(c.ahead[s], turn * 16 + 16 * had[s])

    with c.nc.Fori(0, turns - 1) as turn:
        body(turn, wait_loaded(turn),
             lambda sp, wait_free=None: fetch(c, sp, head_loads(w_in, [col + CHUNK for col in columns], turn), wait_free))
    for s in range(len(columns)):
        c.ahead_n[s] = had[s] + turns - 1
    body(turns - 1, wait_loaded(turns - 1), lambda sp, wait_free=None: fetch(c, sp, following, wait_free))


def staggered(c, turns, columns, w_in, projections, core, following):
    if not c.fetched:
        with c.stage() as block:
            @block.sync
            def _(sp):
                fetch(c, sp, head_loads(w_in, columns, 0))
    had = list(c.ahead_n)

    projections(0, None, lambda engine, s: engine.wait_ge(c.ahead[s], 16 * had[s]))
    with c.nc.Fori(0, turns - 1) as turn:
        core(turn, lambda sp: fetch(c, sp, head_loads(w_in, [col + CHUNK for col in columns], turn)))
        projections(turn + 1, turn, lambda engine, s: engine.wait_ge(c.ahead[s], turn * 16 + 16 * (had[s] + 1)))
    for s in range(len(columns)):
        c.ahead_n[s] = had[s] + turns - 1
    core(turns - 1, lambda sp: fetch(c, sp, following))
    projections(None, turns - 1, None)


def mlstm(c, a, layer, w_in, full, following):
    lo = 0 if full else NCTX
    n = T - lo
    gcol, gh, headg, q, k, v, o, bc, A0, A1, E, den, hs, sq = c.carve(
        (2 * 4, 4), (2 * 4,), (2,), (2, T), (2, T), (4, ML_D), (2, T), (4, T), (4, T), (4, T), (2, T), (2, T), (2, T), (2, T))
    *_, gates, b, g, m, out_rows, wg, wg_apart = c.carve(
        (2 * 4, 4), (2 * 4,), (2,), (2, T), (2, T), (4, ML_D), (2, T), (4, T), (4, T), (2, T), (2, T), (2, T), (4, T), (KT, 16),
        (KT, P))
    logf, e = out_rows[:, 0:2], out_rows[:, 2:4]
    H = ML_HEADS

    class Gates:

        @staticmethod
        def sync(sp):
            sp.dma_start(wg, w_in[:, :, COL_GATE:COL_GATE + 16]).then_inc(c.stored, 16)
            sp.wait_ge(c.vec_out, 3)
            sp.wait_ge(c.act_out, 5)
            sp.dma_start(a["rows"], out_rows[0:H]).then_inc(c.stored, 16)
            sp.wait_ge(c.stored, 32)

        @staticmethod
        def products(pe):
            pe.wait_ge(c.drained, 1)
            for k in range(KT):
                last = pe.matmul(c.banks[7][:], wg_apart[:, k, :], c.h[:, k, :], start=k == 0, stop=k == KT - 1)
            last.then_inc(c.turned, 1)

        @staticmethod
        def turn(pe):
            pe.wait_ge(c.vec_out, 1)
            for d in range(2):
                for j in range(4):
                    last = pe.matmul(c.banks[6][:, (4 * d + j) * 4:(4 * d + j + 1) * 4], g[0:H, d, j * P:(j + 1) * P],
                                     c.constant("ident")[0:H, 0:H], start=True, stop=True)
            last.then_inc(c.turned, 1)
            pe.wait_ge(c.vec_out, 3)

        @staticmethod
        def scalar(act):
            act.wait_ge(c.turned, 1)
            for j in range(4):
                act.activation(gates[0:H, j, :], c.banks[7][32 * j:32 * j + H, :], ACT.Identity,
                               bias=c.vector("gate_b", layer, layer + 1)[32 * j:32 * j + H]).then_inc(c.act_out, 1)
            act.wait_ge(c.vec_done, 4)
            act.activation(e[0:H], e[0:H], ACT.Exp).then_inc(c.act_done, 1)
            act.wait_ge(c.act_done, 1)
            act.activation(e[0:H], e[0:H], ACT.Ln, bias=1.0).then_inc(c.act_done, 1)
            act.wait_ge(c.vec_out, 2)
            act.activation(out_rows[0:H, 2:4], m[0:H], ACT.Exp, scale=-1.0).then_inc(c.act_out, 1)

        @staticmethod
        def vector(dve):
            chain = Chain(dve, c.vec_done)
            dve.memset(wg_apart, 0.0).then_inc(c.copied, 1)
            dve.wait_ge(c.copied, 1)
            dve.wait_ge(c.stored, 16)
            apart = wg_apart.rearrange("p k (j x) -> p k j x", j=4)[:, :, :, 0:H]
            dve.tensor_copy(apart, wg.rearrange("p k (j x) -> p k j x", j=4)).then_inc(c.drained, 1)
            dve.wait_ge(c.act_out, 4)
            for d in range(2):
                f = gates[0:H, 2 * d + 1, :]
                chain(dve.tensor_scalar(e[0:H, d], f, -1.0, None, ALU.mult))
                chain(dve.tensor_tensor(e[0:H, d], e[0:H, d], f, ALU.min))
            dve.wait_ge(c.act_done, 2)
            for d in range(2):
                chain(dve.scalar_tensor_tensor(logf[0:H, d], gates[0:H, 2 * d + 1, :], 0.0, e[0:H, d], ALU.min, ALU.subtract))
            ones = c.constant("ones")[0:H, 0:1]
            chain(dve.tensor_tensor_scan(b[0:H, 0], ones.to_broadcast([H, T]), logf[0:H, 0], 0.0, ALU.mult, ALU.add))
            chain(dve.tensor_tensor_scan(b[0:H, 1, NCTX - 1::-1], ones.to_broadcast([H, NCTX]), logf[0:H, 1, NCTX - 1::-1],
                                         0.0, ALU.mult, ALU.add))
            chain(dve.tensor_tensor_scan(b[0:H, 1, T - 1:NCTX - 1:-1], ones.to_broadcast([H, NLAT]),
                                         logf[0:H, 1, T - 1:NCTX - 1:-1], b[0:H, 1, 0:1], ALU.mult, ALU.add))
            for d in range(2):
                chain(dve.tensor_tensor(g[0:H, d], gates[0:H, 2 * d, :], b[0:H, d], ALU.subtract))
            dve.sem_inc(c.vec_out, 1)
            chain(dve.tensor_tensor_scan(m[0:H, 0], g[0:H, 0], g[0:H, 0], 0.0, ALU.max, ALU.max))
            chain(dve.tensor_tensor_scan(m[0:H, 1, NCTX - 1::-1], g[0:H, 1, NCTX - 1::-1], g[0:H, 1, NCTX - 1::-1], 0.0,
                                         ALU.max, ALU.max))
            chain(dve.tensor_tensor_scan(m[0:H, 1, T - 1:NCTX - 1:-1], g[0:H, 1, T - 1:NCTX - 1:-1],
                                         g[0:H, 1, T - 1:NCTX - 1:-1], m[0:H, 1, 0:1], ALU.max, ALU.max))
            chain(dve.tensor_scalar(out_rows[0:H, 0:2], m[0:H], -1.0, None, ALU.mult))
            chain(dve.tensor_tensor(m[0:H], m[0:H], b[0:H], ALU.add))
            dve.sem_inc(c.vec_out, 1)
            dve.wait_ge(c.turned, 2)
            dve.tensor_copy(gcol, c.banks[6][:, 0:32].rearrange("p (x h) -> p x h", h=4)).then_inc(c.vec_out, 1)
            dve.wait_ge(c.vec_out, 3)

    A = (A0, A1)
    runs = [[(j, max(j * P, lo), T) for j in range(4)],
            [(1, lo, T), (0, 0, P), (0, NCTX, T), (3, NCTX, T), (2, NCTX, NCTX + P)]]
    runs = [[r for r in rs if r[1] < r[2] and (full or r[1] >= NCTX)] for rs in runs]
    sources = [(j, max(lo, 0 if j < 2 else NCTX), T) for j in range(4)]

    outputs = ((4, 5, 6), (0, 1, 7))

    def projections(head, ending, wait_loaded):
        with c.stage() as block:
            if head is not None:
                @block.sync
                def _(sp):
                    if ending is None:
                        Gates.sync(sp)
                    else:
                        sp.wait_ge(c.vec_out, 2)
                    sp.dma_start(bc, a["rows"][bass.ds(head, 1)].rearrange("h a t -> (h a) t").partition_broadcast(P)
                                 ).then_inc(c.side_loaded, 16)
                    sp.wait_ge(c.side_loaded, 16)

            @block.tensor
            def _(pe):
                def tokens_last(s, bank, first):
                    wait_loaded(pe, s)
                    for half in range(2):
                        for kk in range(KT):
                            last = pe.matmul(c.banks[bank + half][:, 0:T - first], c.ring[:, s, kk, half * P:(half + 1) * P],
                                             c.h[:, kk, first:T], start=kk == 0, stop=kk == KT - 1)
                        last.then_inc(c.product, 1)

                if head is not None:
                    tokens_last(1, 2, 0)
                if ending is None:
                    Gates.products(pe)
                if ending is not None:
                    for half in range(2):
                        pe.wait_ge(c.act_out, half + 3)
                        last = pe.matmul(c.banks[7][:, 0:n], c.constant("ones"), sq[:, half, lo:T], start=half == 0,
                                         stop=half == 1)
                    last.then_inc(c.pe_out, 1)
                if head is None:
                    return
                tokens_last(0, 0, lo)
                tokens_last(2, 4, lo)
                wait_loaded(pe, 3)
                if ending is not None:
                    pe.wait_ge(c.vec_out, 3)
                else:
                    Gates.turn(pe)
                for j in range(4):
                    for kk in range(KT):
                        last = pe.matmul(c.banks[6 + j // 2][:, (j % 2) * ML_D:(j % 2 + 1) * ML_D],
                                         c.h[:, kk, j * P:(j + 1) * P], c.ring[:, 3, kk, :], start=kk == 0, stop=kk == KT - 1)
                    last.then_inc(c.product, 1)

            @block.vector
            def _(dve):
                if ending is not None:
                    chain = Chain(dve, c.vec_done)
                    for d in range(2):
                        dve.wait_ge(c.act_out, d + 1)
                        chain(dve.tensor_tensor(den[:, d, lo:T], den[:, d, lo:T], bc[:, 2 + d, lo:T], ALU.max))
                        chain(dve.reciprocal(den[:, d, lo:T], den[:, d, lo:T]))
                        out = hs if d == 0 else E
                        for half in range(2):
                            chain.mark(dve.tensor_tensor(out[:, half, lo:T], c.banks[outputs[d][half]][:, 0:n],
                                                         den[:, d, lo:T], ALU.mult))
                    chain.wait()
                    for half in range(2):
                        dve.tensor_tensor(hs[:, half, lo:T], hs[:, half, lo:T], E[:, half, lo:T], ALU.add
                                          ).then_inc(c.vec_out, 1)
                    dve.wait_ge(c.pe_out, 1)
                    chain(dve.tensor_scalar(den[:, 0, lo:T], c.banks[7][:, 0:n], 1.0 / ML_D, EPS, ALU.mult, ALU.add))
                    dve.reciprocal(den[:, 0, lo:T], den[:, 0, lo:T]).then_inc(c.vec_out, 1)
                    dve.wait_ge(c.act_out, 5)
                    flat = c.big[:].rearrange("p k t -> p (k t)")
                    for half in range(2):
                        chain(dve.scalar_tensor_tensor(sq[:, half, lo:T], hs[:, half, lo:T], headg[:, half:half + 1],
                                                       E[:, 0, lo:T], ALU.mult, ALU.mult))
                        dve.tensor_tensor(flat[:, bass.ds(ending * (2 * T) + (half * T + lo), n)], sq[:, half, lo:T],
                                          o[:, half, lo:T], ALU.mult).then_inc(c.vec_out, 1)
                else:
                    Gates.vector(dve)
                if head is None:
                    return
                for half in range(2):
                    dve.wait_ge(c.product, half + 1)
                    dve.tensor_scalar(k[:, half, :], c.banks[2 + half][:], ML_D ** -0.5, None, ALU.mult)
                for half in range(2):
                    dve.wait_ge(c.product, half + 3)
                    dve.tensor_copy(q[:, half, lo:T], c.banks[half][:, 0:n])
                dve.tensor_copy(gh, gcol[:, :, bass.ds(head, 1)].rearrange("p x h -> p (x h)"))
                dve.tensor_copy(headg, c.vector("ml_head_g")[:, bass.ds(head * 2 + layer * KT, 2)])
                for j in range(0, 4, 2):
                    dve.wait_ge(c.product, 8 + j)
                    dve.tensor_copy(v[:, j:j + 2, :], c.banks[6 + j // 2][:].rearrange("p (j e) -> p j e", j=2))

            @block.scalar
            def _(act):
                if ending is not None:
                    for d in range(2):
                        act.activation(den[:, d, lo:T], c.banks[outputs[d][2]][:, 0:n], ACT.Abs).then_inc(c.act_out, 1)
                    for half in range(2):
                        act.wait_ge(c.vec_out, half + 1)
                        act.activation(sq[:, half, lo:T], hs[:, half, lo:T], ACT.Square).then_inc(c.act_out, 1)
                    act.wait_ge(c.vec_out, 3)
                    act.activation(E[:, 0, lo:T], den[:, 0, lo:T], ACT.Sqrt).then_inc(c.act_out, 1)
                else:
                    Gates.scalar(act)
                if head is None:
                    return
                if ending is not None:
                    act.wait_ge(c.vec_out, 5)
                for half in range(2):
                    act.wait_ge(c.product, half + 5)
                    act.activation(o[:, half, lo:T], c.banks[4 + half][:, 0:n], ACT.Sigmoid)

    def core(head, fetch_next):
        with c.stage() as block:
            @block.sync
            def _(sp):
                fetch_next(sp)

            @block.tensor
            def _(pe):
                for j, a0, a1 in sources:
                    for half in range(2):
                        last = pe.matmul(c.banks[j][:, a0 - lo:a1 - lo], k[:, half, j * P:(j + 1) * P], q[:, half, a0:a1],
                                         start=half == 0, stop=half == 1)
                    last.then_inc(c.product, 1)
                for d in range(2):
                    pe.wait_ge(c.vec_out, 4 * (d + 1))
                    for bank, lhs in zip(outputs[d], (0, 1, None)):
                        for i, (j, a0, a1) in enumerate(runs[d]):
                            weights = c.constant("ones") if lhs is None else v[:, j, lhs * P:(lhs + 1) * P]
                            pe.matmul(c.banks[bank][:, a0 - lo:a1 - lo], weights, A[d][:, j, a0:a1], start=i == 0,
                                      stop=i == len(runs[d]) - 1)

            @block.scalar
            def _(act):
                for d in range(2):
                    for i, (j, a0, a1) in enumerate(sources):
                        act.wait_ge(c.vec_done, 4 * d + i + 1)
                        act.activation(A[d][:, j, a0:a1], A[d][:, j, a0:a1], ACT.Exp).then_inc(c.act_out, 1)

            @block.vector
            def _(dve):
                chain = Chain(dve, c.vec_done)
                for d in range(2):
                    for j, a0, a1 in sources:
                        chain.mark(dve.tensor_scalar(A[d][:, j, a0:a1], bc[:, d, a0:a1], gh[:, 4 * d + j:4 * d + j + 1], 0.0,
                                                     ALU.add, ALU.min))
                for d in range(2):
                    mask = c.constant("upper" if d == 0 else "lower")
                    for i, (j, a0, a1) in enumerate(sources):
                        dve.wait_ge(c.act_out, 4 * d + i + 1)
                        dve.wait_ge(c.product, i + 1)
                        chain(dve.tensor_tensor(A[d][:, j, a0:a1], A[d][:, j, a0:a1], c.banks[j][:, a0 - lo:a1 - lo], ALU.mult))
                        diagonal = A[d][:, j, j * P:(j + 1) * P]
                        if j * P >= lo:
                            chain(dve.tensor_tensor(diagonal, diagonal, mask, ALU.mult))
                        dve.sem_inc(c.vec_out, 1)

    staggered(c, ML_HEADS, ML_COLUMNS, w_in, projections, core, following)


def diff_attention(c, a, layer, w_in, full, following):
    lo = 0 if full else NCTX
    n = T - lo
    tiles = [t for t in range(4) if t * P >= lo]
    items = [(half, t) for half in range(2) for t in tiles]
    q, k, v, rot, pr, aw, aT0, aT1, stats, headg, sq, ms, rs = c.carve(
        (2, T), (2, T), (4, 2 * P), (2, NLAT), (4, T), (2, T), (4, T), (4, T), (8, 8), (2,), (2, T), (2, T), (2, T))
    aT = (aT0, aT1)
    keep = 1.0 - (0.8 - 0.6 * math.exp(-0.3 * layer))

    def projections(pair, ending, wait_loaded):
        ended = 0 if ending is None else 2
        with c.stage() as block:
            @block.tensor
            def _(pe):
                def tokens_last(s, first):
                    wait_loaded(pe, s)
                    for half in range(2):
                        for kk in range(KT):
                            last = pe.matmul(c.banks[2 * s + half][:, first:T], c.ring[:, s, kk, half * P:(half + 1) * P],
                                             c.h[:, kk, first:T], start=kk == 0, stop=kk == KT - 1)
                        last.then_inc(c.product, 1)

                if pair is not None:
                    tokens_last(0, lo)
                if ending is not None:
                    for half in range(2):
                        pe.wait_ge(c.act_out, half + 1)
                        pe.matmul(c.banks[4 + half][:, 0:n], c.constant("ones"), sq[:, half, lo:T], start=True,
                                  stop=True).then_inc(c.pe_out, 1)
                if pair is None:
                    return
                tokens_last(1, 0)
                if ending is not None:
                    pe.wait_ge(c.vec_out, 4)
                for i, x in enumerate((q, k)):
                    pe.wait_ge(c.copied, 2 * i + 2)
                    for half in range(2):
                        pe.matmul(c.banks[6 + i][:, half * NLAT:(half + 1) * NLAT], c.constant("turn"), x[:, half, NCTX:T],
                                  start=True, stop=True).then_inc(c.pe_out, 1)
                wait_loaded(pe, 2)
                for j in range(4):
                    for kk in range(KT):
                        last = pe.matmul(c.banks[4 + j // 2][:, (j % 2) * 2 * P:(j % 2 + 1) * 2 * P],
                                         c.h[:, kk, j * P:(j + 1) * P], c.ring[:, 2, kk, :], start=kk == 0, stop=kk == KT - 1)
                    last.then_inc(c.product, 1)

            @block.scalar
            def _(act):
                if ending is not None:
                    for half in range(2):
                        act.activation(sq[:, half, lo:T], c.banks[6 + half][:, 0:n], ACT.Square).then_inc(c.act_out, 1)
                    for half in range(2):
                        act.wait_ge(c.vec_out, half + 1)
                        act.activation(rs[:, half, lo:T], ms[:, half, lo:T], ACT.Sqrt).then_inc(c.act_out, 1)

            @block.vector
            def _(dve):
                chain = Chain(dve, c.vec_done)
                if ending is not None:
                    for half in range(2):
                        dve.wait_ge(c.pe_out, half + 1)
                        chain(dve.tensor_scalar(ms[:, half, lo:T], c.banks[4 + half][:, 0:n], 1.0 / P, EPS, ALU.mult, ALU.add))
                        dve.reciprocal(ms[:, half, lo:T], ms[:, half, lo:T]).then_inc(c.vec_out, 1)
                    flat = c.big[:].rearrange("p k t -> p (k t)")
                    for half in range(2):
                        dve.wait_ge(c.act_out, 3 + half)
                        dve.scalar_tensor_tensor(flat[:, bass.ds(ending * (2 * T) + ((KT + half) * T + lo), n)],
                                                 c.banks[6 + half][:, 0:n], headg[:, half:half + 1], rs[:, half, lo:T],
                                                 ALU.mult, ALU.mult).then_inc(c.vec_out, 1)
                if pair is None:
                    return
                for i, (x, first) in enumerate(((q, lo), (k, 0))):
                    for half in range(2):
                        dve.wait_ge(c.product, 2 * i + half + 1)
                        dve.tensor_copy(x[:, half, first:T], c.banks[2 * i + half][:, first:T]).then_inc(c.copied, 1)
                for i, x in enumerate((q, k)):
                    for half in range(2):
                        dve.wait_ge(c.pe_out, ended + 2 * i + 2)
                        chain(dve.tensor_tensor(rot[:, half], c.banks[6 + i][:, half * NLAT:(half + 1) * NLAT],
                                                c.constant("sin"), ALU.mult))
                        chain(dve.tensor_tensor(x[:, half, NCTX:T], x[:, half, NCTX:T], c.constant("cos"), ALU.mult))
                        chain(dve.tensor_tensor(x[:, half, NCTX:T], x[:, half, NCTX:T], rot[:, half], ALU.add))
                if ending is not None:
                    dve.wait_ge(c.vec_out, 4)
                dve.tensor_scalar(headg, c.vector("da_head_g")[:, bass.ds(pair * 2 + layer * KT, 2)], keep, None, ALU.mult)
                for j in range(0, 4, 2):
                    dve.wait_ge(c.product, 6 + j)
                    dve.tensor_copy(v[:, j:j + 2, :], c.banks[4 + j // 2][:].rearrange("p (j e) -> p j e", j=2))

    def core(pair, fetch_next):
        def keys(i):
            return NCTX if items[i][1] < 2 else T

        with c.stage() as block:
            @block.sync
            def _(sp):
                fetch_next(sp)

            @block.tensor
            def _(pe):
                def turn(i):
                    pe.wait_ge(c.vec_out, i + 1)
                    if i >= 2:
                        pe.wait_ge(c.drained, i - 1)
                    for j in range(keys(i) // P):
                        last = pe.transpose(c.banks[4 + i % 2][:, j * P:(j + 1) * P], aw[:, i % 2, j * P:(j + 1) * P],
                                            c.constant("ident"))
                    last.then_inc(c.turned, 1)

                def output(half):
                    pe.wait_ge(c.drained, len(tiles) * (half + 1))
                    for a0, a1, sources in ([(0, NCTX, 2)] if full else []) + [(NCTX, T, 4)]:
                        for j in range(sources):
                            pe.matmul(c.banks[6 + half][:, a0 - lo:a1 - lo], v[:, j, half * P:(half + 1) * P],
                                      aT[half][:, j, a0:a1], start=j == 0, stop=j == sources - 1)

                for i, (half, t) in enumerate(items):
                    for m in range(2):
                        u = 2 * i + m
                        if u >= 4:
                            pe.wait_ge(c.act_out, u - 3)
                        pe.matmul(c.banks[u % 4][:, 0:keys(i)], q[m * 64:(m + 1) * 64, half, t * P:(t + 1) * P],
                                  k[m * 64:(m + 1) * 64, half, 0:keys(i)], start=True, stop=True).then_inc(c.product, 1)
                    if i >= 2:
                        turn(i - 2)
                    if i - 2 == len(tiles):
                        output(0)
                turn(len(items) - 2)
                if len(items) - 2 == len(tiles):
                    output(0)
                turn(len(items) - 1)
                output(1)

            @block.scalar
            def _(act):
                for i in range(len(items)):
                    for m in range(2):
                        u = 2 * i + m
                        act.wait_ge(c.maxima, u + 1)
                        if i >= 2:
                            act.wait_ge(c.vec_out, i - 1)
                        act.activation(pr[:, u % 4, 0:keys(i)], c.banks[u % 4][:, 0:keys(i)], ACT.Exp,
                                       bias=stats[:, i, m:m + 1], scale=DA_DH ** -0.5,
                                       accum_out=stats[:, i, 2 + m:3 + m]).then_inc(c.act_out, 1)

            @block.vector
            def _(dve):
                chain = Chain(dve, c.vec_done)

                def maxima(i):
                    for m in range(2):
                        dve.wait_ge(c.product, 2 * i + m + 1)
                        chain(dve.reduce_max(stats[:, i, 6 + m:7 + m], c.banks[(2 * i + m) % 4][:, 0:keys(i)], AX.X))
                        dve.tensor_scalar(stats[:, i, m:m + 1], stats[:, i, 6 + m:7 + m], -(DA_DH ** -0.5), None,
                                          ALU.mult).then_inc(c.maxima, 1)

                def combine(i):
                    w = keys(i)
                    dve.wait_ge(c.act_out, 2 * i + 2)
                    chain(dve.reciprocal(stats[:, i, 4:6], stats[:, i, 2:4]))
                    chain(dve.tensor_tensor(stats[:, i, 5:6], stats[:, i, 5:6], c.lam[:, 14 + layer:15 + layer], ALU.mult))
                    p0, p1 = (pr[:, (2 * i + m) % 4, 0:w] for m in range(2))
                    chain(dve.tensor_scalar(p1, p1, stats[:, i, 5:6], None, ALU.mult))
                    if i >= 2:
                        dve.wait_ge(c.turned, i - 1)
                    dve.scalar_tensor_tensor(aw[:, i % 2, 0:w], p0, stats[:, i, 4:5], p1, ALU.mult,
                                             ALU.subtract).then_inc(c.vec_out, 1)

                def spread(i):
                    half, t = items[i]
                    dve.wait_ge(c.turned, i + 1)
                    dve.tensor_copy(aT[half][:, 0:keys(i) // P, t * P:(t + 1) * P],
                                    c.banks[4 + i % 2][:, 0:keys(i)].rearrange("p (j t) -> p j t", t=P)).then_inc(c.drained, 1)

                maxima(0)
                maxima(1)
                for i in range(len(items)):
                    combine(i)
                    if i >= 1:
                        spread(i - 1)
                    if i + 2 < len(items):
                        maxima(i + 2)
                spread(len(items) - 1)

    staggered(c, DA_HEADS // 2, DA_COLUMNS, w_in, projections, core, following)


def fourier(c, w_in, full, following):
    lo = 0 if full else NCTX
    z, ab = c.carve((2, T), (4, 2 * FN_C))
    dft = c.constant("dft").rearrange("p (k n) -> p k n", k=2)
    tiles = [t for t in range(4) if t * P >= lo]

    def one_group(group, wait_loaded, fetch_next):
        with c.stage() as block:
            @block.sync
            def _(sp):
                fetch_next(sp, lambda s: sp.wait_ge(c.product, 2) if s == 0 else None)

            @block.tensor
            def _(pe):
                wait_loaded(pe, 0)
                for half in range(2):
                    for k in range(KT):
                        last = pe.matmul(c.banks[half][:, lo:T], c.ring[:, 0, k, half * P:(half + 1) * P], c.h[:, k, lo:T],
                                         start=k == 0, stop=k == KT - 1)
                    last.then_inc(c.product, 1)
                pe.wait_ge(c.vec_done, 2)
                for i, t in enumerate(tiles):
                    for k in range(2):
                        last = pe.matmul(c.banks[2 + i][:], z[:, k, t * P:(t + 1) * P], dft[:, k, 0:2 * FN_C], start=k == 0,
                                         stop=k == 1)
                    last.then_inc(c.product, 1)
                pe.wait_ge(c.vec_done, 2 + len(tiles))
                for half in range(2):
                    for stream in range(lo // NCTX, 2):
                        for i in range(4):
                            j, part = i // 2, i % 2
                            last = pe.matmul(c.banks[6 + half][:, stream * NCTX:(stream + 1) * NCTX],
                                             ab[:, 2 * stream + j, part * FN_C + half * P:part * FN_C + (half + 1) * P],
                                             dft[:, j, part * 2 * FN_C:part * 2 * FN_C + FN_C], start=i == 0, stop=i == 3)
                    last.then_inc(c.product, 1)

            @block.vector
            def _(dve):
                chain = Chain(dve, c.vec_done)
                for half in range(2):
                    dve.wait_ge(c.product, half + 1)
                    chain.mark(dve.tensor_copy(z[:, half, lo:T], c.banks[half][:, lo:T]))
                for i, t in enumerate(tiles):
                    dve.wait_ge(c.product, 3 + i)
                    chain.mark(dve.tensor_copy(ab[:, t, :], c.banks[2 + i][:]))
                flat = c.big[:].rearrange("p k t -> p (k t)")
                for half in range(2):
                    dve.wait_ge(c.product, 3 + len(tiles) + half)
                    dve.tensor_copy(flat[:, bass.ds(group * (2 * T) + ((2 * KT + half) * T + lo), T - lo)],
                                    c.banks[6 + half][:, lo:T])

    over_turns(c, FN_GROUPS, FN_COLUMNS, w_in, one_group, following)


def merge(c, a, layer, w_in, full, following):
    lo = 0 if full else NCTX
    n = T - lo
    gate, = c.carve((KT, T))
    names = ("w_br_ml", "w_br_da", "w_br_fn")
    for i, name in enumerate(names):
        branch = rows(a[name][layer])
        project(c, w_in, COL_MERGE + i * D, D // CHUNK, moving(c.h, lo, T), n,
                lambda e, bank, tile: e.activation(gate[:, tile, lo:T], bank, ACT.Sigmoid), on="scalar",
                following=first_loads(branch, 0, D // CHUNK))

        def gated(e, bank, tile):
            out = c.mg[:, tile, lo:T]
            if i == 0:
                return e.tensor_tensor(out, bank, gate[:, tile, lo:T], ALU.mult)
            return e.tensor_tensor(gate[:, tile, lo:T], bank, gate[:, tile, lo:T], ALU.mult)

        after = first_loads(w_in, COL_MERGE + (i + 1) * D, D // CHUNK) if i + 1 < len(names) else following
        project(c, branch, 0, D // CHUNK, moving(c.big[:, i * KT:(i + 1) * KT, :], lo, T), n, gated, following=after)
        if i:
            with c.stage() as block:
                @block.vector
                def _(dve):
                    for k in range(KT):
                        dve.tensor_tensor(c.mg[:, k, lo:T], c.mg[:, k, lo:T], gate[:, k, lo:T], ALU.add)


def add_gated(c, weight, rhs, parts, gate_tile, splits=((0, KT),), following=None):
    lo = parts[0][0]

    def evacuate(e, bank, tile):
        for first, last, which in parts:
            out = c.x[:, tile, first:last]
            ins = e.scalar_tensor_tensor(out, bank[:, first - lo:last - lo], c.mod[:, gate_tile + tile, which:which + 1], out,
                                         ALU.mult, ALU.add)
        return ins

    project(c, weight, 0, D // CHUNK, rhs, T - lo, evacuate, splits=splits, following=following)


def feed_forward(c, a, layer, parts, following):
    lo = parts[0][0]
    n = T - lo
    flat = c.big[:].rearrange("p k t -> p (k t)")
    w, w_out = rows(a["w_ffn_in"][layer]), rows(a["w_ffn_out"][layer])
    ks = D_FF // P
    splits = tuple((k0, min(KT, ks - k0)) for k0 in range(0, ks, KT))
    project(c, w, 0, D_FF // CHUNK, moving(c.h, lo, T), n,
            lambda e, bank, tile: e.activation(flat[:, bass.ds(tile * T + lo, n)], bank, ACT.Silu), on="scalar",
            following=first_loads(w, D_FF, D_FF // CHUNK))
    project(c, w, D_FF, D_FF // CHUNK, moving(c.h, lo, T), n,
            lambda e, bank, tile: e.tensor_tensor(flat[:, bass.ds(tile * T + lo, n)], bank,
                                                  flat[:, bass.ds(tile * T + lo, n)], ALU.mult),
            following=first_loads(w_out, 0, D // CHUNK, splits))
    add_gated(c, w_out, moving(c.big[:, 0:ks, :], lo, T), parts, 5 * KT, splits=splits, following=following)


def first_block(c, a):
    for layer in range(DEPTH):
        full = layer < DEPTH - 1
        streams = [(0, NCTX, 0), (NCTX, T, 1)]
        kept = streams if full else streams[1:]
        w_in = rows(a["w_in"][layer])
        conditions = c.cond[:, 0:2, :].rearrange("p a k -> p k a")
        adaln(c, rows(a["w_ada"][layer]), conditions, c.vector("b_ada", 48 * layer, 48 * (layer + 1)), 2,
              head_loads(w_in, ML_COLUMNS, 0))
        gains = [c.vector("norm_g", (2 * layer + i) * KT, (2 * layer + i + 1) * KT) for i in range(2)]
        norm(c, c.x, c.h, gains[0], [(f, l, w, 0, KT) for f, l, w in streams])
        mlstm(c, a, layer, w_in, full, head_loads(w_in, DA_COLUMNS, 0))
        diff_attention(c, a, layer, w_in, full, head_loads(w_in, FN_COLUMNS, 0))
        fourier(c, w_in, full, first_loads(w_in, COL_MERGE, D // CHUNK))
        w_out = rows(a["w_out"][layer])
        merge(c, a, layer, w_in, full, first_loads(w_out, 0, D // CHUNK))
        add_gated(c, w_out, moving(c.mg, kept[0][0], T), kept, 2 * KT,
                  following=first_loads(rows(a["w_ffn_in"][layer]), 0, D_FF // CHUNK))
        norm(c, c.x, c.h, gains[1], [(f, l, w, 3 * KT, 4 * KT) for f, l, w in kept])
        next_ada = rows(a["w_ada"][layer + 1]) if full else rows(a["ada_w_2"][0])
        feed_forward(c, a, layer, kept, first_loads(next_ada, 0, 6 * D // CHUNK))
    norm(c, c.x, c.h, c.vector("final_g"), [(NCTX, T, 1, 0, 0)], modulated=False, into=c.x)


def hgrn_blocks(c, a):
    w_in = rows(a["w_in_2"][0])
    hs = moving(c.h, NCTX, T)
    H, B, L = HG_HEADS, HG_BLOCKS, HG_SUB
    N = H * NLAT
    big = c.big[:].rearrange("p k t -> p (k t)")
    q, f, g, u, kk, lf, bl, e1, qe, kend, sq, rs = (big[:, i * N:(i + 1) * N] for i in range(12))
    vt, v16, at, pairs, state = c.carve((2, HG_W), (B, HG_W), (N,), (2, N), (2, HG_W))
    lb = c.hg_bounds[:]
    kt = c.ring[:].rearrange("p s k n -> p (s k n)")
    per_tile = NLAT
    parts = ((q, 0, ACT.Silu), (g, 3 * HG_W, ACT.Silu), (f, HG_W, ACT.Sigmoid), (u, 4 * HG_W, ACT.Copy))
    for i, (buffer, col, func) in enumerate(parts):
        project(c, w_in, col, HG_W // CHUNK, hs, NLAT,
                lambda e, bank, tile: e.activation(buffer[:, tile * per_tile:(tile + 1) * per_tile], bank, func), on="scalar",
                following=first_loads(w_in, parts[i + 1][1] if i + 1 < len(parts) else 2 * HG_W, HG_W // CHUNK))

    c.fetched = False
    with c.stage() as block:
        @block.sync
        def _(sp):
            sp.wait_ge(c.vec_out, 2)
            for b in range(B):
                sp.dma_start(v16[0:L, b, :], vt[(b % 8) * L:(b % 8 + 1) * L, b // 8, :]).then_inc(c.stored, 16)
            sp.wait_ge(c.stored, 16 * B)

        @block.tensor
        def _(pe):
            for s in range(2):
                pe.wait_ge(c.ahead[s], 16 * c.ahead_n[s])
                for t in range(2):
                    for k in range(KT):
                        last = pe.matmul(c.banks[t][:, s * CHUNK:(s + 1) * CHUNK], hs[:, k, t * P:(t + 1) * P],
                                         c.ring[:, s, k, :], start=k == 0, stop=k == KT - 1)
            last.then_inc(c.product, 1)

        @block.vector
        def _(dve):
            dve.wait_ge(c.product, 1)
            for t in range(2):
                dve.tensor_copy(vt[:, t, :], c.banks[t][:]).then_inc(c.vec_out, 1)

    def blocks(x):
        return x.rearrange("p (b l) -> p b l", l=L)

    with c.stage() as block:
        @block.scalar
        def _(act):
            act.wait_ge(c.vec_out, 1)
            act.activation(lb[:, 1:3, :], lb[:, 1:3, :], ACT.Exp).then_inc(c.act_out, 1)
            act.wait_ge(c.vec_out, 2)
            act.activation(lf, f, ACT.Ln).then_inc(c.act_out, 1)
            act.wait_ge(c.vec_out, 3)
            act.activation(e1, bl, ACT.Exp).then_inc(c.act_out, 1)
            act.wait_ge(c.vec_out, 4)
            act.activation(kend, kend, ACT.Exp).then_inc(c.act_out, 1)

        @block.vector
        def _(dve):
            chain = Chain(dve, c.vec_done)
            b0, b1 = c.vector("bounds", 0, 4), c.vector("bounds", 4, 8)
            chain(dve.tensor_tensor(lb[:, 0, :], b0, b1, ALU.max))
            chain(dve.tensor_tensor(lb[:, 1, :], b0, lb[:, 0, :], ALU.subtract))
            chain(dve.tensor_tensor(lb[:, 2, :], b1, lb[:, 0, :], ALU.subtract))
            dve.sem_inc(c.vec_out, 1)
            dve.wait_ge(c.act_out, 1)
            chain(dve.tensor_tensor(lb[:, 3, :], lb[:, 1, :], lb[:, 2, :], ALU.add))
            chain(dve.reciprocal(lb[:, 3, :], lb[:, 3, :]))
            chain(dve.tensor_tensor(lb[:, 4, :], lb[:, 1, :], lb[:, 3, :], ALU.mult))
            chain(dve.tensor_scalar(lb[:, 5, :], lb[:, 4, :], -1.0, 1.0, ALU.mult, ALU.add))
            for h in range(H):
                part = f[:, h * NLAT:(h + 1) * NLAT]
                chain(dve.tensor_scalar(part, part, lb[:, 5, h:h + 1], lb[:, 4, h:h + 1], ALU.mult, ALU.add))
            dve.sem_inc(c.vec_out, 1)
            dve.tensor_scalar(kk, f, -1.0, 1.0, ALU.mult, ALU.add)
            chain(dve.tensor_scalar(q, q, P ** -0.5, None, ALU.mult))
            dve.wait_ge(c.act_out, 2)
            chain(dve.tensor_tensor_scan(bl, c.constant("inner"), lf, 0.0, ALU.mult, ALU.add))
            dve.sem_inc(c.vec_out, 1)
            chain(dve.tensor_tensor(blocks(kend), blocks(bl)[:, :, L - 1:L].to_broadcast([P, H * B, L]), blocks(bl),
                                    ALU.subtract))
            dve.sem_inc(c.vec_out, 1)
            dve.wait_ge(c.act_out, 3)
            dve.tensor_tensor(qe, q, e1, ALU.mult)
            dve.wait_ge(c.act_out, 4)
            dve.tensor_tensor(kend, kend, kk, ALU.mult)

    with c.stage() as block:
        pick = c.constant("pick").rearrange("p (j l) -> p j l", l=L)
        buffers = (pairs[:, 0], pairs[:, 1], sq, rs)
        R = len(buffers)

        @block.vector
        def _(dve):
            chain = Chain(dve, c.vec_done)

            def first(j):
                w = L - j
                part = blocks(buffers[j % R])[:, :, 0:w]
                if j >= R:
                    dve.wait_ge(c.product, j - R + 1)
                dve.tensor_tensor(part, blocks(bl)[:, :, j:L], blocks(bl)[:, :, j:j + 1].to_broadcast([P, H * B, w]),
                                  ALU.subtract).then_inc(c.vec_out, 1)

            first(0)
            first(1)
            for j in range(L):
                w = L - j
                part = blocks(buffers[j % R])[:, :, 0:w]
                if j + 2 < L:
                    first(j + 2)
                dve.wait_ge(c.act_out, j + 1)
                chain(dve.tensor_tensor(part, part, blocks(q)[:, :, j:L], ALU.mult))
                chain(dve.tensor_tensor(part, part, blocks(kk)[:, :, j:j + 1].to_broadcast([P, H * B, w]), ALU.mult))
            dve.wait_ge(c.product, L)
            for half in range(2):
                dve.tensor_copy(at[0:L, half * 512:(half + 1) * 512], c.banks[half][0:L, :])

        @block.scalar
        def _(act):
            for j in range(L):
                part = blocks(buffers[j % R])[:, :, 0:L - j]
                act.wait_ge(c.vec_out, j + 1)
                act.activation(part, part, ACT.Exp).then_inc(c.act_out, 1)
            for r in range(H * B // 4):
                act.wait_ge(c.turned, r + 1)
                act.activation(kt[0:L, r * 512:(r + 1) * 512], c.banks[2 + r % 6][0:L, :], ACT.Copy).then_inc(c.drained, 1)

        @block.tensor
        def _(pe):
            for j in range(L):
                pe.wait_ge(c.vec_done, 2 * j + 2)
                for half in range(2):
                    last = pe.matmul(blocks(c.banks[half][0:L, :])[:, :, j:L], pick[:, j, :],
                                     blocks(buffers[j % R])[:, half * 32:(half + 1) * 32, 0:L - j],
                                     start=j == 0, stop=j == L - 1)
                last.then_inc(c.product, 1)
            for r in range(H * B // 4):
                if r >= 6:
                    pe.wait_ge(c.drained, r - 5)
                for i in range(4):
                    last = pe.transpose(c.banks[2 + r % 6][0:L, i * P:(i + 1) * P], blocks(kend)[:, 4 * r + i, :],
                                        c.constant("ident"))
                last.then_inc(c.turned, 1)


class S5Tables:

    def __init__(self, c):
        self.c = c
        spare = c.work[:, 15360 - 8 * NLAT:].rearrange("p (i t) -> p i t", i=8)
        self.table = ((c.x[:, :, 0:NLAT], c.h[:, :, 0:NLAT]), (c.mg[:, :, NLAT:T], spare))
        self.kept = c.s5_kept
        self.s = c.work[:, 8192:8192 + 16 * S5_TILES].rearrange("p (a i) -> p a i", i=S5_TILES)
        self.turn = c.work[:, 9216:9216 + 2 * S5_TILES].rearrange("p (a i) -> p a i", i=S5_TILES)
        at = 9728
        self.scratch = [c.work[:, at + i * (4 * NLAT):at + (i + 1) * (4 * NLAT)] for i in range(2)]

    MAGIC = 1.5 * 2.0 ** 23

    def reduce(self, dve, chain, out, n, x, step, parts):
        chain(dve.tensor_scalar(n, x, 1.0 / step, self.MAGIC, ALU.mult, ALU.add))
        chain(dve.tensor_scalar(n, n, self.MAGIC, None, ALU.subtract))
        for part in parts:
            chain(dve.scalar_tensor_tensor(out, n, -part, x, ALU.mult, ALU.add))
            x = out

    def series(self, dve, chain, out, x, coefficients):
        *rest, last = coefficients
        chain(dve.tensor_scalar(out, x, last, None, ALU.mult))
        for coefficient in reversed(rest):
            chain(dve.scalar_tensor_tensor(out, out, coefficient, x, ALU.add, ALU.mult))

    def exponential(self, dve, chain, out, x, r, n, scratch):
        ln2 = math.log(2.0)
        hi = 0.693359375
        chain(dve.tensor_scalar(scratch, x, -87.0, 88.0, ALU.max, ALU.min))
        self.reduce(dve, chain, r, n, scratch, ln2, (hi, ln2 - hi))
        self.series(dve, chain, out, r, [1.0 / math.factorial(i) for i in range(1, 9)])
        chain(dve.tensor_scalar(n, n, 127.0, 2.0 ** 23, ALU.add, ALU.mult))
        chain(dve.tensor_copy(scratch.bitcast(I32), n))
        chain(dve.scalar_tensor_tensor(out, out, 1.0, scratch, ALU.add, ALU.mult))

    def vector(self, dve):
        c, s, kept, turn = self.c, self.s, self.kept, self.turn
        chain = Chain(dve, c.vec_done)
        are, aim = c.vector("s5_are"), c.vector("s5_aim")
        for half in range(2):
            dve.memset(self.table[0][half][:, :, 0:1], 1.0)
            chain(dve.memset(self.table[1][half][:, :, 0:1], 0.0))
        self.exponential(dve, chain, s[:, 0], c.vector("s5_dt"), s[:, 8], s[:, 9], s[:, 10])
        chain(dve.tensor_tensor(s[:, 1], are, s[:, 0], ALU.mult))
        self.exponential(dve, chain, kept[:, 0], s[:, 1], s[:, 8], s[:, 9], s[:, 10])
        chain(dve.tensor_tensor(s[:, 3], aim, s[:, 0], ALU.mult))
        hi = 1.5703125
        mid = float(np.float32(math.pi / 2 - hi))
        self.reduce(dve, chain, s[:, 4], s[:, 8], s[:, 3], math.pi / 2, (hi, mid, math.pi / 2 - hi - mid))
        chain(dve.tensor_tensor(s[:, 5], s[:, 4], s[:, 4], ALU.mult))
        self.series(dve, chain, s[:, 9], s[:, 5], [(-1.0) ** i / math.factorial(2 * i + 1) for i in range(1, 6)])
        chain(dve.scalar_tensor_tensor(s[:, 9], s[:, 9], 1.0, s[:, 4], ALU.add, ALU.mult))
        self.series(dve, chain, s[:, 10], s[:, 5], [(-1.0) ** i / math.factorial(2 * i) for i in range(1, 7)])
        chain(dve.tensor_scalar(s[:, 10], s[:, 10], 1.0, None, ALU.add))
        self.reduce(dve, chain, s[:, 11], s[:, 12], s[:, 8], 4.0, (4.0,))
        chain(dve.tensor_scalar(s[:, 12], s[:, 11], -1.0, None, ALU.mult))
        chain(dve.tensor_tensor(s[:, 12], s[:, 12], s[:, 11], ALU.max))
        chain(dve.tensor_scalar(s[:, 13], s[:, 12], -1.0, 1.0, ALU.mult, ALU.add))
        chain(dve.scalar_tensor_tensor(s[:, 14], s[:, 12], -2.0, s[:, 11], ALU.add, ALU.mult))
        for out, first, second, op in ((7, (10, 13), (9, 14), ALU.add), (6, (9, 13), (10, 14), ALU.subtract)):
            chain(dve.tensor_tensor(s[:, 11], s[:, first[0]], s[:, first[1]], ALU.mult))
            chain(dve.tensor_tensor(s[:, 12], s[:, second[0]], s[:, second[1]], ALU.mult))
            chain(dve.tensor_tensor(s[:, out], s[:, 11], s[:, 12], op))
        chain(dve.tensor_tensor(s[:, 9], kept[:, 0], s[:, 7], ALU.mult))
        chain(dve.tensor_tensor(s[:, 2], kept[:, 0], s[:, 6], ALU.mult))
        chain(dve.tensor_scalar(s[:, 9], s[:, 9], -1.0, None, ALU.add))
        chain(dve.tensor_tensor(s[:, 10], are, are, ALU.mult))
        chain(dve.tensor_tensor(s[:, 11], aim, aim, ALU.mult))
        chain(dve.tensor_tensor(s[:, 10], s[:, 10], s[:, 11], ALU.add))
        chain(dve.reciprocal(s[:, 10], s[:, 10]))
        for out, first, second, op in ((1, (s[:, 9], are), (s[:, 2], aim), ALU.add),
                                       (2, (s[:, 2], are), (s[:, 9], aim), ALU.subtract)):
            chain(dve.tensor_tensor(s[:, 11], *first, ALU.mult))
            chain(dve.tensor_tensor(s[:, 12], *second, ALU.mult))
            chain(dve.tensor_tensor(s[:, 11], s[:, 11], s[:, 12], op))
            chain(dve.tensor_tensor(kept[:, out], s[:, 11], s[:, 10], ALU.mult))
        dve.tensor_copy(turn[:, 0], s[:, 7])
        chain(dve.tensor_copy(turn[:, 1], s[:, 6]))
        for k in range(S5_STEPS):
            w = 1 << k
            for half in range(2):
                cos, sin = self.table[0][half], self.table[1][half]
                re, im = (turn[:, r, 8 * half:8 * half + 8].unsqueeze(2).to_broadcast([P, 8, w]) for r in range(2))
                s0, s1 = (x[:, 0:8 * w].rearrange("p (i t) -> p i t", i=8) for x in self.scratch)
                chain.mark(dve.tensor_tensor(s0, cos[:, :, 0:w], re, ALU.mult))
                chain(dve.tensor_tensor(s1, sin[:, :, 0:w], im, ALU.mult))
                chain(dve.tensor_tensor(cos[:, :, w:2 * w], s0, s1, ALU.subtract))
                chain.mark(dve.tensor_tensor(s0, cos[:, :, 0:w], im, ALU.mult))
                chain(dve.tensor_tensor(s1, sin[:, :, 0:w], re, ALU.mult))
                chain(dve.tensor_tensor(sin[:, :, w:2 * w], s0, s1, ALU.add))
            if k + 1 < S5_STEPS:
                chain.mark(dve.tensor_tensor(s[:, 11], turn[:, 0], turn[:, 0], ALU.mult))
                chain.mark(dve.tensor_tensor(s[:, 12], turn[:, 1], turn[:, 1], ALU.mult))
                chain(dve.tensor_tensor(s[:, 13], turn[:, 0], turn[:, 1], ALU.mult))
                chain.mark(dve.tensor_tensor(turn[:, 0], s[:, 11], s[:, 12], ALU.subtract))
                chain(dve.tensor_scalar(turn[:, 1], s[:, 13], 2.0, None, ALU.mult))


def recurrences(c, a, tables, following):
    H, B, L, N = HG_HEADS, HG_BLOCKS, HG_SUB, S5_TILES
    assert B == N
    W = H * NLAT
    big = c.big[:].rearrange("p k t -> p (k t)")
    g, u, e1, qe, sq, rs = (big[:, i * W:(i + 1) * W] for i in (2, 3, 7, 8, 10, 11))
    _, v16, at, pairs, state = c.carve((2, HG_W), (B, HG_W), (W,), (2, W), (2, HG_W))
    kt = c.ring[:].rearrange("p s k n -> p (s k n)")
    R = 4
    x = big[:, 0:2 * W].rearrange("p (i r t) -> p i r t", i=R, r=2)
    a0, a1, b0, b1, re, im = (big[:, 4 * W + i * NLAT:4 * W + (i + 1) * NLAT] for i in range(6))
    wb = big[:, 6 * W:7 * W].rearrange("p (r i n) -> p r i n", r=2, i=4)
    wc = big[:, 9 * W:10 * W].rearrange("p (r i n) -> p r i n", r=2, i=N)
    ws, scratch = (pairs[:, i].rearrange("p (r i n) -> p r i n", r=2, i=N) for i in range(2))
    u = u.rearrange("p (i t) -> p i t", i=4)
    y = big[:, 4 * W:5 * W].rearrange("p (i t) -> p i t", i=4)
    gate = big[:, 5 * W:6 * W].rearrange("p (i t) -> p i t", i=4)
    glu = rows(a["s5_glu_w_2"][0])
    ks = HG_W // P

    with c.stage() as block:
        @block.sync
        def _(sp):
            sp.dma_start(wb, a["s5_b"].rearrange("r p i n -> p r i n")).then_inc(c.side_loaded, 16)
            sp.dma_start(wc, a["s5_c"].rearrange("r p i n -> p r i n")).then_inc(c.stored, 16)
            fetch(c, sp, first_loads(glu, 0, HG_W // CHUNK, ((0, ks),)), lambda s: sp.wait_ge(c.product, B))

        @block.tensor
        def _(pe):
            def inputs(i):
                part = slice(32 * (i % 4), 32 * (i % 4) + 32)
                if i >= 2:
                    pe.wait_ge(c.drained, i - 1)
                for r in range(2):
                    last = pe.matmul(c.banks[6 + i % 2][:, r * NLAT:(r + 1) * NLAT], wb[part, r, i // 4, :],
                                     u[part, i // 4, :], start=True, stop=True)
                last.then_inc(c.turned, 1)

            def outputs(i):
                pe.wait_ge(c.vec_out, i + 1)
                half = (i // 4) % 2
                out = c.banks[4 + i // 8][32 * (i % 4):32 * (i % 4) + 32, half * NLAT:(half + 1) * NLAT]
                pe.matmul(out, ws[:, 0, i, :], x[:, i % R, 0, :], start=True, stop=False)
                pe.matmul(out, ws[:, 1, i, :], x[:, i % R, 1, :], start=False, stop=True).then_inc(c.pe_out, 1)

            for b in range(B):
                if b:
                    pe.wait_ge(c.copied, b)
                for h in range(H):
                    out = c.banks[h // 2][:, (h % 2) * NLAT + b * L:(h % 2) * NLAT + (b + 1) * L]
                    pe.matmul(out, v16[0:L, b, h * P:(h + 1) * P], at[0:L, h * NLAT + b * L:h * NLAT + (b + 1) * L],
                              start=True, stop=b == 0)
                    if b:
                        pe.matmul(out, state[:, b % 2, h * P:(h + 1) * P], qe[:, h * NLAT + b * L:h * NLAT + (b + 1) * L],
                                  start=False, stop=True)
                for h in range(H):
                    last = pe.matmul(c.banks[2 + b % 2][:, h * P:(h + 1) * P], kt[0:L, (h * B + b) * P:(h * B + b + 1) * P],
                                     v16[0:L, b, h * P:(h + 1) * P], start=True, stop=True)
                last.then_inc(c.product, 1)
                if b == 0:
                    pe.wait_ge(c.side_loaded, 16)
                    inputs(0)
                if b + 1 < N:
                    inputs(b + 1)
                if b:
                    outputs(b - 1)
            outputs(N - 1)
            for half in range(2):
                pe.wait_ge(c.act_out, half + 1)
                pe.matmul(c.banks[2 + half][:], c.constant("ones"), sq[:, half * 512:(half + 1) * 512], start=True,
                          stop=True).then_inc(c.pe_out, 1)

        @block.vector
        def _(dve):
            chain = Chain(dve, c.vec_done)
            decay = e1.rearrange("p (h b l) -> p h b l", h=H, l=L)
            kr, ki = (tables.kept[:, r].unsqueeze(2).to_broadcast([P, N, 2 * S5_H]) for r in (1, 2))
            dve.wait_ge(c.stored, 16)
            chain.mark(dve.tensor_tensor(scratch[:, 0], wc[:, 0], kr, ALU.mult))
            chain(dve.tensor_tensor(scratch[:, 1], wc[:, 1], ki, ALU.mult))
            chain(dve.tensor_tensor(ws[:, 0], scratch[:, 0], scratch[:, 1], ALU.subtract))
            chain.mark(dve.tensor_tensor(scratch[:, 0], wc[:, 0], ki, ALU.mult))
            chain(dve.tensor_tensor(scratch[:, 1], wc[:, 1], kr, ALU.mult))
            chain(dve.scalar_tensor_tensor(ws[:, 1], scratch[:, 0], -1.0, scratch[:, 1], ALU.mult, ALU.subtract))

            def carry(b):
                after, before = state[:, (b + 1) % 2], state[:, b % 2]
                if b == 0:
                    dve.wait_ge(c.product, 1)
                    dve.tensor_copy(after, c.banks[2][:]).then_inc(c.copied, 1)
                    return
                dve.wait_ge(c.copied, b)
                chain.mark(dve.tensor_tensor(after.rearrange("p (h v) -> p h v", h=H),
                                             before.rearrange("p (h v) -> p h v", h=H),
                                             decay[:, :, b, L - 1:L].to_broadcast([P, H, P]), ALU.mult))
                dve.wait_ge(c.product, b + 1)
                chain.wait()
                dve.tensor_tensor(after, after, c.banks[2 + b % 2][:], ALU.add).then_inc(c.copied, 1)

            def states(i):
                cos, sin = (tables.table[r][i // 8][:, i % 8, :] for r in range(2))
                br, bi = (c.banks[6 + i % 2][:, r * NLAT:(r + 1) * NLAT] for r in range(2))
                xr, xi = x[:, i % R, 0, :], x[:, i % R, 1, :]
                modulus = tables.kept[:, 0, i:i + 1].to_broadcast([P, NLAT])
                dve.wait_ge(c.turned, i + 1)
                chain.mark(dve.tensor_tensor(a0, br, cos, ALU.mult))
                first = chain.mark(dve.tensor_tensor(a1, bi, sin, ALU.mult))
                chain.mark(dve.tensor_tensor(b0, bi, cos, ALU.mult))
                dve.tensor_tensor(b1, br, sin, ALU.mult).then_inc(c.drained, 1)
                chain.wait(first)
                first = chain.mark(dve.tensor_tensor(re, a0, a1, ALU.add))
                dve.wait_ge(c.drained, i + 1)
                second = chain.mark(dve.tensor_tensor(im, b0, b1, ALU.subtract))
                chain.wait(first)
                first = chain.mark(dve.tensor_tensor_scan(re, modulus, re, 0.0, ALU.mult, ALU.add))
                chain.wait(second)
                second = chain.mark(dve.tensor_tensor_scan(im, modulus, im, 0.0, ALU.mult, ALU.add))
                chain.wait(first)
                chain.mark(dve.tensor_tensor(a0, re, cos, ALU.mult))
                chain.mark(dve.tensor_tensor(b1, re, sin, ALU.mult))
                chain.wait(second)
                first = chain.mark(dve.tensor_tensor(a1, im, sin, ALU.mult))
                second = chain.mark(dve.tensor_tensor(b0, im, cos, ALU.mult))
                chain.wait(first)
                if i >= R:
                    dve.wait_ge(c.pe_out, i - R + 1)
                chain.mark(dve.tensor_tensor(xr, a0, a1, ALU.subtract))
                chain.wait()
                dve.tensor_tensor(xi, b0, b1, ALU.add).then_inc(c.vec_out, 1)

            for b in range(B):
                carry(b)
                states(b)
            for half in range(2):
                part = slice(half * 512, (half + 1) * 512)
                dve.wait_ge(c.pe_out, N + half + 1)
                chain(dve.tensor_scalar(rs[:, part], c.banks[2 + half][:], 1.0 / P, EPS, ALU.mult, ALU.add))
                dve.reciprocal(rs[:, part], rs[:, part]).then_inc(c.vec_out, 1)
            for half in range(2):
                part = slice(half * 512, (half + 1) * 512)
                dve.wait_ge(c.act_out, 3 + half)
                chain(dve.scalar_tensor_tensor(sq[:, part], c.banks[half][:], c.vector("gnorm"), rs[:, part], ALU.mult,
                                               ALU.mult))
                dve.tensor_tensor(c.mg[:, 2 * half:2 * half + 2, 0:NLAT],
                                  sq[:, part].rearrange("p (h t) -> p h t", h=2),
                                  g[:, part].rearrange("p (h t) -> p h t", h=2), ALU.mult)
            dve.wait_ge(c.vec_out, N + 2)
            for i in range(4):
                dve.scalar_tensor_tensor(y[:, i], u[:, i], c.vector("s5_d", i, i + 1),
                                         c.banks[4 + i // 2][:, (i % 2) * NLAT:(i % 2 + 1) * NLAT], ALU.mult,
                                         ALU.add).then_inc(c.vec_out, 1)

        @block.scalar
        def _(act):
            act.wait_ge(c.product, B)
            for half in range(2):
                act.activation(sq[:, half * 512:(half + 1) * 512], c.banks[half][:], ACT.Square).then_inc(c.act_out, 1)
            for half in range(2):
                act.wait_ge(c.vec_out, N + half + 1)
                part = rs[:, half * 512:(half + 1) * 512]
                act.activation(part, part, ACT.Sqrt).then_inc(c.act_out, 1)
            for i in range(4):
                act.wait_ge(c.vec_out, N + 2 + i + 1)
                act.activation(y[:, i], y[:, i], ACT.Gelu)

    project(c, glu, 0, HG_W // CHUNK, y, NLAT,
            lambda e, bank, tile: e.activation(gate[:, tile], bank, ACT.Sigmoid, bias=c.vector("glu_b", tile, tile + 1)),
            on="scalar", splits=((0, ks),), following=following)
    with c.stage() as block:
        @block.vector
        def _(dve):
            dve.tensor_tensor(c.mg[:, ks:2 * ks, 0:NLAT], y, gate, ALU.mult)


def peer(c, a):
    H, K, S = PEER_H, PEER_K, PEER_SLOTS
    LOWEST = -3.0e38
    big = c.big[:].rearrange("p k t -> p (k t)")
    qh = big[:, 0:16 * NLAT].rearrange("p (i t) -> p i t", i=16)
    scores = big[:, 16 * NLAT:32 * NLAT]
    tokens = big[:, 32 * NLAT:32 * NLAT + 2 * D].rearrange("p (t f) -> p t f", t=2)
    keys = big[:, 32 * NLAT + 2 * D:32 * NLAT + 2 * D + 2 * PEER_N].rearrange("p (r n) -> p r n", r=2)
    experts = big[:, 11008:11008 + 2 * S]
    gates = big[:, 11264:11264 + 2 * S]
    experts_u = experts.bitcast(U32)
    hs = moving(c.h, NCTX, T)
    project(c, rows(a["peer_wq_2"][0]), 0, 2 * H * P // CHUNK, hs, NLAT,
            lambda e, bank, tile: e.tensor_copy(qh[:, tile, :], bank))

    with c.stage() as block:
        @block.sync
        def _(sp):
            sp.dma_start(keys, a["keys"]).then_inc(c.side_loaded, 16)

        @block.tensor
        def _(pe):
            for r in range(4):
                for i in range(4):
                    t, k = (4 * r + i) // KT, (4 * r + i) % KT
                    last = pe.transpose(c.banks[r][:, i * P:(i + 1) * P], hs[:, k, t * P:(t + 1) * P], c.constant("ident"))
                last.then_inc(c.product, 1)
            pe.wait_ge(c.side_loaded, 16)
            for t in range(2):
                for i in range(2 * H):
                    n = (2 * H * t + i) // 4
                    if i % 4 == 0 and n >= 4:
                        pe.wait_ge(c.drained, n)
                    last = pe.matmul(c.banks[4 + n if n < 4 else n - 4][:, (i % 4) * P:(i % 4 + 1) * P],
                                     qh[:, i, t * P:(t + 1) * P], keys[:, i % 2, :], start=True, stop=True)
                    if i % 4 == 3:
                        last.then_inc(c.product, 1)

        @block.vector
        def _(dve):
            for r in range(4):
                dve.wait_ge(c.product, r + 1)
                dve.tensor_copy(tokens[:, r // 2, (r % 2) * 512:(r % 2 + 1) * 512], c.banks[r][:]).then_inc(c.drained, 1)
            for n in range(8):
                dve.wait_ge(c.product, 5 + n)
                dve.tensor_copy(scores[:, n * 512:(n + 1) * 512], c.banks[4 + n if n < 4 else n - 4][:]).then_inc(c.drained, 1)

    R = PEER_RING
    G = K // R
    apart, diag, place, dot, gl, w, gate4, acc, s, v, idx, idf, cand, best, less, pos, sel, eq, ef, small = c.carve(
        (R // 2, 2 * D), (R, P), (R,), (R,), (R,), (R,), (R,), (D,),
        (2, PEER_N), (2, K), (2, K), (2, K), (1, K * K), (1, K), (1, K), (1, K), (2, K), (K, K), (2, K), (2,))
    in_ring = c.ring[:].rearrange("p s k n -> p (s k n)").rearrange("p (r n) -> p r n", n=2 * D)
    fetched = [in_ring[:, r] for r in range(R // 2)] + [apart[:, r] for r in range(R // 2)]
    urows, vrows = [x[:, 0:D] for x in fetched], [x[:, D:2 * D] for x in fetched]
    place_u = place.bitcast(U32)
    idx, pos = idx.bitcast(U32), pos.bitcast(U32)
    sel_u = sel.bitcast(U32)

    class Search:

        def __init__(self, dve, unit):
            self.dve, self.unit, self.n = dve, unit, 0

        def mark(self, instruction):
            instruction.then_inc(c.searched, 1)
            self.n += 1
            return self.n

        def wait(self, n=None):
            self.dve.wait_ge(c.searched, self.n if n is None else n)

        def __call__(self, instruction):
            self.mark(instruction)
            self.wait()

        def best16(self, table, values, places, count):
            dve = self.dve
            for r in range(2):
                part = slice(8 * r, 8 * r + 8)
                for i in range(count):
                    done = self.mark(dve.max(out=values[:, i, part], in_=table[:, i, :]))
                self.wait(done)
                for i in range(count):
                    done = self.mark(dve.max_index(out=places[:, i, part], in_max=values[:, i, part], in_values=table[:, i, :]))
                self.wait(done)
                if r == 0:
                    for i in range(count):
                        done = self.mark(dve.match_replace(out=table[:, i, :], in_to_replace=values[:, i, part],
                                                           in_values=table[:, i, :], imm_value=LOWEST))
                    self.wait(done)

        def halves(self):
            self.dve.sem_clear(c.searched)
            self(self.dve.tensor_copy(s.rearrange("p i n -> p (i n)"),
                                      scores[:, bass.ds(self.unit * (2 * PEER_N), 2 * PEER_N)]))
            self.best16(s, v, idx, 2)
            self(self.dve.tensor_copy(idf, idx))

        def pairs(self):
            dve = self.dve
            self(dve.tensor_tensor(cand.rearrange("p h (x y) -> p (h x) y", y=K), v[:, 0, :].unsqueeze(2).to_broadcast([P, K, K]),
                                   v[:, 1, :].unsqueeze(1).to_broadcast([P, K, K]), ALU.add))
            self.best16(cand, best, pos, 1)
            self(dve.tensor_tensor(less[:, 0, :], best[:, 0, :], best[:, 0, 0:1].to_broadcast([P, K]), ALU.subtract))
            dve.sem_inc(c.shifted, 1)

        def numbers(self):
            dve = self.dve
            self(dve.tensor_scalar(sel_u[:, 0], pos[:, 0, :], 4, None, ALU.logical_shift_right))
            self(dve.tensor_scalar(sel_u[:, 1], pos[:, 0, :], K - 1, None, ALU.bitwise_and))
            self(dve.tensor_copy(ef, sel_u))
            for r in range(2):
                self(dve.tensor_tensor(eq, ef[:, r].unsqueeze(2).to_broadcast([P, K, K]),
                                       c.constant("iota").unsqueeze(1).to_broadcast([P, K, K]), ALU.is_equal))
                self(dve.tensor_tensor(eq, eq, idf[:, r, :].unsqueeze(1).to_broadcast([P, K, K]), ALU.mult))
                self(dve.tensor_reduce(sel[:, r], eq, AX.X, ALU.add))
            self(dve.tensor_scalar(sel[:, 0], sel[:, 0], float(PEER_N), None, ALU.mult))
            self(dve.tensor_tensor(experts_u[:, bass.ds(self.unit * K, K)], sel[:, 0], sel[:, 1], ALU.add))
            dve.sem_inc(c.ranked, 1)

        def weights(self, head):
            dve = self.dve
            dve.wait_ge(c.powers, head)
            self(dve.reduce_sum(small[:, 0:1], less[:, 0, :], AX.X))
            self(dve.reciprocal(small[:, 1:2], small[:, 0:1]))
            self(dve.tensor_tensor(gates[:, bass.ds(self.unit * K, K)], less[:, 0, :], small[:, 1:2].to_broadcast([P, K]),
                                   ALU.mult))

    def exponentials(act, count):
        act.wait_ge(c.shifted, count)
        act.activation(less, less, ACT.Exp).then_inc(c.powers, 1)

    with c.stage() as block:
        @block.vector
        def _(dve):
            search = Search(dve, 0)
            search.halves()
            search.pairs()
            search.numbers()
            search.weights(1)

        @block.scalar
        def _(act):
            exponentials(act, 1)

    groups = H * G
    for t in range(2):
        with c.stage() as block:
            def run(engine, body):
                body(0)
                with engine.Fori(0, H - 2) as j:
                    body(j + 1)
                body(H - 1)

            def searches(h):
                return not (t == 1 and isinstance(h, int) and h == H - 1)

            had = 16 * groups * t

            @block.gpsimd
            def _(pool):
                def body(h):
                    first_head = isinstance(h, int) and h == 0
                    if not first_head:
                        pool.wait_ge(c.ranked, 1)
                        pool.sem_clear(c.ranked)
                    for q in range(G):
                        for r in range(R):
                            if not first_head or q:
                                pool.wait_ge(c.u_free[r], 1)
                                pool.sem_clear(c.u_free[r])
                                pool.wait_ge(c.v_free[r], 1)
                                pool.sem_clear(c.v_free[r])
                            pool.tensor_copy(place_u[:, r:r + 1], experts_u[:, bass.ds(h * K + (q * R + r + t * S), 1)]
                                             ).then_inc(c.pool_done, 1)
                            pool.wait_ge(c.pool_done, 1)
                            pool.sem_clear(c.pool_done)
                            pool.indirect_dma_start(
                                out=fetched[r], out_offset=None, in_=a["experts"],
                                in_offset=bass.IndirectOffsetOnAxis(ap=place_u[:, r:r + 1], axis=0)
                            ).then_inc(c.gathered[r], 16)

                run(pool, body)

            @block.vector
            def _(dve):
                def body(h):
                    if searches(h):
                        search = Search(dve, h + (t * H + 1))
                        steps = (search.halves, search.pairs, search.numbers, lambda: search.weights(h + 1))
                    for q in range(G):
                        if q or not (isinstance(h, int) and h == 0):
                            dve.wait_ge(c.act_out, h * K + q * R)
                        dve.tensor_copy(gate4, gates[:, bass.ds(h * K + (q * R + t * S), R)]).then_inc(c.vec_done, 1)
                        for r in range(R):
                            if searches(h) and r % 4 == 0:
                                steps[(q * R + r) // 4]()
                            dve.wait_ge(c.gathered[r], h * (16 * G) + (16 * q + 16 + had))
                            dve.tensor_tensor_reduce(out=urows[r], in0=urows[r], in1=tokens[:, t, :], scale=1.0,
                                                     scalar=0.0, op0=ALU.mult, op1=ALU.add, accum_out=dot[:, r:r + 1]
                                                     ).then_inc(c.vec_out, 1)

                run(dve, body)

            @block.scalar
            def _(act):
                def body(h):
                    for q in range(G):
                        if q == G // 2 and searches(h):
                            exponentials(act, h + 1)
                        act.wait_ge(c.vec_done, h * G + (q + 1))
                        for r in range(R):
                            act.wait_ge(c.vec_out, h * K + (q * R + r + 1))
                            act.sem_inc(c.u_free[r], 1)
                            act.activation(gl[:, r:r + 1], dot[:, r:r + 1], ACT.Gelu).then_inc(c.act_done, 1)
                            act.wait_ge(c.act_done, h * (2 * K) + (2 * (q * R + r) + 1))
                            act.activation(w[:, r:r + 1], gl[:, r:r + 1], ACT.Copy, scale=gate4[:, r:r + 1]
                                           ).then_inc(c.act_done, 1)
                            act.wait_ge(c.act_done, h * (2 * K) + (2 * (q * R + r) + 2))
                            if q or not (isinstance(h, int) and h == 0):
                                act.wait_ge(c.product, h * K + (q * R + r + 1 - R))
                            act.activation(diag[:, r, :], c.constant("ident"), ACT.Copy, scale=w[:, r:r + 1]
                                           ).then_inc(c.act_out, 1)

                run(act, body)

            @block.tensor
            def _(pe):
                def body(h):
                    for q in range(G):
                        for r in range(R):
                            pe.wait_ge(c.act_out, h * K + (q * R + r + 1))
                            pe.wait_ge(c.gathered[r], h * (16 * G) + (16 * q + 16 + had))
                            first = isinstance(h, int) and h == 0 and q == 0 and r == 0
                            final = isinstance(h, int) and h == H - 1 and q == G - 1 and r == R - 1
                            for half in range(2):
                                last = pe.matmul(c.banks[half][:], diag[:, r, :], vrows[r][:, half * 512:(half + 1) * 512],
                                                 start=first, stop=final)
                            last.then_inc(c.product, 1)
                            pe.wait_ge(c.product, h * K + (q * R + r + 1))
                            pe.sem_inc(c.v_free[r], 1)

                run(pe, body)

        with c.stage() as block:
            @block.vector
            def _(dve):
                for half in range(2):
                    dve.tensor_copy(acc[:, half * 512:(half + 1) * 512], c.banks[half][:]).then_inc(c.vec_out, 1)
                for half in range(2):
                    dve.wait_ge(c.product, half + 1)
                    for i in range(4):
                        k = 4 * half + i
                        out = c.x[:, k, NCTX + t * P:NCTX + (t + 1) * P]
                        dve.scalar_tensor_tensor(out, c.banks[2 + half][:, i * P:(i + 1) * P], c.mod[:, 5 * KT + k, 0:1], out,
                                                 ALU.mult, ALU.add)

            @block.tensor
            def _(pe):
                for half in range(2):
                    pe.wait_ge(c.vec_out, half + 1)
                    for i in range(4):
                        last = pe.transpose(c.banks[2 + half][:, i * P:(i + 1) * P],
                                            acc[:, (4 * half + i) * P:(4 * half + i + 1) * P], c.constant("ident"))
                    last.then_inc(c.product, 1)


def second_block(c, a):
    lat = (NCTX, T)
    tables = S5Tables(c)
    adaln(c, rows(a["ada_w_2"][0]), c.cond[:, 2:3, :].rearrange("p a k -> p k a"), c.vector("ada_b_2"), 1,
          first_loads(rows(a["w_in_2"][0]), 0, HG_W // CHUNK), beside=tables)
    norm(c, c.x, c.h, c.vector("norm_mix"), [(*lat, 0, 0, KT)])
    hgrn_blocks(c, a)
    w_out = rows(a["w_out_2"][0])
    recurrences(c, a, tables, first_loads(w_out, 0, D // CHUNK))
    add_gated(c, w_out, c.mg[:, :, 0:NLAT], [(*lat, 0)], 2 * KT,
              following=first_loads(rows(a["peer_wq_2"][0]), 0, 2 * PEER_H * P // CHUNK))
    norm(c, c.x, c.h, c.vector("norm_ffn"), [(*lat, 0, 3 * KT, 4 * KT)])
    peer(c, a)
    norm(c, c.x, c.h, c.vector("final_norm"), [(*lat, 0, 0, 0)], modulated=False)


STREAMED = ("w_ada", "w_in", "w_br_ml", "w_br_da", "w_br_fn", "w_out", "w_ffn_in", "w_ffn_out", "ada_w_2", "w_in_2", "w_out_2",
            "s5_glu_w_2", "peer_wq_2")
PACKED = ("vectors", "constants", "residual", "s5_b", "s5_c", "keys", "experts")
OUT = (P, KT, NLAT)


def build(nc, a, out):
    ctx = ExitStack()
    with ctx:
        c = Core(nc, ctx)
        load_small(c, a, first_loads(rows(a["w_ada"][0]), 0, 6 * D // CHUNK))
        first_block(c, a)
        second_block(c, a)
        with nc.Block() as block:
            @block.sync
            def _(sp):
                sp.dma_start(out, c.h[:, :, NCTX:T]).then_inc(c.stored, 16)
                sp.wait_ge(c.stored, 16)


def columns(v):
    v = np.asarray(v)
    return v.reshape(-1, P).T


def pack_vectors(x):
    out = np.zeros((P, N_VEC), np.float32)

    def put(name, value):
        at, width = VEC[name]
        assert value.shape[1] == width, (name, value.shape, width)
        out[:value.shape[0], at:at + width] = value

    put("c", np.concatenate([columns(x["c_ctx"]), columns(x["c"]), columns(x["c_2"])], 1))
    for name, key in (("b_ada", "b_ada"), ("norm_g", "norm_g"), ("ml_head_g", "ml_head_g"), ("da_head_g", "da_head_g"),
                      ("final_g", "final_g"), ("ada_b_2", "ada_b_2"), ("norm_mix", "norm_mix_w_2"),
                      ("norm_ffn", "norm_ffn_w_2"), ("final_norm", "final_norm_w_2"), ("gnorm", "hg_gnorm_w_2"),
                      ("s5_d", "s5_d_2"), ("glu_b", "s5_glu_b_2"), ("bounds", "hg_lower_bounds_2")):
        put(name, columns(x[key]))
    put("lam", np.broadcast_to(x["da_lam"].reshape(1, -1), (P, 2 * 4 * DA_DH)))
    gate_b = np.zeros((P, DEPTH), np.float32)
    for j in range(4):
        gate_b[32 * j:32 * j + ML_HEADS] = x["ml_gate_b"].reshape(DEPTH, 4, ML_HEADS)[:, j].T
    put("gate_b", gate_b)
    put("s5_are", columns(x["s5_a_re_2"]))
    put("s5_aim", columns(x["s5_a_im_2"]))
    put("s5_dt", columns(np.repeat(x["s5_log_dt_2"].reshape(-1), S5_P)))
    return out


def pack_constants():
    out = np.zeros((P, N_CST), np.float32)

    def put(name, value):
        at, width = CST[name]
        out[:, at:at + width] = np.broadcast_to(value, (P, width))

    at = np.arange(P)
    put("ident", np.eye(P))
    put("ones", np.ones((P, P)))
    put("upper", at[:, None] <= at[None, :])
    put("lower", at[:, None] >= at[None, :])
    turn = np.zeros((P, P))
    half = DA_DH // 2
    for p in range(P):
        first = p % DA_DH < half
        turn[p + half if first else p - half, p] = -1.0 if first else 1.0
    put("turn", turn)
    n_freq = DA_DH // 4
    inv = np.float32(10000.0) ** (-np.arange(n_freq, dtype=np.float32) / n_freq)
    r, col = np.repeat(np.arange(NLAT // 64, dtype=np.float32), 64), np.tile(np.arange(64, dtype=np.float32), NLAT // 64)
    angle = np.concatenate([r[:, None] * inv, col[:, None] * inv], -1)
    spread = angle[:, at % half].T
    put("cos", np.cos(spread))
    put("sin", np.sin(spread))
    k = np.arange(FN_C)
    phase = 2 * np.pi * (np.outer(k, k) % FN_C) / FN_C
    dft = np.concatenate([np.cos(phase), np.sin(phase), -np.sin(phase)], 1) / FN_C ** 0.5
    put("dft", dft.reshape(2, P, 3 * FN_C).transpose(1, 0, 2).reshape(P, -1))
    put("pick", np.eye(HG_SUB).reshape(1, -1))
    put("inner", (np.arange(HG_HEADS * NLAT) % HG_SUB != 0)[None, :])
    put("iota", np.arange(PEER_K)[None, :])
    return out


def pack_inputs(x):
    tokens = np.concatenate([x["ctx"][0], x["x"][0]], 0)
    m = {name: np.ascontiguousarray(x[name]) for name in STREAMED}
    m["vectors"] = pack_vectors(x)
    m["constants"] = pack_constants()
    m["residual"] = np.ascontiguousarray(tokens.T.reshape(KT, P, T).transpose(1, 0, 2))
    b = np.zeros((2, P, 4, P), np.float32)
    cc = np.zeros((2, P, S5_TILES, 2 * S5_H), np.float32)
    for part, (bn, cn) in enumerate((("s5_b_re_2", "s5_c_re_2"), ("s5_b_im_2", "s5_c_im_2"))):
        for g in range(S5_G):
            i, second = g // 2, g % 2
            row = 2 * S5_H * (i % 4) + S5_H * second
            b[part, row:row + S5_H, i // 4, S5_P * second:S5_P * (second + 1)] = x[bn][0, g].T
            cc[part, S5_P * second:S5_P * (second + 1), i, S5_H * second:S5_H * (second + 1)] = x[cn][0, g].T
    m["s5_b"], m["s5_c"] = b, cc
    m["experts"] = np.concatenate([x["peer_u_2"][0], x["peer_v_2"][0]], 1)
    m["keys"] = np.ascontiguousarray(np.stack([x["peer_keys1_2"][0].T, x["peer_keys2_2"][0].T], 1))
    return m


def kernel(**inputs):
    import concourse.bacc as _bacc
    from concourse.bass_utils import run_bass_kernel_spmd as _run

    arrays = pack_inputs({k: np.asarray(v) for k, v in inputs.items()})
    nc = _bacc.Bacc("TRN2", target_bir_lowering=False, num_devices=1)
    a = {n: nc.dram_tensor(n, v.shape, F32, kind="ExternalInput").ap() for n, v in arrays.items()}
    a["rows"] = nc.dram_tensor("rows", (ML_HEADS, 4, T), F32, kind="Internal").ap()
    out = nc.dram_tensor("out", OUT, F32, kind="ExternalOutput").ap()
    build(nc, a, out)
    r = _run(nc, [arrays], core_ids=[0])
    got = r.results[0]["out"]
    return np.ascontiguousarray(got.transpose(2, 1, 0)).reshape(1, NLAT, D)
```
